# Optimizing a Trainium2 kernel written in Bass

```python
import numpy as np
import jax
import jax.numpy as jnp
from jax import lax
import jax, jax.numpy as jnp

D_MODEL = 1024
BATCH = 1
SEQ = 256
DEPTH = 2

GRID_W = 64
CTX_LEN = 256
N_MIXERS = 2
N_HEADS = 16
HEAD_DIM = D_MODEL // N_HEADS
D_FF = 2816
CONV_WIDTH = 31
WIN_R = 8
WIN_C = 16
N_MOD = 9
N_CONV_LAYERS = (DEPTH + 1) // 2
N_NA_LAYERS = DEPTH // 2
RMS_EPS = 1e-6
LN_EPS = 1e-5
MASK_VALUE = -1e30


def _rmsnorm(x, g):
    xf = x.astype(jnp.float32)
    y = xf * lax.rsqrt(jnp.mean(xf * xf, axis=-1, keepdims=True) + RMS_EPS)
    return y.astype(x.dtype) * g

def _layernorm(x, g, b):
    xf = x.astype(jnp.float32)
    mu = jnp.mean(xf, axis=-1, keepdims=True)
    var = jnp.mean(jnp.square(xf - mu), axis=-1, keepdims=True)
    return ((xf - mu) * lax.rsqrt(var + LN_EPS)).astype(x.dtype) * g + b

def _modulate(h, shift, scale):
    return h * (1 + scale) + shift

def _swiglu(h, wg, wu, wd):
    return (jax.nn.silu(h @ wg) * (h @ wu)) @ wd

def _ffn_half(s, mod, g, wg, wu, wd):
    shift, scale, gate = mod
    h = _modulate(_rmsnorm(s, g), shift, scale)
    return s + 0.5 * gate * _swiglu(h, wg, wu, wd)

def _conv_module(h, w1, b1, wdw, bdw, lng, lnb, w2, b2):
    a, gt = jnp.split(h @ w1 + b1, 2, axis=-1)
    u = a * jax.nn.sigmoid(gt)
    u = lax.conv_general_dilated(
        u, wdw[:, None, :], window_strides=(1,),
        padding=[(CONV_WIDTH // 2, CONV_WIDTH // 2)],
        dimension_numbers=('NWC', 'WIO', 'NWC'),
        feature_group_count=u.shape[-1]) + bdw
    u = jax.nn.silu(_layernorm(u, lng, lnb))
    return u @ w2 + b2

def _col_window_tables():
    ncb = GRID_W // WIN_C
    span = 2 * WIN_C
    n = np.arange(ncb)
    blk_start = np.clip(n * WIN_C - WIN_C // 2, 0, GRID_W - span)
    key_cols = blk_start[:, None] + np.arange(span)[None, :]
    q_cols = n[:, None] * WIN_C + np.arange(WIN_C)[None, :]
    q_start = np.clip(q_cols - WIN_C // 2, 0, GRID_W - WIN_C)
    kc3 = key_cols[:, None, :]
    valid = (kc3 >= q_start[:, :, None]) & (kc3 < q_start[:, :, None] + WIN_C)
    rel = np.clip(kc3 - q_cols[:, :, None], -(WIN_C - 1), WIN_C - 1) + WIN_C - 1
    return key_cols.astype(np.int32), valid, rel.astype(np.int32)

def _neighbourhood_attention(q, k, v, kc, vc, rpb):
    B, T, H, Dh = q.shape
    rows = T // GRID_W
    wr = min(WIN_R, rows)
    key_cols, valid, rel_idx = _col_window_tables()
    ncb, span = key_cols.shape
    key_cols_j = jnp.asarray(key_cols)
    rel_idx_j = jnp.asarray(rel_idx)
    valid_j = jnp.asarray(valid)[None, None, :, :, None, :]
    rpb32 = rpb.astype(jnp.float32)
    qg = (q * (Dh ** -0.5)).reshape(B, rows, ncb, WIN_C, H, Dh).transpose(1, 0, 2, 3, 4, 5)
    kg = k.reshape(B, rows, GRID_W, H, Dh)
    vg = v.reshape(B, rows, GRID_W, H, Dh)

    def row_step(args):
        r, q_row = args
        r0 = jnp.clip(r - wr // 2, 0, rows - wr)
        k_band = lax.dynamic_slice_in_dim(kg, r0, wr, axis=1)
        v_band = lax.dynamic_slice_in_dim(vg, r0, wr, axis=1)
        k_blk = jnp.take(k_band, key_cols_j, axis=2)
        v_blk = jnp.take(v_band, key_cols_j, axis=2)
        s_lat = jnp.einsum('bnqhd,bjnmhd->bhnqjm', q_row, k_blk).astype(jnp.float32)
        rel_r = r0 + jnp.arange(wr) - r + WIN_R - 1
        bias = jnp.take(rpb32, rel_r, axis=1)
        bias = jnp.take(bias, rel_idx_j, axis=2).transpose(0, 2, 3, 1, 4)
        s_lat = jnp.where(valid_j, s_lat + bias, MASK_VALUE)
        s_ctx = jnp.einsum('bnqhd,bkhd->bhnqk', q_row, kc).astype(jnp.float32)
        s = jnp.concatenate([s_lat.reshape(B, H, ncb, WIN_C, wr * span), s_ctx], axis=-1)
        p = jax.nn.softmax(s, axis=-1).astype(v.dtype)
        p_lat = p[..., :wr * span].reshape(B, H, ncb, WIN_C, wr, span)
        p_ctx = p[..., wr * span:]
        return (jnp.einsum('bhnqjm,bjnmhd->bnqhd', p_lat, v_blk)
                + jnp.einsum('bhnqk,bkhd->bnqhd', p_ctx, vc))

    o = lax.map(row_step, (jnp.arange(rows), qg))
    return o.transpose(1, 0, 2, 3, 4, 5).reshape(B, T, H * Dh)

def _context_attention(qc, kc, vc):
    B, K, H, Dh = qc.shape
    s = jnp.einsum('bqhd,bkhd->bhqk', qc * (Dh ** -0.5), kc).astype(jnp.float32)
    p = jax.nn.softmax(s, axis=-1).astype(vc.dtype)
    return jnp.einsum('bhqk,bkhd->bqhd', p, vc).reshape(B, K, H * Dh)

def first_inputs(seed: int = 0) -> dict:
    key = jax.random.key(seed)
    ks = iter(jax.random.split(key, 32))

    def nrm(shape, scale):
        return jax.random.normal(next(ks), shape, jnp.float32) * scale

    D, F = D_MODEL, D_FF
    return {
        'x': nrm((BATCH, SEQ, D), 1.0),
        'c': nrm((BATCH, D), 1.0),
        'ctx': nrm((BATCH, CTX_LEN, D), 1.0),
        'c_ctx': nrm((D,), 1.0),
        'mod_w': nrm((DEPTH, D, N_MOD * D), 0.5 * D ** -0.5),
        'mod_b': nrm((DEPTH, N_MOD * D), 0.02),
        'norm_g': 1.0 + nrm((DEPTH, 3, D), 0.05),
        'ffn_w_gate': nrm((DEPTH, 2, D, F), D ** -0.5),
        'ffn_w_up': nrm((DEPTH, 2, D, F), D ** -0.5),
        'ffn_w_down': nrm((DEPTH, 2, F, D), F ** -0.5),
        'conv_w_pw1': nrm((N_CONV_LAYERS, D, 2 * D), D ** -0.5),
        'conv_b_pw1': nrm((N_CONV_LAYERS, 2 * D), 0.02),
        'conv_w_dw': nrm((N_CONV_LAYERS, CONV_WIDTH, D), CONV_WIDTH ** -0.5),
        'conv_b_dw': nrm((N_CONV_LAYERS, D), 0.02),
        'conv_ln_g': 1.0 + nrm((N_CONV_LAYERS, D), 0.05),
        'conv_ln_b': nrm((N_CONV_LAYERS, D), 0.02),
        'conv_w_pw2': nrm((N_CONV_LAYERS, D, D), D ** -0.5),
        'conv_b_pw2': nrm((N_CONV_LAYERS, D), 0.02),
        'na_w_qkv': nrm((N_NA_LAYERS, D, 3 * D), D ** -0.5),
        'na_b_qkv': nrm((N_NA_LAYERS, 3 * D), 0.02),
        'na_rpb': nrm((N_NA_LAYERS, N_HEADS, 2 * WIN_R - 1, 2 * WIN_C - 1), 0.1),
        'na_w_o': nrm((N_NA_LAYERS, D, D), D ** -0.5),
        'na_b_o': nrm((N_NA_LAYERS, D), 0.02),
        'final_g': 1.0 + nrm((D,), 0.05),
    }

def first_block(x, c, ctx, c_ctx, mod_w, mod_b, norm_g, ffn_w_gate, ffn_w_up, ffn_w_down,
              conv_w_pw1, conv_b_pw1, conv_w_dw, conv_b_dw, conv_ln_g, conv_ln_b, conv_w_pw2, conv_b_pw2,
              na_w_qkv, na_b_qkv, na_rpb, na_w_o, na_b_o, final_g):
    B, T, D = x.shape
    K = ctx.shape[1]
    xc = ctx
    for i in range(DEPTH):
        mixer = i % N_MIXERS
        j = i // N_MIXERS
        last = i == DEPTH - 1
        run_ctx = (not last) or mixer == 1
        ml = (jax.nn.silu(c) @ mod_w[i] + mod_b[i]).reshape(B, 1, N_MOD, D)
        mc = (jax.nn.silu(c_ctx) @ mod_w[i] + mod_b[i]).reshape(N_MOD, D)
        lat_m = [ml[:, :, n] for n in range(N_MOD)]
        ctx_m = [mc[n] for n in range(N_MOD)]

        x = _ffn_half(x, lat_m[0:3], norm_g[i, 0], ffn_w_gate[i, 0], ffn_w_up[i, 0], ffn_w_down[i, 0])
        if run_ctx:
            xc = _ffn_half(xc, ctx_m[0:3], norm_g[i, 0], ffn_w_gate[i, 0], ffn_w_up[i, 0], ffn_w_down[i, 0])

        h = _modulate(_rmsnorm(x, norm_g[i, 1]), lat_m[3], lat_m[4])
        if run_ctx:
            hc = _modulate(_rmsnorm(xc, norm_g[i, 1]), ctx_m[3], ctx_m[4])
        if mixer == 0:
            conv_p = (conv_w_pw1[j], conv_b_pw1[j], conv_w_dw[j], conv_b_dw[j],
                      conv_ln_g[j], conv_ln_b[j], conv_w_pw2[j], conv_b_pw2[j])
            y = _conv_module(h, *conv_p)
            if not last:
                yc = _conv_module(hc, *conv_p)
        else:
            qkv = (h @ na_w_qkv[j] + na_b_qkv[j]).reshape(B, T, 3, N_HEADS, HEAD_DIM)
            qkvc = (hc @ na_w_qkv[j] + na_b_qkv[j]).reshape(B, K, 3, N_HEADS, HEAD_DIM)
            kc, vc = qkvc[:, :, 1], qkvc[:, :, 2]
            o = _neighbourhood_attention(qkv[:, :, 0], qkv[:, :, 1], qkv[:, :, 2], kc, vc, na_rpb[j])
            y = o @ na_w_o[j] + na_b_o[j]
            if not last:
                yc = _context_attention(qkvc[:, :, 0], kc, vc) @ na_w_o[j] + na_b_o[j]
        x = x + lat_m[5] * y

        x = _ffn_half(x, lat_m[6:9], norm_g[i, 2], ffn_w_gate[i, 1], ffn_w_up[i, 1], ffn_w_down[i, 1])
        if not last:
            xc = xc + ctx_m[5] * yc
            xc = _ffn_half(xc, ctx_m[6:9], norm_g[i, 2], ffn_w_gate[i, 1], ffn_w_up[i, 1], ffn_w_down[i, 1])
    return _rmsnorm(x, final_g)


PLE_DIM = 256
R_HEADS = 4
R_DK = 64
R_DV = 128
R_CHUNK = 128
ROPE_BASE = 10000.0
M_HEADS = 4
M_DK = 64
M_DV = 128
M_CHUNK = 64
M_CONV = 4
AB_MIX = R_HEADS * R_DV + M_HEADS * M_DV
AB_SIZES = (R_HEADS * R_DK, R_HEADS * R_DK, R_HEADS * R_DV, R_HEADS * R_DV,
            M_HEADS * M_DK, M_HEADS * M_DK, M_HEADS * M_DV, M_HEADS * M_DV,
            M_HEADS, M_HEADS)
AB_COLS = sum(AB_SIZES)
N_KV_GROUPS = 2
HEAD_DIM_2 = 64
CMP_BLOCK = 32
CMP_STRIDE = 16
CMP_HIDDEN = 256
SLC_BLOCK = 64
N_SELECT = 16
WINDOW = 512
Q_BLOCK = 128
NSA_SIZES = (N_HEADS * HEAD_DIM_2,) + (N_KV_GROUPS * HEAD_DIM_2,) * 6 + (N_HEADS * 3,)
NSA_COLS = sum(NSA_SIZES)
FFN_CONV = 3

NEG = -1e30
BIG = 1e30
EPS = 1e-6


def rms_norm(x, g):
    xf = x.astype(jnp.float32)
    y = xf * lax.rsqrt(jnp.mean(xf * xf, axis=-1, keepdims=True) + EPS)
    return (y * g.astype(jnp.float32)).astype(x.dtype)

def split_cols(z, sizes):
    return jnp.split(z, np.cumsum(sizes)[:-1].tolist(), axis=-1)

def causal_dwconv(x, w, b):
    K = w.shape[0]
    T = x.shape[1]
    xp = jnp.pad(x, ((0, 0), (K - 1, 0), (0, 0)))
    y = b
    for j in range(K):
        y = y + xp[:, j:j + T] * w[j]
    return y

def to_chunks(x, L):
    B, T = x.shape[:2]
    x = x.reshape((B, T // L, L) + x.shape[2:])
    return jnp.moveaxis(x, (1, 2), (0, 3))

def from_chunks(y):
    y = jnp.moveaxis(y, (0, 3), (1, 2))
    return y.reshape((y.shape[0], y.shape[1] * y.shape[2]) + y.shape[3:])

def rotary(x, pos):
    half = x.shape[-1] // 2
    inv = ROPE_BASE ** (-jnp.arange(half, dtype=jnp.float32) / half)
    ang = pos[:, None] * inv[None, :]
    cos = jnp.cos(ang)[:, None, :]
    sin = jnp.sin(ang)[:, None, :]
    x1, x2 = x[..., :half], x[..., half:]
    return jnp.concatenate([x1 * cos - x2 * sin, x1 * sin + x2 * cos], axis=-1)

def retention_chunkwise(q, k, v):
    B, T, H, DK = q.shape
    DV = v.shape[-1]
    L = R_CHUNK
    log_g = jnp.log1p(-jnp.exp2(-5.0 - jnp.arange(H, dtype=jnp.float32)))
    idx = jnp.arange(L, dtype=jnp.float32)
    diff = idx[:, None] - idx[None, :]
    causal = diff >= 0
    dmask = jnp.where(causal, jnp.exp(jnp.where(causal, diff, 0.0)[None] * log_g[:, None, None]), 0.0)
    q_dec = jnp.exp((idx + 1.0)[None, :] * log_g[:, None])
    k_dec = jnp.exp((L - 1.0 - idx)[None, :] * log_g[:, None])
    c_dec = jnp.exp(L * log_g)

    def step(R, xs):
        qc, kc, vc = xs
        s = jnp.einsum('bhld,bhmd->bhlm', qc, kc) * dmask
        o = (jnp.einsum('bhlm,bhme->bhle', s, vc)
             + jnp.einsum('bhld,bhde->bhle', qc, R) * q_dec[..., None])
        R = c_dec[:, None, None] * R + jnp.einsum('bhmd,bhme->bhde', kc * k_dec[..., None], vc)
        return R, o

    R0 = jnp.zeros((B, H, DK, DV), jnp.float32)
    _, o = lax.scan(step, R0, (to_chunks(q, L), to_chunks(k, L), to_chunks(v, L)))
    return from_chunks(o)

def mlstm_chunkwise(q, k, v, ig, lf):
    B, T, H, DK = q.shape
    DV = v.shape[-1]
    L = M_CHUNK
    causal = jnp.tril(jnp.ones((L, L), dtype=bool))

    def step(carry, xs):
        C, n, m = carry
        qc, kc, vc, ic, fc = xs
        b = jnp.cumsum(fc, axis=-1)
        dlog = jnp.where(causal, b[..., :, None] - b[..., None, :] + ic[..., None, :], NEG)
        inter = b + m[..., None]
        m_t = jnp.maximum(inter, jnp.max(dlog, axis=-1))
        s = jnp.einsum('bhld,bhsd->bhls', qc, kc) * jnp.exp(dlog - m_t[..., None])
        w_inter = jnp.exp(inter - m_t)
        num = (jnp.einsum('bhls,bhse->bhle', s, vc)
               + w_inter[..., None] * jnp.einsum('bhld,bhde->bhle', qc, C))
        den = jnp.sum(s, axis=-1) + w_inter * jnp.einsum('bhld,bhd->bhl', qc, n)
        h = num / jnp.maximum(jnp.abs(den), jnp.exp(-m_t))[..., None]
        b_last = b[..., -1]
        wlog = b_last[..., None] - b + ic
        m_new = jnp.maximum(b_last + m, jnp.max(wlog, axis=-1))
        decay = jnp.exp(b_last + m - m_new)
        wk = kc * jnp.exp(wlog - m_new[..., None])[..., None]
        C = decay[..., None, None] * C + jnp.einsum('bhsd,bhse->bhde', wk, vc)
        n = decay[..., None] * n + jnp.sum(wk, axis=2)
        return (C, n, m_new), h

    init = (jnp.zeros((B, H, DK, DV), jnp.float32), jnp.zeros((B, H, DK), jnp.float32),
            jnp.zeros((B, H), jnp.float32))
    xs = (to_chunks(q, L), to_chunks(k, L), to_chunks(v, L), to_chunks(ig, L), to_chunks(lf, L))
    _, h = lax.scan(step, init, xs)
    return from_chunks(h)

def ab_mixer(h, w_in, conv_w, conv_b, ret_g, ig_b, fg_b, m_g, w_out):
    B, T, _ = h.shape
    z = (h @ w_in).astype(jnp.float32)
    rq, rk, rv, rg, mq, mk, mv, mo, mi, mf = split_cols(z, AB_SIZES)
    pos = jnp.arange(T, dtype=jnp.float32)
    rq = rotary(rq.reshape(B, T, R_HEADS, R_DK), pos)
    rk = rotary(rk.reshape(B, T, R_HEADS, R_DK), pos) * (R_DK ** -0.5)
    ret = retention_chunkwise(rq, rk, rv.reshape(B, T, R_HEADS, R_DV))
    ret = rms_norm(ret, ret_g.reshape(R_HEADS, R_DV)).reshape(B, T, -1) * jax.nn.silu(rg)
    mqk = jax.nn.silu(causal_dwconv(jnp.concatenate([mq, mk], axis=-1), conv_w, conv_b))
    mq, mk = jnp.split(mqk, 2, axis=-1)
    hm = mlstm_chunkwise(mq.reshape(B, T, M_HEADS, M_DK) * (M_DK ** -0.5),
                         mk.reshape(B, T, M_HEADS, M_DK),
                         mv.reshape(B, T, M_HEADS, M_DV),
                         mi + ig_b,
                         jax.nn.log_sigmoid(mf + fg_b))
    mlstm = jax.nn.sigmoid(mo) * rms_norm(hm, m_g.reshape(M_HEADS, M_DV)).reshape(B, T, -1)
    y = jnp.concatenate([ret, mlstm], axis=-1) @ w_out
    return y.astype(h.dtype)

def nsa_mixer(h, w_in, q_g, k_g, pos_k, pos_v, w1k, w2k, w1v, w2v, gate_b, w_out):
    B, T, _ = h.shape
    G, HG, HD = N_KV_GROUPS, N_HEADS // N_KV_GROUPS, HEAD_DIM_2
    z = (h @ w_in).astype(jnp.float32)
    q, kc, vc, ks, vs, kw, vw, gt = split_cols(z, NSA_SIZES)
    q = rms_norm(q.reshape(B, T, G, HG, HD), q_g).transpose(0, 2, 3, 1, 4)

    def kv(t):
        return t.reshape(B, T, G, HD)

    nc = (T - CMP_BLOCK) // CMP_STRIDE + 1
    c_start = jnp.arange(nc) * CMP_STRIDE
    cidx = c_start[:, None] + jnp.arange(CMP_BLOCK)[None, :]

    def compress(t, pos, w1, w2):
        blk = kv(t)[:, cidx] + pos[:, None, :]
        blk = blk.transpose(0, 3, 1, 2, 4).reshape(B, G, nc, CMP_BLOCK * HD)
        return jax.nn.gelu(blk @ w1) @ w2

    kc = rms_norm(compress(kc, pos_k, w1k, w2k), k_g[0])
    vc = compress(vc, pos_v, w1v, w2v)
    ks = rms_norm(kv(ks), k_g[1]).transpose(0, 2, 1, 3)
    vs = kv(vs).transpose(0, 2, 1, 3)
    kw = rms_norm(kv(kw), k_g[2]).transpose(0, 2, 1, 3)
    vw = kv(vw).transpose(0, 2, 1, 3)
    ns = T // SLC_BLOCK
    n_sel = min(N_SELECT, ns)
    ks_blk = ks.reshape(B, G, ns, SLC_BLOCK, HD)
    vs_blk = vs.reshape(B, G, ns, SLC_BLOCK, HD)
    pad = ((0, 0), (0, 0), (WINDOW, 0), (0, 0))
    kw_pad = jnp.pad(kw, pad)
    vw_pad = jnp.pad(vw, pad)
    gates = jax.nn.sigmoid(gt.reshape(B, T, G, HG, 3) + gate_b.reshape(G, HG, 3)).transpose(0, 2, 3, 1, 4)
    cmp_end = c_start + CMP_BLOCK - 1
    sj = jnp.arange(ns)
    overlap = ((c_start[:, None] < (sj[None, :] + 1) * SLC_BLOCK)
               & (c_start[:, None] + CMP_BLOCK > sj[None, :] * SLC_BLOCK)).astype(jnp.float32)
    scale = HD ** -0.5
    bi = jnp.arange(B)[:, None, None, None]
    gi = jnp.arange(G)[None, :, None, None]

    def query_block(qb):
        t0 = qb * Q_BLOCK
        tpos = t0 + jnp.arange(Q_BLOCK)
        qq = lax.dynamic_slice_in_dim(q, t0, Q_BLOCK, axis=3)
        s = jnp.einsum('bghqd,bgnd->bghqn', qq, kc) * scale
        cvalid = cmp_end[None, :] <= tpos[:, None]
        p_c = jnp.where(cvalid, jax.nn.softmax(jnp.where(cvalid, s, NEG), axis=-1), 0.0)
        o_cmp = jnp.einsum('bghqn,bgnd->bghqd', p_c, vc)
        imp = jnp.einsum('bghqn,ns->bgqs', p_c, overlap)
        cur = tpos // SLC_BLOCK
        forced = (sj[None, :] == 0) | (sj[None, :] == cur[:, None]) | (sj[None, :] == cur[:, None] - 1)
        bvalid = sj[None, :] <= cur[:, None]
        score = jnp.where(forced, BIG, jnp.where(bvalid, imp, NEG))
        _, sel = lax.top_k(score, n_sel)
        kg = ks_blk[bi, gi, sel]
        vg = vs_blk[bi, gi, sel]
        kpos = sel[..., None] * SLC_BLOCK + jnp.arange(SLC_BLOCK)
        smask = (kpos <= tpos[:, None, None])[:, :, None]
        s = jnp.einsum('bghqd,bgqnkd->bghqnk', qq, kg) * scale
        s = jnp.where(smask, s, NEG).reshape(B, G, HG, Q_BLOCK, n_sel * SLC_BLOCK)
        p_s = jax.nn.softmax(s, axis=-1).reshape(B, G, HG, Q_BLOCK, n_sel, SLC_BLOCK)
        o_slc = jnp.einsum('bghqnk,bgqnkd->bghqd', p_s, vg)
        kwb = lax.dynamic_slice_in_dim(kw_pad, t0, WINDOW + Q_BLOCK, axis=2)
        vwb = lax.dynamic_slice_in_dim(vw_pad, t0, WINDOW + Q_BLOCK, axis=2)
        wpos = t0 - WINDOW + jnp.arange(WINDOW + Q_BLOCK)
        wmask = ((wpos[None, :] <= tpos[:, None]) & (wpos[None, :] > tpos[:, None] - WINDOW)
                 & (wpos[None, :] >= 0))
        s = jnp.einsum('bghqd,bgkd->bghqk', qq, kwb) * scale
        p_w = jax.nn.softmax(jnp.where(wmask, s, NEG), axis=-1)
        o_win = jnp.einsum('bghqk,bgkd->bghqd', p_w, vwb)
        g = lax.dynamic_slice_in_dim(gates, t0, Q_BLOCK, axis=3)
        return g[..., 0:1] * o_cmp + g[..., 1:2] * o_slc + g[..., 2:3] * o_win

    o = lax.map(query_block, jnp.arange(T // Q_BLOCK))
    o = o.transpose(1, 0, 4, 2, 3, 5).reshape(B, T, N_HEADS * HD)
    return (o @ w_out).astype(h.dtype)

def conv_ffn(h, w_up, conv_w, conv_b, w_down):
    a, b = jnp.split(h @ w_up, 2, axis=-1)
    a = causal_dwconv(a, conv_w, conv_b)
    return (jax.nn.gelu(a) * b) @ w_down

def second_inputs(seed: int = 0) -> dict:
    key = jax.random.key(seed)
    keys = iter(jax.random.split(key, 64))
    f32 = jnp.float32
    NE = (DEPTH + 1) // 2
    NO = DEPTH // 2

    def nrm(shape, scale):
        return scale * jax.random.normal(next(keys), shape, f32)

    def gain(shape):
        return 1.0 + nrm(shape, 0.02)

    return {
        'x': nrm((BATCH, SEQ, D_MODEL), 1.0),
        'p': nrm((DEPTH, BATCH, SEQ, PLE_DIM), 1.0),
        'ab_norm_g': gain((NE, D_MODEL)),
        'ab_w_in': nrm((NE, D_MODEL, AB_COLS), D_MODEL ** -0.5),
        'ab_conv_w': nrm((NE, M_CONV, 2 * M_HEADS * M_DK), M_CONV ** -0.5),
        'ab_conv_b': nrm((NE, 2 * M_HEADS * M_DK), 0.02),
        'ab_ret_norm_g': gain((NE, R_HEADS * R_DV)),
        'ab_ig_b': nrm((NE, M_HEADS), 0.1),
        'ab_fg_b': jnp.linspace(3.0, 6.0, M_HEADS, dtype=f32)[None, :] + nrm((NE, M_HEADS), 0.1),
        'ab_m_norm_g': gain((NE, M_HEADS * M_DV)),
        'ab_w_out': nrm((NE, AB_MIX, D_MODEL), AB_MIX ** -0.5),
        'nsa_norm_g': gain((NO, D_MODEL)),
        'nsa_w_in': nrm((NO, D_MODEL, NSA_COLS), D_MODEL ** -0.5),
        'nsa_q_norm_g': gain((NO, HEAD_DIM_2)),
        'nsa_k_norm_g': gain((NO, 3, HEAD_DIM_2)),
        'nsa_cmp_pos_k': nrm((NO, CMP_BLOCK, HEAD_DIM_2), 0.1),
        'nsa_cmp_pos_v': nrm((NO, CMP_BLOCK, HEAD_DIM_2), 0.1),
        'nsa_cmp_w1k': nrm((NO, CMP_BLOCK * HEAD_DIM_2, CMP_HIDDEN), (CMP_BLOCK * HEAD_DIM_2) ** -0.5),
        'nsa_cmp_w2k': nrm((NO, CMP_HIDDEN, HEAD_DIM_2), CMP_HIDDEN ** -0.5),
        'nsa_cmp_w1v': nrm((NO, CMP_BLOCK * HEAD_DIM_2, CMP_HIDDEN), (CMP_BLOCK * HEAD_DIM_2) ** -0.5),
        'nsa_cmp_w2v': nrm((NO, CMP_HIDDEN, HEAD_DIM_2), CMP_HIDDEN ** -0.5),
        'nsa_gate_b': nrm((NO, N_HEADS * 3), 0.1),
        'nsa_w_out': nrm((NO, N_HEADS * HEAD_DIM_2, D_MODEL), (N_HEADS * HEAD_DIM_2) ** -0.5),
        'ffn_norm_g': gain((DEPTH, D_MODEL)),
        'ffn_w_up': nrm((DEPTH, D_MODEL, 2 * D_FF), D_MODEL ** -0.5),
        'ffn_conv_w': nrm((DEPTH, FFN_CONV, D_FF), FFN_CONV ** -0.5),
        'ffn_conv_b': nrm((DEPTH, D_FF), 0.02),
        'ffn_w_down': nrm((DEPTH, D_FF, D_MODEL), D_FF ** -0.5),
        'ple_w': nrm((DEPTH, PLE_DIM, D_MODEL), PLE_DIM ** -0.5),
        'ple_norm_g': gain((DEPTH, D_MODEL)),
        'ple_gate_norm_g': gain((DEPTH, D_MODEL)),
        'ple_w_gate': nrm((DEPTH, D_MODEL, D_MODEL), D_MODEL ** -0.5),
    }

def second_block(x, p, ab_norm_g, ab_w_in, ab_conv_w, ab_conv_b, ab_ret_norm_g, ab_ig_b, ab_fg_b,
              ab_m_norm_g, ab_w_out, nsa_norm_g, nsa_w_in, nsa_q_norm_g, nsa_k_norm_g,
              nsa_cmp_pos_k, nsa_cmp_pos_v, nsa_cmp_w1k, nsa_cmp_w2k, nsa_cmp_w1v, nsa_cmp_w2v,
              nsa_gate_b, nsa_w_out, ffn_norm_g, ffn_w_up, ffn_conv_w, ffn_conv_b, ffn_w_down,
              ple_w, ple_norm_g, ple_gate_norm_g, ple_w_gate):
    h = x
    for i in range(DEPTH):
        j = i // 2
        if i % 2 == 0:
            h = h + ab_mixer(rms_norm(h, ab_norm_g[j]), ab_w_in[j], ab_conv_w[j], ab_conv_b[j],
                             ab_ret_norm_g[j], ab_ig_b[j], ab_fg_b[j], ab_m_norm_g[j], ab_w_out[j])
        else:
            h = h + nsa_mixer(rms_norm(h, nsa_norm_g[j]), nsa_w_in[j], nsa_q_norm_g[j], nsa_k_norm_g[j],
                              nsa_cmp_pos_k[j], nsa_cmp_pos_v[j], nsa_cmp_w1k[j], nsa_cmp_w2k[j],
                              nsa_cmp_w1v[j], nsa_cmp_w2v[j], nsa_gate_b[j], nsa_w_out[j])
        h = h + conv_ffn(rms_norm(h, ffn_norm_g[i]), ffn_w_up[i], ffn_conv_w[i], ffn_conv_b[i], ffn_w_down[i])
        e = rms_norm(p[i] @ ple_w[i], ple_norm_g[i])
        gate = jax.nn.sigmoid(rms_norm(h, ple_gate_norm_g[i]) @ ple_w_gate[i])
        h = h + gate * e
    return h


def setup_inputs(seed=0):
    out = dict(first_inputs(seed))
    for name, value in second_inputs(seed + 1).items():
        if name != "x":
            out[name + "_2"] = value
    return out


def reference(
    x, c, ctx, c_ctx, mod_w, mod_b, norm_g, ffn_w_gate, ffn_w_up, ffn_w_down, conv_w_pw1,
    conv_b_pw1, conv_w_dw, conv_b_dw, conv_ln_g, conv_ln_b, conv_w_pw2, conv_b_pw2, na_w_qkv,
    na_b_qkv, na_rpb, na_w_o, na_b_o, final_g, p_2, ab_norm_g_2, ab_w_in_2, ab_conv_w_2,
    ab_conv_b_2, ab_ret_norm_g_2, ab_ig_b_2, ab_fg_b_2, ab_m_norm_g_2, ab_w_out_2, nsa_norm_g_2,
    nsa_w_in_2, nsa_q_norm_g_2, nsa_k_norm_g_2, nsa_cmp_pos_k_2, nsa_cmp_pos_v_2, nsa_cmp_w1k_2,
    nsa_cmp_w2k_2, nsa_cmp_w1v_2, nsa_cmp_w2v_2, nsa_gate_b_2, nsa_w_out_2, ffn_norm_g_2,
    ffn_w_up_2, ffn_conv_w_2, ffn_conv_b_2, ffn_w_down_2, ple_w_2, ple_norm_g_2,
    ple_gate_norm_g_2, ple_w_gate_2,
):
    x = first_block(
        x, c, ctx, c_ctx, mod_w, mod_b, norm_g, ffn_w_gate, ffn_w_up, ffn_w_down, conv_w_pw1,
        conv_b_pw1, conv_w_dw, conv_b_dw, conv_ln_g, conv_ln_b, conv_w_pw2, conv_b_pw2,
        na_w_qkv, na_b_qkv, na_rpb, na_w_o, na_b_o, final_g,
    )
    return second_block(
        x, p_2, ab_norm_g_2, ab_w_in_2, ab_conv_w_2, ab_conv_b_2, ab_ret_norm_g_2, ab_ig_b_2,
        ab_fg_b_2, ab_m_norm_g_2, ab_w_out_2, nsa_norm_g_2, nsa_w_in_2, nsa_q_norm_g_2,
        nsa_k_norm_g_2, nsa_cmp_pos_k_2, nsa_cmp_pos_v_2, nsa_cmp_w1k_2, nsa_cmp_w2k_2,
        nsa_cmp_w1v_2, nsa_cmp_w2v_2, nsa_gate_b_2, nsa_w_out_2, ffn_norm_g_2, ffn_w_up_2,
        ffn_conv_w_2, ffn_conv_b_2, ffn_w_down_2, ple_w_2, ple_norm_g_2, ple_gate_norm_g_2,
        ple_w_gate_2,
    )


_drawn_inputs = setup_inputs


def setup_inputs(seed=0):
    import zlib

    import numpy as np

    out = dict(_drawn_inputs(seed))
    spreads = {}
    factors = {'conv_b_pw1': 8.0,
     'conv_b_dw': 4.378,
     'conv_ln_g': 3.309,
     'conv_ln_b': 8.0,
     'conv_b_pw2': 4.296,
     'na_b_qkv': 4.886,
     'na_rpb': 8.0,
     'na_b_o': 4.555,
     'ab_norm_g_2': 2.731,
     'ab_conv_b_2': 6.08,
     'ab_ret_norm_g_2': 7.4,
     'ab_ig_b_2': 200.0,
     'ab_m_norm_g_2': 8.0,
     'nsa_norm_g_2': 8.0,
     'nsa_q_norm_g_2': 8.0,
     'nsa_k_norm_g_2': 8.0,
     'nsa_cmp_pos_k_2': 8.0,
     'nsa_gate_b_2': 6.809,
     'ffn_norm_g_2': 3.084,
     'ffn_conv_b_2': 4.537,
     'ple_norm_g_2': 5.47,
     'ple_gate_norm_g_2': 8.0,
     'nsa_cmp_pos_v_2': 8.0}
    for name, (base, spread) in spreads.items():
        noise = np.random.default_rng([zlib.crc32(name.encode()), seed]).standard_normal(out[name].shape)
        drawn = base * np.exp(spread * noise) if base else spread * noise
        out[name] = jnp.asarray(drawn.astype(out[name].dtype))
    for name, factor in factors.items():
        out[name] = (out[name] * factor).astype(out[name].dtype)
    return out
```

```python
from contextlib import ExitStack

import numpy as np

import concourse.bass as bass
from concourse import mybir

F32 = mybir.dt.float32
ALU = mybir.AluOpType
ACT = mybir.ActivationFunctionType
AX = mybir.AxisListType

P = 128
D = 1024
KC = D // P
T = 256
C = 256
F = 2816
FC = F // P
RING = 11
TILE = 2048
TAPS = 31
PAD = TAPS // 2
UP = T + 2 * PAD
H = 16
DH = 64
GRID = 64
CB = 31
MASKED = -1e30
NC_CMP = 15
PLE = 256
assert FC == 2 * RING


class Stage:
    def __init__(self, w, j, pair, m, part, a):
        self.w, self.j, self.pair, self.m, self.part, self.a = w, j, pair, m, part, a


def plan():
    stages, w, j, pair, m, part, a = {}, 0, 0, 0, 0, 0, 0
    for name, jobs, tiles, mods, parts, acts in (
        ("mod", 0, 0, 8, 0, 0),
        ("gu0", 22, 22, 22, 0, 22), ("down0", 8, RING, 0, 7, 0),
        ("pw1", 8, 8, 8, 0, 8), ("pw2", 4, 4, 4, 0, 0),
        ("gu1", 22, 22, 22, 0, 22), ("down1", 8, RING, 0, 7, 0),
        ("gu2", 22, 22, 0, 0, 22), ("down2", 8, RING, 0, 7, 0),
        ("na_qk", 8, 8, 8, 0, 0), ("na_v", 8, 4, 0, 4, 0), ("na_o", 4, 4, 0, 0, 0),
        ("gu3", 22, 22, 0, 0, 22), ("down3", 8, RING, 0, 7, 0),
        ("ab_in", 12, 12, 0, 0, 0), ("ab_out", 4, 4, 0, 0, 0),
        ("gu4", 22, 22, 0, 0, 22), ("down4", 8, RING, 0, 7, 0),
        ("ple_e0", 4, 1, 0, 3, 0), ("ple_g0", 4, 4, 0, 0, 4),
        ("nsa_in", 8, 8, 0, 0, 0), ("nsa_mlp", 2, 4, 0, 0, 0), ("nsa_out", 4, 4, 0, 0, 0),
        ("gu5", 22, 22, 0, 0, 22), ("down5", 8, RING, 0, 7, 0),
        ("ple_e1", 4, 1, 0, 3, 0), ("ple_g1", 4, 4, 0, 0, 4),
    ):
        stages[name] = Stage(w, j, pair, m, part, a)
        w, j, pair = w + tiles + mods, j + jobs, (pair + jobs) % 3
        m, part, a = m + mods, part + parts, a + acts
    assert m == 72
    return stages, w, j


STAGES, NTILES, NJOBS = plan()

COLS = {}
_at = 0
for _name, _n in (
    ("cond", 2 * KC), ("mod_b", 288), ("norm_g", 6 * KC), ("b_pw1", 2 * KC), ("w_dw", TAPS * KC),
    ("b_dw", KC), ("ln_g", KC), ("ln_b", KC), ("b_pw2", KC), ("b_qkv", 3 * KC), ("b_o", KC),
    ("final_g", KC), ("ab_norm_g", KC), ("ab_conv_w", 4 * 4), ("ab_conv_b", 4), ("ret_g", 4),
    ("m_g", 4), ("gate_bias", 2), ("ab_wgate", 8 * KC), ("nsa_norm_g", KC), ("q_g", 1), ("k_g", 3),
    ("pos_k", 16), ("pos_v", 16), ("gate_b", 48), ("nsa_wgate", 48 * KC), ("w2k", 2 * DH),
    ("w2v", 2 * DH), ("ffn_norm_g", 2 * KC), ("ffn_conv_w", 2 * 3 * FC), ("ffn_conv_b", 2 * FC),
    ("ple_norm_g", 2 * KC), ("ple_gate_norm_g", 2 * KC),
):
    COLS[_name] = (_at, _n)
    _at += _n
NCOLS = _at

CONST = {}
_at = 0
for _name, _n in (
    ("ident", P), ("mean_all", P), ("ones", P), ("mean64", P), ("mean128", P), ("rot", P),
    ("cos", T), ("sin", T), ("causal", P), ("causal_t", P), ("decay", 4 * T), ("window", GRID),
    ("cmp_add", 2 * 16), ("cmp_valid", 2 * 16), ("sel", 4 * P), ("eps6", 1), ("eps5", 1), ("one", 1),
):
    CONST[_name] = (_at, _n)
    _at += _n
NCONST = _at


def build(nc, x_in, params, consts, weights, rpb, p_in, out):
    ctx = ExitStack()
    with ctx:
        def sb(name, shape):
            return ctx.enter_context(nc.sbuf_tensor(name, shape, F32))

        def sem(name):
            return ctx.enter_context(nc.semaphore(name))

        ring = [sb(f"weights{s}", [P, TILE]) for s in range(RING)]
        X = sb("X", [P, KC, T + C])
        HN = sb("HN", [P, KC, T + C])
        hid = sb("hid", [P, FC * (T + C)])
        G = sb("G", [P, 3, T + C])
        SQ = sb("SQ", [P, 2, T + C])
        STD = sb("STD", [P, T + C])
        cols = sb("cols", [P, NCOLS])
        con = sb("con", [P, NCONST])
        MOD = sb("MOD", [P, 144, 2])
        A = sb("A", [P, KC, 2])
        GT = sb("GT", [P, KC, 2])
        bank = [ctx.enter_context(nc.psum_tensor(f"bank{b}", [P, 512], F32)) for b in range(8)]

        def col(name, a=0, n=1):
            return cols[:, COLS[name][0] + a:COLS[name][0] + a + n]

        def const(name, a=0, n=None):
            at, size = CONST[name]
            return con[:, at + a:at + a + (size - a if n is None else n)]

        def mod(layer, n):
            a = layer * 72 + n * KC
            return MOD[:, a:a + KC, :]

        HID = hid[:, :].rearrange("p (f t) -> p f t", f=FC)
        nU = KC * 2 * UP
        U = hid[:, 0:nU].rearrange("p (c s t) -> p c s t", c=KC, s=2)
        CV = hid[:, nU:nU + KC * 512].rearrange("p (c t) -> p c t", c=KC)
        NQ = hid[:, 0:2048].rearrange("p (c t) -> p c t", c=KC)
        NK = hid[:, 2048:6144].rearrange("p (c t) -> p c t", c=KC)
        NV = hid[:, 6144:10240].rearrange("p (s d) -> p s d", s=4)
        NP = hid[:, 10240:11264].rearrange("p (b k) -> p b k", b=2)
        RB_T = sb("bias_rows", [P, 2, 6 * GRID])
        RBT = sb("bias_masked", [P, 2, 6 * GRID])
        SC = sb("SC", [P, KC, 2])
        MODU = MOD[:, :, :].rearrange("p (m f) s -> p m (f s)", f=2)
        MODB = cols[:, COLS["mod_b"][0]:COLS["mod_b"][0] + 288].rearrange("p (m x) -> p m x", x=4)

        landed = [sem(f"landed{s}") for s in range(RING)]
        tile_used = sem("tile_used")
        params_in = sem("params_in")
        consts_in = sem("consts_in")
        x_loaded = sem("x_loaded")
        cond_ready = sem("cond_ready")
        part_done = sem("part_done")
        drained = sem("drained")
        act_out = sem("act_out")
        mod_drained = sem("mod_drained")
        sq_ready = sem("sq_ready")
        sq_used = sem("sq_used")
        std_ready = sem("std_ready")
        scaled = sem("scaled")
        h_ready = sem("h_ready")
        v_step = sem("v_step")
        a_step = sem("a_step")
        out_sent = sem("out_sent")
        conv_out = sem("conv_out")
        gelu_out = sem("gelu_out")
        cv_ready = sem("cv_ready")
        mu_ready = sem("mu_ready")
        cv_centred = sem("cv_centred")
        cvn_ready = sem("cvn_ready")
        bias_in = [sem(f"bias_in{b}") for b in range(2)]
        bias_ready = sem("bias_ready")
        s_ready = sem("s_ready")
        s_max = sem("s_max")
        p_ready = sem("p_ready")
        dg_ready = sem("dg_ready")
        pt_ready = sem("pt_ready")
        pts_ready = sem("pts_ready")
        o_ready = sem("o_ready")
        o_out = sem("o_out")

        DG = sb("DG", [P, 2, P])
        PTS = G[:, 0:2, :].rearrange("p a b -> p (a b)").rearrange("p (k q) -> p k q", k=4)
        PTS2 = SQ[:, :, :].rearrange("p a b -> p (a b)").rearrange("p (k q) -> p k q", k=4)
        NM = sb("NM", [P, 64])
        SUM = sb("SUM", [P, 64])
        RSUM = sb("RSUM", [P, 64])

        norm_no = {n: i for i, n in enumerate(
            ("ffn0", "conv", "ln", "ffn1", "ffn2", "na", "ffn3", "final",
             "ab", "ffn4", "e0", "pg0", "nsa", "ffn5", "e1", "pg1"))}
        shift_no = {n: i for i, n in enumerate(("ffn0", "conv", "ffn1", "ffn2", "na", "ffn3"))}


        PIN = X[:, 0:4, T:2 * T]
        EMT = HN[:, 0:4, T:2 * T]
        DEN = HN[:, 4:6, T:2 * T]
        E = hid[:, 0:2048].rearrange("p (c t) -> p c t", c=KC)
        RQK = hid[:, 0:1024].rearrange("p (c t) -> p c t", c=4)
        MQK = hid[:, 1024:2048].rearrange("p (c t) -> p c t", c=4)
        RG = hid[:, 2048:3072].rearrange("p (c t) -> p c t", c=4)
        MO = hid[:, 3072:4096].rearrange("p (c t) -> p c t", c=4)
        RV = hid[:, 4096:5120].rearrange("p (s d) -> p s d", s=2)
        MV = hid[:, 5120:6144].rearrange("p (s d) -> p s d", s=2)
        MPAD = hid[:, 6144:6144 + 4 * 260].rearrange("p (c t) -> p c t", c=4)
        SW = hid[:, 7200:7200 + 768].rearrange("p (e t) -> p e t", e=2)
        IG, XF, LROW, BROW, AROW, MROW, NMT = (hid[:, 8000 + T * n:8000 + T * (n + 1)] for n in range(7))
        ACOL = hid[:, 9800:9808]
        WT = G[:, :, :].rearrange("p a b -> p (a b)").rearrange("p (h t) -> p h t", h=4)
        ones_row = con[0:4, CONST["ones"][0]:CONST["ones"][0] + 1].to_broadcast([4, T])
        sel = const("sel").rearrange("p (h q) -> p h q", h=4)
        ab_wgate = col("ab_wgate", 0, 8 * KC).rearrange("p (k n) -> p k n", k=KC)
        gb = COLS["gate_bias"][0]
        AB_SRC = [(RQK[:, c, :], RQK[:, 2 + c, :], RV) for c in range(2)] + \
                 [(MQK[:, c, :], MQK[:, 2 + c, :], MV) for c in range(2)]
        AB_BASE = [0, 7, 14, 22, 30]
        ffn_conv_w = col("ffn_conv_w", 0, 6 * FC).rearrange("p (j f o) -> p j f o", j=6, o=1)
        ffn_conv_b = col("ffn_conv_b", 0, 2 * FC).rearrange("p (j f o) -> p j f o", j=2, o=1)
        QK = hid[:, 0:2560].rearrange("p (c t) -> p c t", c=10)
        BLK = hid[:, 2560:3520].rearrange("p (m k n) -> p m k n", m=2, k=16)
        SV = hid[:, 3520:4032].rearrange("p (s d) -> p s d", s=2)
        GATE = hid[:, 4032:4128]
        HC = hid[:, 4128:4248].rearrange("p (m f n) -> p m f n", m=2, f=2)
        KCN = hid[:, 4248:4263]
        VCS = hid[:, 4264:4392]
        PC = hid[:, 4392:4904].rearrange("p (t h n) -> p t h n", t=2, h=H)
        CM = hid[:, 4904:4936].rearrange("p (t h) -> p t h", t=2)
        QG = hid[:, 4936:4937]
        PTC = hid[:, 4944:5456].rearrange("p (n q) -> p n q", n=2)
        NP2 = hid[:, 5456:6480].rearrange("p (b k) -> p b k", b=2)
        DG2 = hid[:, 6480:6992].rearrange("p (u b q) -> p u b q", u=2, b=2)
        nsa_wgate = col("nsa_wgate", 0, 48 * KC).rearrange("p (k n) -> p k n", k=KC)
        w2k = col("w2k", 0, 2 * DH).rearrange("p (f n) -> p f n", f=2)
        w2v = col("w2v", 0, 2 * DH).rearrange("p (f n) -> p f n", f=2)
        cmp_add = const("cmp_add").rearrange("p (t n) -> p t n", t=2)
        cmp_valid = const("cmp_valid").rearrange("p (t n) -> p t n", t=2)
        p_loaded = sem("p_loaded")
        gate_step = sem("gate_step")
        ab_step = sem("ab_step")
        nsa_step = sem("nsa_step")
        rotated = sem("rotated")
        rope_done = sem("rope_done")
        mconv_ready = sem("mconv_ready")
        mqk_ready = sem("mqk_ready")
        rg_ready = sem("rg_ready")
        mo_ready = sem("mo_ready")
        tap_out = sem("tap_out")
        qsq_ready = sem("qsq_ready")
        qmean_ready = sem("qmean_ready")
        qstd_ready = sem("qstd_ready")
        qn_ready = sem("qn_ready")
        ngate_ready = sem("ngate_ready")
        pc_exp = sem("pc_exp")
        ns_ready = sem("ns_ready")
        ns_max = sem("ns_max")
        np_ready = sem("np_ready")
        ndg_ready = sem("ndg_ready")
        npt_ready = sem("npt_ready")
        npts_ready = sem("npts_ready")
        no_ready = sem("no_ready")
        no_out = sem("no_out")

        block = ctx.enter_context(nc.Block())

        @block.sync
        def _(sp):
            sp.dma_start(cols[:, :], params).then_inc(params_in, 16)
            sp.dma_start(con[:, :], consts).then_inc(consts_in, 16)

            def load(n, i=0, first=False):
                s = n % RING
                if not first:
                    sp.wait_ge(tile_used, n - RING + 1 + RING * i)
                sp.dma_start(ring[s][:, :], weights[n + RING * i, :, :]).then_inc(landed[s], 16)

            for n in range(RING):
                load(n, first=True)
                if n == 3:
                    sp.dma_start(X[:, :, :], x_in).then_inc(x_loaded, 16)
            laps = (NTILES - RING) // RING
            with sp.Fori(0, laps) as i:
                for n in range(RING):
                    load(RING + n, i)
            for n in range(RING * (laps + 1), NTILES):
                load(n)

            sp.wait_ge(drained, NJOBS)
            sp.dma_start(out, X[:, :, 0:T]).then_inc(out_sent, 16)
            sp.wait_ge(out_sent, 16)

        def pair_banks(pair):
            return bank[2 + 2 * (pair % 3)], bank[3 + 2 * (pair % 3)]

        @block.tensor
        def _(pe):
            def tile(n, i=0, laps=1):
                pe.wait_ge(landed[n % RING], 16 * (n // RING + 1) + 16 * laps * i)
                return ring[n % RING]

            def banks_free(j, i=0):
                if j >= 2:
                    pe.wait_ge(drained, j - 1 + RING * i)

            def mod_unit(m, w, i=0):
                W = tile(w, i, 2)[:, :].rearrange("p (k n) -> p k n", k=KC)
                if m >= 1:
                    pe.wait_ge(mod_drained, m + RING * i)
                for f in range(2):
                    for k in range(KC):
                        mm = nc.tensor.matmul(bank[0][:, 2 * f:2 * f + 2],
                                              W[:, k, f * P:(f + 1) * P], SC[:, k, :],
                                              start=(k == 0), stop=(k == KC - 1))
                mm.then_inc(tile_used, 1)

            def pair_job(j, w, pair, n, src, norm=None, i=0, laps=1):
                W = tile(w, i, laps)[:, :].rearrange("p (k n) -> p k n", k=KC)
                banks_free(j, i)
                a, b = pair_banks(pair)
                for k in range(KC):
                    if norm is not None:
                        pe.wait_ge(h_ready, KC * norm_no[norm] + k + 1)
                    for f, ps in enumerate((a, b)):
                        mm = nc.tensor.matmul(ps[:, 0:n], W[:, k, f * P:(f + 1) * P], src[:, k, 0:n],
                                              start=(k == 0), stop=(k == KC - 1))
                mm.then_inc(tile_used, 1)

            def gate_up(name, n, norm, mods=False):
                S = STAGES[name]
                laps = 2 if mods else 1
                with pe.Fori(0, 2) as i:
                    for k in range(RING):
                        pair_job(S.j + k, S.w + laps * k, S.pair + k, n, HN, norm, i, laps)
                        if mods:
                            mod_unit(S.m + k, S.w + 2 * k + 1, i)

            def down(name, n, mods=0):
                S = STAGES[name]
                pe.wait_ge(drained, S.j)
                if mods:
                    pe.wait_ge(mod_drained, mods)
                for t in range(RING):
                    W = tile(S.w + t)[:, :].rearrange("p (k n) -> p k n", k=2)
                    if t < RING - 1:
                        for k in range(2):
                            for f in range(KC):
                                mm = nc.tensor.matmul(bank[f][:, 0:n], W[:, k, f * P:(f + 1) * P],
                                                      HID[:, 2 * t + k, 0:n],
                                                      start=(t == 0 and k == 0), stop=False)
                        mm.then_inc(tile_used, 1)
                    else:
                        for f in range(KC):
                            for k in range(2):
                                mm = nc.tensor.matmul(bank[f][:, 0:n], W[:, k, f * P:(f + 1) * P],
                                                      HID[:, 2 * t + k, 0:n], start=False, stop=(k == 1))
                            mm.then_inc(part_done if f < KC - 1 else tile_used, 1)

            def stats(name, n, mods=0):
                if mods:
                    pe.wait_ge(mod_drained, mods)
                for c in range(KC):
                    pe.wait_ge(sq_ready, KC * norm_no[name] + c + 1)
                    nc.tensor.matmul(bank[0][:, 0:n], const("mean_all"), SQ[:, c % 2, 0:n],
                                     start=(c == 0), stop=(c == KC - 1)).then_inc(sq_used, 1)


            def token_job(j, w, pair):
                W = tile(w)[:, :].rearrange("p (k n) -> p k n", k=KC)
                banks_free(j)
                for s, ps in enumerate(pair_banks(pair)):
                    for k in range(KC):
                        mm = nc.tensor.matmul(ps[:, 0:256], HN[:, k, s * P:(s + 1) * P], W[:, k, :],
                                              start=(k == 0), stop=(k == KC - 1))
                mm.then_inc(tile_used, 1)

            def conv_ffn(i):
                stats(f"ffn{4 + i}", T)
                gate_up(f"gu{4 + i}", T, f"ffn{4 + i}")
                down(f"down{4 + i}", T)

            def per_layer(i):
                S = STAGES[f"ple_e{i}"]
                pe.wait_ge(p_loaded, 16)
                W = tile(S.w)[:, :].rearrange("p (k n) -> p k n", k=2)
                pe.wait_ge(drained, S.j)
                for j in range(4):
                    banks_free(S.j + j)
                    for f, ps in enumerate(pair_banks(S.pair + j)):
                        for k in range(2):
                            mm = nc.tensor.matmul(ps[:, 0:T], W[:, k, (2 * j + f) * P:(2 * j + f + 1) * P],
                                                  PIN[:, 2 * i + k, :], start=(k == 0), stop=(k == 1))
                    mm.then_inc(part_done if j < 3 else tile_used, 1)
                stats(f"e{i}", T)
                stats(f"pg{i}", T)
                S = STAGES[f"ple_g{i}"]
                for k in range(4):
                    pair_job(S.j + k, S.w + k, S.pair + k, T, HN, f"pg{i}")

            pe.wait_ge(cond_ready, 1)
            for m in range(8):
                mod_unit(m, m)
            pe.wait_ge(consts_in, 16)
            stats("ffn0", T + C, mods=8)
            gate_up("gu0", T + C, "ffn0", mods=True)
            down("down0", T + C, mods=STAGES["pw1"].m)
            stats("conv", T + C)
            S = STAGES["pw1"]
            for k in range(8):
                pair_job(S.j + k, S.w + 2 * k, S.pair + k, T + C, HN, "conv")
                mod_unit(S.m + k, S.w + 2 * k + 1)
            pe.wait_ge(mod_drained, STAGES["pw2"].m)
            for c in range(KC):
                pe.wait_ge(cv_ready, c + 1)
                mm = nc.tensor.matmul(bank[1][:, :], const("mean_all"), CV[:, c, :],
                                      start=(c == 0), stop=(c == KC - 1))
            mm.then_inc(mu_ready, 1)
            stats("ln", T + C)
            S = STAGES["pw2"]
            for k in range(4):
                pair_job(S.j + k, S.w + 2 * k, S.pair + k, T + C, HN, "ln")
                mod_unit(S.m + k, S.w + 2 * k + 1)
            stats("ffn1", T + C, mods=STAGES["gu1"].m)
            gate_up("gu1", T + C, "ffn1", mods=True)
            down("down1", T + C, mods=STAGES["gu2"].m)
            stats("ffn2", T + C)
            gate_up("gu2", T + C, "ffn2")
            down("down2", T + C)
            stats("na", T + C)
            S = STAGES["na_qk"]
            for k in range(8):
                pair_job(S.j + k, S.w + 2 * k, S.pair + k, T if k < 4 else T + C, HN, "na")
                mod_unit(S.m + k, S.w + 2 * k + 1)
            S = STAGES["na_v"]
            for k in range(4):
                W = tile(S.w + k)[:, :].rearrange("p (k n) -> p k n", k=KC)
                for half in range(2):
                    j = 2 * k + half
                    banks_free(S.j + j)
                    for ps, s in zip(pair_banks(S.pair + j), (2 * half, 2 * half + 1)):
                        for kk in range(KC):
                            mm = nc.tensor.matmul(ps[:, 0:256], HN[:, kk, s * P:(s + 1) * P], W[:, kk, :],
                                                  start=(kk == 0), stop=(kk == KC - 1))
                    mm.then_inc(part_done if half == 0 else tile_used, 1)
            pe.wait_ge(drained, STAGES["na_o"].j)

            def scores(u):
                h, t = u // 2, u % 2
                r = DH * (h % 2)
                if u >= 4:
                    pe.wait_ge(p_ready, u - 3)
                nc.tensor.matmul(bank[u % 4][:, :], NQ[r:r + DH, h // 2, t * P:(t + 1) * P],
                                 NK[r:r + DH, h // 2, :], start=True, stop=True).then_inc(s_ready, 1)

            def transposed(u):
                pe.wait_ge(dg_ready, u + 1)
                if u >= 2:
                    pe.wait_ge(pts_ready, u - 1)
                for k in range(4):
                    mm = nc.tensor.matmul(bank[4 + u % 2][:, k * P:(k + 1) * P],
                                          NP[:, u % 2, k * P:(k + 1) * P], DG[:, u % 2, :],
                                          start=True, stop=True)
                mm.then_inc(pt_ready, 1)

            def outputs(h):
                r = DH * (h % 2)
                pe.wait_ge(pts_ready, 2 * h + 2)
                if h >= 2:
                    pe.wait_ge(o_out, h - 1)
                pt = (PTS, PTS2)[h % 2]
                for k in range(4):
                    mm = nc.tensor.matmul(bank[6 + h % 2][r:r + DH, 0:T], NV[:, k, h * DH:(h + 1) * DH],
                                          pt[:, k, :], start=(k == 0), stop=(k == 3))
                mm.then_inc(o_ready, 1)

            for u in range(2 * H + 3):
                if u < 2 * H:
                    scores(u)
                if 1 <= u <= 2 * H:
                    transposed(u - 1)
                if u >= 3 and u % 2 == 1:
                    outputs((u - 3) // 2)
            S = STAGES["na_o"]
            pe.wait_ge(o_out, H)
            for k in range(4):
                pair_job(S.j + k, S.w + k, S.pair + k, T, HN)
            stats("ffn3", T)
            gate_up("gu3", T, "ffn3")
            down("down3", T)
            stats("final", T)

            stats("ab", T)
            S = STAGES["ab_in"]
            for k in range(12):
                if k in (2, 3, 8, 9):
                    token_job(S.j + k, S.w + k, S.pair + k)
                else:
                    pair_job(S.j + k, S.w + k, S.pair + k, T, HN, "ab")
            for b, ps in enumerate((bank[0], bank[1])):
                for k in range(KC):
                    mm = nc.tensor.matmul(ps[0:4, 0:T], ab_wgate[:, k, 4 * b:4 * b + 4], HN[:, k, 0:T],
                                          start=(k == 0), stop=(k == KC - 1))
            mm.then_inc(gate_step, 1)
            pe.wait_ge(drained, S.j + 12)
            for c in range(4):
                nc.tensor.matmul(bank[4 + c][:, 0:T], const("rot"), RQK[:, c, :], start=True, stop=True)\
                    .then_inc(rotated, 1)
            pe.wait_ge(gate_step, 4)
            for s in range(2):
                nc.tensor.matmul(bank[0][:, 4 * s:4 * s + 4], AROW[0:4, s * P:(s + 1) * P], con[0:4, 0:4],
                                 start=True, stop=True)
            for h in range(4):
                nc.tensor.matmul(bank[2 + h // 2][:, (h % 2) * T:(h % 2 + 1) * T], sel[0:4, h, :],
                                 MROW[0:4, :], start=True, stop=True)
            pe.wait_ge(rope_done, 4)
            for h in range(4):
                mm = nc.tensor.matmul(bank[4 + h // 2][:, (h % 2) * T:(h % 2 + 1) * T], sel[0:4, h, :],
                                      NMT[0:4, :], start=True, stop=True)
            mm.then_inc(gate_step, 1)
            pe.wait_ge(gate_step, 7)
            for pr in range(4):
                q, k, v = AB_SRC[pr]
                base = AB_BASE[pr]
                if pr:
                    pe.wait_ge(ab_step, base)
                else:
                    pe.wait_ge(mqk_ready, 4)
                for e in range(2):
                    r = slice(DH * e, DH * e + DH)
                    nc.tensor.matmul(bank[2 + e][:, 0:T], k[r, 0:P], q[r, :], start=True, stop=True)
                    mm = nc.tensor.matmul(bank[2 + e][:, T:T + P], k[r, P:T], q[r, P:T],
                                          start=True, stop=True)
                mm.then_inc(ab_step, 1)
                pe.wait_ge(ab_step, base + 2)
                for e in range(2):
                    h = 2 * (pr % 2) + e
                    for ps, w0, w1 in ((bank[6], v[:, 0, h * P:(h + 1) * P], v[:, 1, h * P:(h + 1) * P]),
                                       (bank[7], const("ones"), const("ones")))[:1 + pr // 2]:
                        nc.tensor.matmul(ps[:, e * T:(e + 1) * T], w0, SW[:, e, 0:T], start=True, stop=False)
                        mm = nc.tensor.matmul(ps[:, e * T + P:(e + 1) * T], w1, SW[:, e, T:T + P],
                                              start=False, stop=True)
                mm.then_inc(ab_step, 1)
                pe.wait_ge(ab_step, base + 4 + pr // 2)
                nc.tensor.matmul(bank[0][:, :], const("mean128"), SQ[:, 0, :], start=True, stop=True)\
                    .then_inc(ab_step, 1)
            S = STAGES["ab_out"]
            pe.wait_ge(ab_step, AB_BASE[4])
            for k in range(4):
                pair_job(S.j + k, S.w + k, S.pair + k, T, HN)
            conv_ffn(0)
            per_layer(0)
            stats("nsa", T)
            S = STAGES["nsa_in"]
            for k in range(7):
                pair_job(S.j + k, S.w + k, S.pair + k, T, HN, "nsa")
            token_job(S.j + 7, S.w + 7, S.pair + 7)
            for s in range(2):
                for k in range(KC):
                    mm = nc.tensor.matmul(bank[0][:, s * 48:(s + 1) * 48], HN[:, k, s * P:(s + 1) * P],
                                          nsa_wgate[:, k, :], start=(k == 0), stop=(k == KC - 1))
            mm.then_inc(nsa_step, 1)
            for n in range(5):
                pe.wait_ge(qsq_ready, n + 1)
                if n >= 1:
                    pe.wait_ge(qstd_ready, n)
                nc.tensor.matmul(bank[1][:, :], const("mean64"), SQ[:, n % 2, :], start=True, stop=True)\
                    .then_inc(qmean_ready, 1)
            S = STAGES["nsa_mlp"]
            pe.wait_ge(drained, S.j)
            for m in range(2):
                banks_free(S.j + m)
                for t in range(2):
                    W = tile(S.w + 2 * m + t)[:, :].rearrange("p (k n) -> p k n", k=KC)
                    for k in range(KC):
                        for f, ps in enumerate(pair_banks(S.pair + m)):
                            mm = nc.tensor.matmul(ps[:, 0:30], W[:, k, f * P:(f + 1) * P],
                                                  BLK[:, m, 8 * t + k, :], start=(t == 0 and k == 0),
                                                  stop=(t == 1 and k == KC - 1))
                    mm.then_inc(tile_used, 1)
            pe.wait_ge(nsa_step, 3)
            for g in range(2):
                for f in range(2):
                    nc.tensor.matmul(bank[1][g * DH:(g + 1) * DH, 0:15], w2k[:, f, :],
                                     HC[:, 0, f, g * 15:(g + 1) * 15], start=(f == 0), stop=(f == 1))
            for g in range(2):
                for f in range(2):
                    mm = nc.tensor.matmul(bank[0][0:15, g * DH:(g + 1) * DH], HC[:, 1, f, g * 15:(g + 1) * 15],
                                          w2v[:, f, :], start=(f == 0), stop=(f == 1))
            mm.then_inc(nsa_step, 1)
            pe.wait_ge(nsa_step, 5)
            nc.tensor.matmul(bank[2][:, 0:15], const("mean64"), SQ[:, 0, 0:15], start=True, stop=True)\
                .then_inc(nsa_step, 1)
            pe.wait_ge(nsa_step, 8)
            for t in range(2):
                for h in range(H):
                    r = DH * (h // 8)
                    mm = nc.tensor.matmul(bank[2 + 2 * t + h // 8][:, 16 * (h % 8):16 * (h % 8) + 15],
                                          QK[r:r + DH, h % 8, t * P:(t + 1) * P], KCN[r:r + DH, :],
                                          start=True, stop=True)
            mm.then_inc(nsa_step, 1)

            def nsa_scores(u):
                c, g, t = u // 4, u // 2 % 2, u % 2
                r, n = DH * g, P * (t + 1)
                if u >= 3:
                    pe.wait_ge(np_ready, u - 2)
                for b in range(2):
                    mm = nc.tensor.matmul(bank[u % 3][:, b * n:(b + 1) * n],
                                          QK[r:r + DH, c, t * P:(t + 1) * P], QK[r:r + DH, 8 + b, 0:n],
                                          start=True, stop=True)
                mm.then_inc(ns_ready, 1)

            def nsa_transposed(u):
                h, t = u // 4 + 8 * (u // 2 % 2), u % 2
                pe.wait_ge(ndg_ready, u + 1)
                if u >= 2:
                    pe.wait_ge(npts_ready, u - 1)
                ps = bank[3 + u % 2]
                for b in range(2):
                    for k in range(t + 1):
                        n = b * (t + 1) + k
                        mm = nc.tensor.matmul(ps[:, n * P:(n + 1) * P], NP2[:, u % 2, n * P:(n + 1) * P],
                                              DG2[:, u % 2, b, :], start=True, stop=True)
                if t == 0:
                    for s in range(2):
                        mm = nc.tensor.matmul(ps[0:15, (2 + s) * P:(3 + s) * P], PC[:, s, h, 0:15],
                                              const("ident"), start=True, stop=True)
                mm.then_inc(npt_ready, 1)

            def nsa_outputs(n):
                g = n % 2
                r = DH * g
                pe.wait_ge(npts_ready, 2 * n + 2)
                if n >= 2:
                    pe.wait_ge(no_out, n - 1)
                ps = bank[6 + n % 2]
                pt = (PTS, PTS2)[n % 2]
                nc.tensor.matmul(ps[r:r + DH, 0:T], VCS[0:15, g * DH:(g + 1) * DH], PTC[0:15, n % 2, :],
                                 start=True, stop=False)
                for b in range(2):
                    v = SV[:, :, 2 * b * DH + g * DH:2 * b * DH + (g + 1) * DH]
                    nc.tensor.matmul(ps[r:r + DH, 0:T], v[:, 0, :], pt[:, 2 * b, :], start=False, stop=False)
                    mm = nc.tensor.matmul(ps[r:r + DH, P:T], v[:, 1, :], pt[:, 2 * b + 1, P:T],
                                          start=False, stop=(b == 1))
                mm.then_inc(no_ready, 1)

            pe.wait_ge(nsa_step, 11)
            for u in range(2 * H + 3):
                if u < 2 * H:
                    nsa_scores(u)
                if 1 <= u <= 2 * H:
                    nsa_transposed(u - 1)
                if u >= 3 and u % 2 == 1:
                    nsa_outputs((u - 3) // 2)
            S = STAGES["nsa_out"]
            pe.wait_ge(no_out, H)
            for k in range(4):
                pair_job(S.j + k, S.w + k, S.pair + k, T, HN)
            conv_ffn(1)
            per_layer(1)

        @block.scalar
        def _(act):
            chain = [0]

            def link(ins):
                chain[0] += 1
                ins.then_inc(a_step, 1)
                act.wait_ge(a_step, chain[0])

            def job(name, k, i=0, laps=1):
                S = STAGES[name]
                act.wait_ge(tile_used, S.w + laps * k + 1 + RING * laps * i)
                if S.j + k >= 2:
                    act.wait_ge(drained, S.j + k - 1 + RING * i)
                return pair_banks(S.pair + k), (S.pair + k) % 3

            def norm(name, n, ready, shift=None, src=X, eps="eps6", dst=HN):
                m = norm_no[name]
                for c in range(KC):
                    ready(c)
                    if m > 0 or c >= 2:
                        act.wait_ge(sq_used, KC * m + c - 1)
                    nc.scalar.activation(SQ[:, c % 2, 0:n], src[:, c, 0:n], ACT.Square)\
                        .then_inc(sq_ready, 1)
                act.wait_ge(sq_used, KC * (m + 1))
                nc.scalar.activation(STD[:, 0:n], bank[0][:, 0:n], ACT.Sqrt, bias=const(eps))\
                    .then_inc(std_ready, 1)
                if shift is not None:
                    for c in range(KC):
                        act.wait_ge(scaled, KC * shift_no[name] + c + 1)
                        for s in range(n // T):
                            ins = nc.scalar.activation(HN[:, c, s * T:(s + 1) * T], HN[:, c, s * T:(s + 1) * T],
                                                       ACT.Identity, bias=shift[:, c, s:s + 1])
                        ins.then_inc(h_ready, 1)

            def x_from(name, per=1):
                return lambda c: act.wait_ge(drained, STAGES[name].j + c // per + 1)

            def silu_gate(name, n, mods=False):
                laps = 2 if mods else 1
                with act.Fori(0, 2) as i:
                    for k in range(RING):
                        (a, b), g = job(name, k, i, laps)
                        nc.scalar.activation(G[:, g, 0:n], a[:, 0:n], ACT.Silu).then_inc(act_out, 1)


            def conv_ffn(i, before):
                norm(f"ffn{4 + i}", T, x_from(before, 2))
                with act.Fori(0, 2) as it:
                    for k in range(RING):
                        (a, b), g = job(f"gu{4 + i}", k, it)
                        n = 2 * RING * i + k + 1
                        nc.scalar.activation(G[:, g, 0:T], a[:, 0:T], ACT.Identity,
                                             scale=ffn_conv_w[:, 3 * i + 2, k + RING * it],
                                             bias=ffn_conv_b[:, i, k + RING * it]).then_inc(act_out, 1)
                        act.wait_ge(conv_out, n + RING * it)
                        nc.scalar.activation(G[:, g, T:2 * T], G[:, g, 0:T], ACT.Gelu_apprx_tanh)\
                            .then_inc(gelu_out, 1)

            def per_layer(i):
                norm(f"e{i}", T, x_from(f"ple_e{i}", 2), src=E)
                act.wait_ge(h_ready, KC * norm_no[f"e{i}"] + 1)
                norm(f"pg{i}", T, x_from(f"down{4 + i}"))
                for k in range(4):
                    (a, b), g = job(f"ple_g{i}", k)
                    nc.scalar.activation(G[:, g, 0:T], a[:, 0:T], ACT.Sigmoid)
                    nc.scalar.activation(G[:, g, T:2 * T], b[:, 0:T], ACT.Sigmoid).then_inc(act_out, 1)

            act.wait_ge(params_in, 16)
            nc.scalar.activation(SC[:, :, :], col("cond", 0, 2 * KC).rearrange("p (k s) -> p k s", s=2),
                                 ACT.Silu).then_inc(cond_ready, 1)
            act.wait_ge(consts_in, 16)
            norm("ffn0", T + C, lambda c: act.wait_ge(x_loaded, 16), mod(0, 0))
            silu_gate("gu0", T + C, True)
            norm("conv", T + C, x_from("down0"), mod(0, 3))
            for k in range(8):
                (a, b), g = job("pw1", k, 0, 2)
                nc.scalar.activation(G[:, g, :], b[:, :], ACT.Sigmoid, bias=col("b_pw1", KC + k))\
                    .then_inc(act_out, 1)
            norm("ln", T + C, lambda c: act.wait_ge(cv_centred, c + 1), src=CV, eps="eps5")
            for c in range(KC):
                act.wait_ge(cvn_ready, c + 1)
                nc.scalar.activation(HN[:, c, :], CV[:, c, :], ACT.Silu, scale=col("ln_g", c),
                                     bias=col("ln_b", c)).then_inc(h_ready, 1)
            norm("ffn1", T + C, x_from("pw2", 2), mod(0, 6))
            silu_gate("gu1", T + C, True)
            norm("ffn2", T + C, x_from("down1"), mod(1, 0))
            silu_gate("gu2", T + C)
            norm("na", T + C, x_from("down2"), mod(1, 3))

            def exponentials(u):
                act.wait_ge(s_max, u + 1)
                if u >= 2:
                    act.wait_ge(pt_ready, u - 1)
                nc.scalar.activation(NP[:, u % 2, :], bank[u % 4][:, :], ACT.Exp, bias=NM[:, u:u + 1],
                                     accum_out=SUM[:, u:u + 1]).then_inc(p_ready, 1)

            def copy_transposed(u):
                h, t = u // 2, u % 2
                act.wait_ge(pt_ready, u + 1)
                if h >= 2:
                    act.wait_ge(o_ready, h - 1)
                nc.scalar.activation((PTS, PTS2)[h % 2][:, :, t * P:(t + 1) * P],
                                     bank[4 + u % 2][:, :].rearrange("p (k q) -> p k q", k=4),
                                     ACT.Copy).then_inc(pts_ready, 1)

            for u in range(2 * H + 1):
                if u < 2 * H:
                    exponentials(u)
                if u >= 1:
                    copy_transposed(u - 1)
            norm("ffn3", T, x_from("na_o", 2), mod(1, 6))
            silu_gate("gu3", T)
            norm("final", T, x_from("down3"))

            norm("ab", T, lambda c: act.wait_ge(h_ready, KC * norm_no["final"] + c + 1))
            S = STAGES["ab_in"]
            act.wait_ge(drained, S.j + 6)
            nc.scalar.activation(RG[:, :, :], RG[:, :, :], ACT.Silu).then_inc(rg_ready, 1)
            act.wait_ge(drained, S.j + 12)
            nc.scalar.activation(MO[:, :, :], MO[:, :, :], ACT.Sigmoid).then_inc(mo_ready, 1)
            for c in range(4):
                act.wait_ge(mconv_ready, c + 1)
                nc.scalar.activation(MQK[:, c, :], MQK[:, c, :], ACT.Silu).then_inc(mqk_ready, 1)
            act.wait_ge(gate_step, 2)
            link(nc.scalar.activation(LROW[0:4, :], XF[0:4, :], ACT.Abs))
            link(nc.scalar.activation(LROW[0:4, :], LROW[0:4, :], ACT.Exp, scale=-1.0))
            nc.scalar.activation(LROW[0:4, :], LROW[0:4, :], ACT.Ln, bias=con[0:4, CONST["one"][0]:CONST["one"][0] + 1])\
                .then_inc(gate_step, 1)
            act.wait_ge(gate_step, 6)
            for h in range(4):
                nc.scalar.activation(WT[:, h, 0:T], WT[:, h, 0:T], ACT.Exp, bias=ACOL[:, h:h + 1])
                nc.scalar.activation(WT[:, h, T:T + P], WT[:, h, T:T + P], ACT.Exp, bias=ACOL[:, 4 + h:5 + h])
            for b in range(2):
                ins = nc.scalar.activation(EMT[:, 2 * b:2 * b + 2, :],
                                           bank[4 + b][:, :].rearrange("p (e t) -> p e t", e=2), ACT.Exp)
            ins.then_inc(gate_step, 1)
            for pr in range(4):
                base = AB_BASE[pr] + pr // 2
                act.wait_ge(ab_step, base + 3)
                nc.scalar.activation(SQ[:, 0, :], bank[6][:, :], ACT.Square).then_inc(ab_step, 1)
                act.wait_ge(ab_step, base + 5)
                nc.scalar.activation(STD[:, :], bank[0][:, :], ACT.Sqrt, bias=const("eps6")).then_inc(ab_step, 1)
            conv_ffn(0, "ab_out")
            per_layer(0)
            norm("nsa", T, x_from("ple_g0", 2))
            for n in range(5):
                act.wait_ge(drained, STAGES["nsa_in"].j + (n + 1 if n < 4 else 7))
                if n >= 2:
                    act.wait_ge(qmean_ready, n - 1)
                nc.scalar.activation(SQ[:, n % 2, :], QK[:, 2 * n:2 * n + 2, :].rearrange("p c t -> p (c t)"),
                                     ACT.Square).then_inc(qsq_ready, 1)
                act.wait_ge(qmean_ready, n + 1)
                if n >= 1:
                    act.wait_ge(qn_ready, n)
                nc.scalar.activation(STD[:, :], bank[1][:, :], ACT.Sqrt, bias=const("eps6"))\
                    .then_inc(qstd_ready, 1)
            act.wait_ge(nsa_step, 2)
            nc.scalar.activation(GATE[:, :], GATE[:, :], ACT.Sigmoid).then_inc(ngate_ready, 1)
            act.wait_ge(drained, STAGES["nsa_out"].j)
            nc.scalar.activation(HC[:, :, :, :].rearrange("p a f n -> p (a f n)"),
                                 HC[:, :, :, :].rearrange("p a f n -> p (a f n)"), ACT.Gelu_apprx_tanh)\
                .then_inc(nsa_step, 1)
            act.wait_ge(nsa_step, 4)
            nc.scalar.activation(SQ[:, 0, 0:15], bank[1][:, 0:15], ACT.Square).then_inc(nsa_step, 1)
            act.wait_ge(nsa_step, 6)
            nc.scalar.activation(STD[:, 0:15], bank[2][:, 0:15], ACT.Sqrt, bias=const("eps6"))\
                .then_inc(nsa_step, 1)
            act.wait_ge(nsa_step, 10)
            nc.scalar.activation(PC[:, :, :, 0:15], PC[:, :, :, 0:15], ACT.Exp).then_inc(pc_exp, 1)

            def nsa_exponentials(u):
                n = P * (u % 2 + 1)
                act.wait_ge(ns_max, u + 1)
                if u >= 2:
                    act.wait_ge(npt_ready, u - 1)
                for b in range(2):
                    ins = nc.scalar.activation(NP2[:, u % 2, b * n:(b + 1) * n], bank[u % 3][:, b * n:(b + 1) * n],
                                               ACT.Exp, bias=NM[:, 2 * u + b:2 * u + b + 1],
                                               accum_out=SUM[:, 2 * u + b:2 * u + b + 1])
                ins.then_inc(np_ready, 1)

            def nsa_copy_transposed(u):
                n, t = u // 2, u % 2
                act.wait_ge(npt_ready, u + 1)
                if n >= 2:
                    act.wait_ge(no_ready, n - 1)
                pt = (PTS, PTS2)[n % 2]
                ps = bank[3 + u % 2]
                if t == 0:
                    nc.scalar.activation(pt[:, 0:4:2, 0:P], ps[:, 0:2 * P].rearrange("p (b q) -> p b q", b=2),
                                         ACT.Copy)
                    nc.scalar.activation(PTC[0:15, n % 2, :], ps[0:15, 2 * P:4 * P], ACT.Copy)\
                        .then_inc(npts_ready, 1)
                else:
                    nc.scalar.activation(pt[:, :, P:T], ps[:, :].rearrange("p (b q) -> p b q", b=4), ACT.Copy)\
                        .then_inc(npts_ready, 1)

            for u in range(2 * H + 1):
                if u < 2 * H:
                    nsa_exponentials(u)
                if u >= 1:
                    nsa_copy_transposed(u - 1)
            conv_ffn(1, "nsa_out")
            per_layer(1)

        @block.vector
        def _(dve):
            chain = [0]

            def link(ins):
                chain[0] += 1
                ins.then_inc(v_step, 1)
                dve.wait_ge(v_step, chain[0])

            def gain(name, layer, n, g):
                link(nc.vector.scalar_tensor_tensor(
                    out=A[:, :, :], in0=mod(layer, n), scalar=1.0,
                    in1=col("norm_g", g * KC, KC).unsqueeze(2).to_broadcast([P, KC, 2]),
                    op0=ALU.add, op1=ALU.mult))

            def norm(name, n, gains, done, src=X, dst=HN):
                dve.wait_ge(std_ready, norm_no[name] + 1)
                link(nc.vector.reciprocal(bank[1][:, 0:n], STD[:, 0:n]))
                for c in range(KC):
                    for s in range(n // T):
                        ins = nc.vector.scalar_tensor_tensor(
                            out=dst[:, c, s * T:(s + 1) * T], in0=src[:, c, s * T:(s + 1) * T],
                            scalar=gains(c, s), in1=bank[1][:, s * T:(s + 1) * T],
                            op0=ALU.mult, op1=ALU.mult)
                    ins.then_inc(done, 1)

            def drain_mod(m, w, i=0):
                dve.wait_ge(tile_used, w + 1 + 2 * RING * i)
                nc.vector.tensor_tensor(MODU[:, m + RING * i, :], bank[0][:, 0:4],
                                        MODB[:, m + RING * i, :], ALU.add).then_inc(mod_drained, 1)

            def drain_gate_up(name, n, mods=False):
                S = STAGES[name]
                with dve.Fori(0, 2) as i:
                    for k in range(RING):
                        dve.wait_ge(act_out, S.a + k + 1 + RING * i)
                        nc.vector.tensor_tensor(HID[:, k + RING * i, 0:n], G[:, (S.pair + k) % 3, 0:n],
                                                pair_banks(S.pair + k)[1][:, 0:n], ALU.mult)\
                            .then_inc(drained, 1)
                        if mods:
                            drain_mod(S.m + k, S.w + 2 * k + 1, i)

            def drain_down(name, n, gate):
                S = STAGES[name]
                for f in range(KC):
                    if f < KC - 1:
                        dve.wait_ge(part_done, S.part + f + 1)
                    else:
                        dve.wait_ge(tile_used, S.w + RING)
                    for s in range(n // T):
                        t = slice(s * T, (s + 1) * T)
                        ins = nc.vector.scalar_tensor_tensor(
                            out=X[:, f, t], in0=bank[f][:, t], scalar=gate(f, s),
                            in1=X[:, f, t], op0=ALU.mult, op1=ALU.add)
                    ins.then_inc(drained, 1)

            def half_gate(layer, n):
                link(nc.vector.tensor_scalar(GT[:, :, :], mod(layer, n), 0.5, None, ALU.mult))

            def drain_biased(name, n, layer, bias, mods):
                S = STAGES[name]
                for k in range(4):
                    w = S.w + (2 * k if mods else k)
                    dve.wait_ge(tile_used, w + 1)
                    for f, ps in enumerate(pair_banks(S.pair + k)):
                        c = 2 * k + f
                        for s in range(n // T):
                            t = slice(s * T, (s + 1) * T)
                            ins = nc.vector.tensor_scalar(ps[:, t], ps[:, t], col(bias, c),
                                                          mod(layer, 5)[:, c, s:s + 1], ALU.add, ALU.mult)
                        link(ins)
                        ins = nc.vector.tensor_tensor(X[:, c, 0:n], X[:, c, 0:n], ps[:, 0:n], ALU.add)
                    ins.then_inc(drained, 1)
                    if mods:
                        drain_mod(S.m + k, w + 1)

            def by_mod(c, s):
                return A[:, c, s:s + 1]


            def drain_plain(name):
                S = STAGES[name]
                for k in range(4):
                    dve.wait_ge(tile_used, S.w + k + 1)
                    for f, ps in enumerate(pair_banks(S.pair + k)):
                        c = 2 * k + f
                        ins = nc.vector.tensor_tensor(X[:, c, 0:T], X[:, c, 0:T], ps[:, 0:T], ALU.add)
                    ins.then_inc(drained, 1)

            def conv_ffn(i):
                norm(f"ffn{4 + i}", T, lambda c, s: col("ffn_norm_g", i * KC + c), h_ready)
                S = STAGES[f"gu{4 + i}"]
                with dve.Fori(0, 2) as it:
                    for k in range(RING):
                        a, b = pair_banks(S.pair + k)
                        g = (S.pair + k) % 3
                        n = 2 * RING * i + k + 1
                        f = k + RING * it
                        dve.wait_ge(act_out, S.a + k + 1 + RING * it)
                        nc.vector.scalar_tensor_tensor(
                            out=G[:, g, 1:T], in0=a[:, 0:T - 1], scalar=ffn_conv_w[:, 3 * i + 1, f],
                            in1=G[:, g, 1:T], op0=ALU.mult, op1=ALU.add).then_inc(tap_out, 1)
                        dve.wait_ge(tap_out, n + RING * it)
                        nc.vector.scalar_tensor_tensor(
                            out=G[:, g, 2:T], in0=a[:, 0:T - 2], scalar=ffn_conv_w[:, 3 * i, f],
                            in1=G[:, g, 2:T], op0=ALU.mult, op1=ALU.add).then_inc(conv_out, 1)
                        dve.wait_ge(gelu_out, n + RING * it)
                        nc.vector.tensor_tensor(HID[:, f, 0:T], G[:, g, T:2 * T], b[:, 0:T], ALU.mult)\
                            .then_inc(drained, 1)
                S = STAGES[f"down{4 + i}"]
                for f in range(KC):
                    if f < KC - 1:
                        dve.wait_ge(part_done, S.part + f + 1)
                    else:
                        dve.wait_ge(tile_used, S.w + RING)
                    nc.vector.tensor_tensor(X[:, f, 0:T], X[:, f, 0:T], bank[f][:, 0:T], ALU.add)\
                        .then_inc(drained, 1)

            def per_layer(i):
                S = STAGES[f"ple_e{i}"]
                for j in range(4):
                    if j < 3:
                        dve.wait_ge(part_done, S.part + j + 1)
                    else:
                        dve.wait_ge(tile_used, S.w + 1)
                    for f, ps in enumerate(pair_banks(S.pair + j)):
                        ins = nc.vector.tensor_copy(E[:, 2 * j + f, :], ps[:, 0:T])
                    ins.then_inc(drained, 1)
                norm(f"e{i}", T, lambda c, s: col("ple_norm_g", i * KC + c), h_ready, src=E, dst=E)
                dve.wait_ge(h_ready, KC * (norm_no[f"e{i}"] + 1))
                norm(f"pg{i}", T, lambda c, s: col("ple_gate_norm_g", i * KC + c), h_ready)
                S = STAGES[f"ple_g{i}"]
                for k in range(4):
                    dve.wait_ge(act_out, S.a + k + 1)
                    g = G[:, (S.pair + k) % 3, :].rearrange("p (f t) -> p f t", f=2)
                    link(nc.vector.tensor_tensor(g, g, E[:, 2 * k:2 * k + 2, :], ALU.mult))
                    nc.vector.tensor_tensor(X[:, 2 * k:2 * k + 2, 0:T], X[:, 2 * k:2 * k + 2, 0:T], g, ALU.add)\
                        .then_inc(drained, 1)

            dve.wait_ge(params_in, 16)
            for m in range(8):
                drain_mod(m, m)
            dve.wait_ge(mod_drained, 8)
            gain("ffn0", 0, 1, 0)
            norm("ffn0", T + C, by_mod, scaled)
            drain_gate_up("gu0", T + C, True)
            dve.wait_ge(mod_drained, STAGES["pw1"].m)
            half_gate(0, 2)
            drain_down("down0", T + C, lambda f, s: GT[:, f, s:s + 1])
            nc.vector.memset(U[:, :, :, 0:PAD], 0.0)
            nc.vector.memset(U[:, :, :, PAD + T:UP], 0.0)
            gain("conv", 0, 4, 1)
            norm("conv", T + C, by_mod, scaled)
            S = STAGES["pw1"]
            for k in range(8):
                dve.wait_ge(act_out, S.a + k + 1)
                nc.vector.scalar_tensor_tensor(
                    out=U[:, k, :, PAD:PAD + T],
                    in0=pair_banks(S.pair + k)[0][:, :].rearrange("p (s t) -> p s t", s=2),
                    scalar=col("b_pw1", k), in1=G[:, (S.pair + k) % 3, :].rearrange("p (s t) -> p s t", s=2),
                    op0=ALU.add, op1=ALU.mult).then_inc(drained, 1)
                drain_mod(S.m + k, S.w + 2 * k + 1)
                dve.wait_ge(drained, S.j + k + 1)
                cv = CV[:, k, :].rearrange("p (s t) -> p s t", s=2)
                link(nc.vector.tensor_scalar(cv, U[:, k, :, 0:T], col("w_dw", k), col("b_dw", k),
                                             ALU.mult, ALU.add))
                for tap in range(1, TAPS):
                    ins = nc.vector.scalar_tensor_tensor(
                        out=cv, in0=U[:, k, :, tap:tap + T], scalar=col("w_dw", tap * KC + k), in1=cv,
                        op0=ALU.mult, op1=ALU.add)
                    if tap < TAPS - 1:
                        link(ins)
                ins.then_inc(cv_ready, 1)
            dve.wait_ge(mu_ready, 1)
            for c in range(KC):
                nc.vector.tensor_tensor(CV[:, c, :], CV[:, c, :], bank[1][:, :], ALU.subtract)\
                    .then_inc(cv_centred, 1)
            dve.wait_ge(std_ready, norm_no["ln"] + 1)
            link(nc.vector.reciprocal(bank[1][:, :], STD[:, :]))
            for c in range(KC):
                nc.vector.tensor_tensor(CV[:, c, :], CV[:, c, :], bank[1][:, :], ALU.mult)\
                    .then_inc(cvn_ready, 1)
            drain_biased("pw2", T + C, 0, "b_pw2", True)
            dve.wait_ge(mod_drained, STAGES["gu1"].m)
            gain("ffn1", 0, 7, 2)
            norm("ffn1", T + C, by_mod, scaled)
            drain_gate_up("gu1", T + C, True)
            half_gate(0, 8)
            drain_down("down1", T + C, lambda f, s: GT[:, f, s:s + 1])
            dve.wait_ge(mod_drained, STAGES["gu2"].m)
            gain("ffn2", 1, 1, 3)
            norm("ffn2", T + C, by_mod, scaled)
            drain_gate_up("gu2", T + C)
            half_gate(1, 2)
            drain_down("down2", T + C, lambda f, s: GT[:, f, s:s + 1])
            gain("na", 1, 4, 4)
            norm("na", T + C, by_mod, scaled)
            S = STAGES["na_qk"]
            for k in range(8):
                dve.wait_ge(tile_used, S.w + 2 * k + 1)
                for f, ps in enumerate(pair_banks(S.pair + k)):
                    c = 2 * k + f
                    if k < 4:
                        ins = nc.vector.tensor_scalar(NQ[:, c, :], ps[:, 0:T], col("b_qkv", c), DH ** -0.5,
                                                      ALU.add, ALU.mult)
                    else:
                        ins = nc.vector.tensor_scalar(NK[:, c - KC, :], ps[:, :], col("b_qkv", c), None,
                                                      ALU.add)
                ins.then_inc(drained, 1)
                drain_mod(S.m + k, S.w + 2 * k + 1)
            S = STAGES["na_v"]
            for j in range(8):
                k, half = j // 2, j % 2
                if half == 0:
                    dve.wait_ge(part_done, S.part + k + 1)
                else:
                    dve.wait_ge(tile_used, S.w + k + 1)
                for f, ps in enumerate(pair_banks(S.pair + j)):
                    ins = nc.vector.tensor_copy(NV[:, 2 * half + f, 256 * k:256 * (k + 1)], ps[:, 0:256])
                ins.then_inc(drained, 1)

            def maxima(u):
                h, t = u // 2, u % 2
                dve.wait_ge(s_ready, u + 1)
                dve.wait_ge(bias_ready, h + 1)
                ps = bank[u % 4]
                at = (2 - 2 * t) * GRID
                link(nc.vector.tensor_tensor(ps[:, 0:T], ps[:, 0:T], RBT[:, h % 2, at:at + T], ALU.add))
                nc.vector.tensor_reduce(NM[:, u:u + 1], ps[:, :], AX.X, ALU.max, negate=True)\
                    .then_inc(s_max, 1)

            def diagonal(u):
                dve.wait_ge(p_ready, u + 1)
                link(nc.vector.reciprocal(RSUM[:, u:u + 1], SUM[:, u:u + 1]))
                if u >= 2:
                    dve.wait_ge(pt_ready, u - 1)
                nc.vector.tensor_scalar(DG[:, u % 2, :], const("ident"), RSUM[:, u:u + 1], None, ALU.mult)\
                    .then_inc(dg_ready, 1)

            def copy_output(h):
                r = DH * (h % 2)
                dve.wait_ge(o_ready, h + 1)
                nc.vector.tensor_scalar(HN[r:r + DH, h // 2, 0:T], bank[6 + h % 2][r:r + DH, 0:T],
                                        cols[r:r + DH, COLS["b_qkv"][0] + 2 * KC + h // 2:
                                             COLS["b_qkv"][0] + 2 * KC + h // 2 + 1],
                                        None, ALU.add).then_inc(o_out, 1)

            for u in range(2 * H + 4):
                if u < 2 * H:
                    maxima(u)
                if 1 <= u <= 2 * H:
                    diagonal(u - 1)
                if u >= 4 and u % 2 == 0:
                    copy_output((u - 4) // 2)
            dve.wait_ge(mod_drained, 72)
            drain_biased("na_o", T, 1, "b_o", False)
            gain("ffn3", 1, 7, 5)
            norm("ffn3", T, by_mod, scaled)
            drain_gate_up("gu3", T)
            half_gate(1, 8)
            drain_down("down3", T, lambda f, s: GT[:, f, s:s + 1])
            norm("final", T, lambda c, s: col("final_g", c), h_ready, dst=X)

            norm("ab", T, lambda c, s: col("ab_norm_g", c), h_ready)
            S = STAGES["ab_in"]
            nc.vector.memset(MPAD[:, :, 0:3], 0.0)
            for k in range(12):
                dve.wait_ge(tile_used, S.w + k + 1)
                for f, ps in enumerate(pair_banks(S.pair + k)):
                    if k < 2:
                        ins = nc.vector.tensor_scalar(RQK[:, 2 * k + f, :], ps[:, 0:T],
                                                      1.0 if k == 0 else DH ** -0.5, None, ALU.mult)
                    elif k in (2, 3, 8, 9):
                        v = RV if k < 4 else MV
                        ins = nc.vector.tensor_copy(v[:, f, (k % 2) * 256:(k % 2 + 1) * 256], ps[:, 0:256])
                    elif k in (6, 7):
                        ins = nc.vector.tensor_copy(MPAD[:, 2 * (k - 6) + f, 3:3 + T], ps[:, 0:T])
                    else:
                        dst = RG if k < 6 else MO
                        ins = nc.vector.tensor_copy(dst[:, 2 * (k % 2) + f, :], ps[:, 0:T])
                ins.then_inc(drained, 1)
            dve.wait_ge(gate_step, 1)
            nc.vector.tensor_scalar(IG[0:4, :], bank[0][0:4, 0:T], cols[0:4, gb:gb + 1], None, ALU.add)
            nc.vector.tensor_scalar(XF[0:4, :], bank[1][0:4, 0:T], cols[0:4, gb + 1:gb + 2], None, ALU.add)\
                .then_inc(gate_step, 1)
            dve.wait_ge(drained, S.j + 12)
            for c in range(4):
                link(nc.vector.tensor_scalar(MQK[:, c, :], MPAD[:, c, 0:T], col("ab_conv_w", c),
                                             col("ab_conv_b", c), ALU.mult, ALU.add))
                for tap in range(1, 4):
                    ins = nc.vector.scalar_tensor_tensor(out=MQK[:, c, :], in0=MPAD[:, c, tap:tap + T],
                                                         scalar=col("ab_conv_w", 4 * tap + c), in1=MQK[:, c, :],
                                                         op0=ALU.mult, op1=ALU.add)
                    if tap < 3:
                        link(ins)
                ins.then_inc(mconv_ready, 1)
            for c in range(4):
                dve.wait_ge(rotated, c + 1)
                nc.vector.tensor_tensor(RQK[:, c, :], RQK[:, c, :], const("cos"), ALU.mult)
                link(nc.vector.tensor_tensor(bank[4 + c][:, 0:T], bank[4 + c][:, 0:T], const("sin"), ALU.mult))
                nc.vector.tensor_tensor(RQK[:, c, :], RQK[:, c, :], bank[4 + c][:, 0:T], ALU.add)\
                    .then_inc(rope_done, 1)
            dve.wait_ge(gate_step, 3)
            link(nc.vector.tensor_scalar(XF[0:4, :], XF[0:4, :], 0.0, None, ALU.min))
            link(nc.vector.tensor_tensor(LROW[0:4, :], XF[0:4, :], LROW[0:4, :], ALU.subtract))
            link(nc.vector.tensor_tensor_scan(BROW[0:4, :], ones_row, LROW[0:4, :], 0.0, ALU.mult, ALU.add))
            link(nc.vector.tensor_tensor(AROW[0:4, :], IG[0:4, :], BROW[0:4, :], ALU.subtract))
            link(nc.vector.tensor_tensor_scan(MROW[0:4, :], AROW[0:4, :], AROW[0:4, :], 0.0, ALU.max, ALU.max))
            nc.vector.scalar_tensor_tensor(out=NMT[0:4, :], in0=BROW[0:4, :], scalar=-1.0, in1=MROW[0:4, :],
                                           op0=ALU.mult, op1=ALU.subtract).then_inc(gate_step, 1)
            dve.wait_ge(gate_step, 5)
            nc.vector.tensor_copy(ACOL[:, :], bank[0][:, 0:8])
            for b in range(2):
                ps = bank[2 + b][:, :].rearrange("p (e t) -> p e t", e=2)
                mask = const("causal_t").unsqueeze(1).to_broadcast([P, 2, P])
                w = WT[:, 2 * b:2 * b + 2, :]
                nc.vector.tensor_tensor(w[:, :, 0:P], mask, ps[:, :, 0:P], ALU.subtract)
                nc.vector.tensor_scalar(w[:, :, P:T], ps[:, :, P:T], -1.0, None, ALU.mult)
                ins = nc.vector.tensor_tensor(w[:, :, T:T + P], mask, ps[:, :, P:T], ALU.subtract)
            ins.then_inc(gate_step, 1)
            dve.wait_ge(rg_ready, 1)
            dve.wait_ge(mo_ready, 1)
            for pr in range(4):
                base = AB_BASE[pr]
                mlstm = pr // 2
                dve.wait_ge(ab_step, base + 1)
                for e in range(2):
                    h = 2 * (pr % 2) + e
                    for a, b in ((0, T), (T, T + P)):
                        if mlstm:
                            ins = nc.vector.scalar_tensor_tensor(
                                out=SW[:, e, a:b], in0=bank[2 + e][:, a:b], scalar=DH ** -0.5,
                                in1=WT[:, h, a:b], op0=ALU.mult, op1=ALU.mult)
                        else:
                            ins = nc.vector.tensor_tensor(SW[:, e, a:b], bank[2 + e][:, a:b],
                                                          const("decay", h * T, b - a), ALU.mult)
                ins.then_inc(ab_step, 1)
                if mlstm:
                    dve.wait_ge(ab_step, base + 3)
                    h = 2 * (pr % 2)
                    den = bank[7][:, :].rearrange("p (e t) -> p e t", e=2)
                    link(nc.vector.tensor_tensor(DEN, den, EMT[:, h:h + 2, :], ALU.max))
                    link(nc.vector.scalar_tensor_tensor(out=DEN, in0=den, scalar=-1.0, in1=DEN,
                                                        op0=ALU.mult, op1=ALU.max))
                    link(nc.vector.reciprocal(DEN, DEN))
                    num = bank[6][:, :].rearrange("p (e t) -> p e t", e=2)
                    nc.vector.tensor_tensor(num, num, DEN, ALU.mult).then_inc(ab_step, 1)
                base += mlstm
                dve.wait_ge(ab_step, base + 6)
                link(nc.vector.reciprocal(STD[:, :], STD[:, :]))
                for e in range(2):
                    h = 2 * (pr % 2) + e
                    t = slice(e * T, (e + 1) * T)
                    link(nc.vector.scalar_tensor_tensor(
                        out=HN[:, 2 * pr + e, 0:T], in0=bank[6][:, t],
                        scalar=col("m_g" if mlstm else "ret_g", h), in1=STD[:, t], op0=ALU.mult, op1=ALU.mult))
                    ins = nc.vector.tensor_tensor(HN[:, 2 * pr + e, 0:T], HN[:, 2 * pr + e, 0:T],
                                                  (MO if mlstm else RG)[:, h, :], ALU.mult)
                ins.then_inc(ab_step, 1)
            drain_plain("ab_out")
            conv_ffn(0)
            per_layer(0)
            norm("nsa", T, lambda c, s: col("nsa_norm_g", c), h_ready)
            S = STAGES["nsa_in"]
            for k in range(8):
                dve.wait_ge(tile_used, S.w + k + 1)
                for f, ps in enumerate(pair_banks(S.pair + k)):
                    if k in (4, 5):
                        pos = col("pos_k" if k == 4 else "pos_v", 0, 16)
                        for lp in range(2):
                            r = slice(DH * lp, DH * lp + DH)
                            rows = ps[r, lp:lp + 255]
                            rows = bass.AP(rows.tensor, rows.offset, [rows.ap[0], [2, 16], [16, NC_CMP]])
                            ins = nc.vector.tensor_tensor(
                                BLK[r, k - 4, :, f * 15:(f + 1) * 15], rows,
                                pos[r, :].unsqueeze(2).to_broadcast([DH, 16, NC_CMP]), ALU.add)
                    elif k == 7:
                        ins = nc.vector.tensor_copy(SV[:, f, :], ps[:, 0:256])
                    else:
                        ins = nc.vector.tensor_copy(QK[:, 2 * min(k, 4) + f, :], ps[:, 0:T])
                ins.then_inc(drained, 1)
                if k == 3:
                    link(nc.vector.tensor_scalar(QG[:, :], col("q_g"), DH ** -0.5, None, ALU.mult))
            dve.wait_ge(nsa_step, 1)
            nc.vector.tensor_tensor(GATE[:, :].rearrange("p (s n) -> p s n", s=2),
                                    bank[0][:, 0:96].rearrange("p (s n) -> p s n", s=2),
                                    col("gate_b", 0, 48).unsqueeze(1).to_broadcast([P, 2, 48]), ALU.add)\
                .then_inc(nsa_step, 1)
            for n in range(5):
                dve.wait_ge(qstd_ready, n + 1)
                link(nc.vector.reciprocal(STD[:, :], STD[:, :]))
                for f in range(2):
                    c = 2 * n + f
                    g = QG[:, :] if c < 8 else col("k_g", c - 7)
                    ins = nc.vector.scalar_tensor_tensor(out=QK[:, c, :], in0=QK[:, c, :], scalar=g,
                                                         in1=STD[:, f * T:(f + 1) * T],
                                                         op0=ALU.mult, op1=ALU.mult)
                ins.then_inc(qn_ready, 1)
            S = STAGES["nsa_mlp"]
            for m in range(2):
                dve.wait_ge(tile_used, S.w + 2 * m + 2)
                for f, ps in enumerate(pair_banks(S.pair + m)):
                    ins = nc.vector.tensor_copy(HC[:, m, f, :], ps[:, 0:30])
                ins.then_inc(drained, 1)
            dve.wait_ge(nsa_step, 7)
            nc.vector.tensor_copy(VCS[0:15, :], bank[0][0:15, 0:P])
            link(nc.vector.reciprocal(STD[:, 0:15], STD[:, 0:15]))
            nc.vector.scalar_tensor_tensor(out=KCN[:, :], in0=bank[1][:, 0:15], scalar=col("k_g", 0),
                                           in1=STD[:, 0:15], op0=ALU.mult, op1=ALU.mult)\
                .then_inc(nsa_step, 1)
            dve.wait_ge(nsa_step, 9)
            for t in range(2):
                pc = PC[:, t, :, 0:15]
                for g in range(2):
                    ps = bank[2 + 2 * t + g][:, 0:128].rearrange("p (h n) -> p h n", h=8)[:, :, 0:15]
                    ins = nc.vector.tensor_tensor(pc[:, 8 * g:8 * g + 8, :], ps,
                                                  cmp_add[:, t:t + 1, 0:15].to_broadcast([P, 8, 15]), ALU.add)
                link(ins)
                link(nc.vector.tensor_reduce(CM[:, t, :], pc, AX.X, ALU.max))
                ins = nc.vector.tensor_tensor(pc, pc, CM[:, t, :].unsqueeze(2).to_broadcast([P, H, 15]),
                                              ALU.subtract)
            ins.then_inc(nsa_step, 1)
            dve.wait_ge(pc_exp, 1)
            dve.wait_ge(ngate_ready, 1)
            gates = GATE[:, :].rearrange("p (s h b) -> p s h b", s=2, b=3)
            for t in range(2):
                pc = PC[:, t, :, 0:15]
                link(nc.vector.tensor_reduce(CM[:, t, :], pc, AX.X, ALU.add))
                link(nc.vector.reciprocal(CM[:, t, :], CM[:, t, :]))
                link(nc.vector.tensor_tensor(CM[:, t, :], CM[:, t, :], gates[:, t, :, 0], ALU.mult))
                link(nc.vector.tensor_tensor(pc, pc, cmp_valid[:, t:t + 1, 0:15].to_broadcast([P, H, 15]),
                                             ALU.mult))
                ins = nc.vector.tensor_tensor(pc, pc, CM[:, t, :].unsqueeze(2).to_broadcast([P, H, 15]), ALU.mult)
            ins.then_inc(nsa_step, 1)

            def nsa_maxima(u):
                t = u % 2
                dve.wait_ge(ns_ready, u + 1)
                ps = bank[u % 3][:, 0:2 * P * (t + 1)].rearrange("p (b k) -> p b k", b=2)
                link(nc.vector.tensor_tensor(ps[:, :, t * P:(t + 1) * P], ps[:, :, t * P:(t + 1) * P],
                                             const("causal").unsqueeze(1).to_broadcast([P, 2, P]), ALU.add))
                nc.vector.tensor_reduce(NM[:, 2 * u:2 * u + 2], ps, AX.X, ALU.max, negate=True)\
                    .then_inc(ns_max, 1)

            def nsa_diagonals(u):
                h, t = u // 4 + 8 * (u // 2 % 2), u % 2
                dve.wait_ge(np_ready, u + 1)
                link(nc.vector.reciprocal(RSUM[:, 2 * u:2 * u + 2], SUM[:, 2 * u:2 * u + 2]))
                link(nc.vector.tensor_tensor(RSUM[:, 2 * u:2 * u + 2], RSUM[:, 2 * u:2 * u + 2],
                                             gates[:, t, h, 1:3], ALU.mult))
                if u >= 2:
                    dve.wait_ge(npt_ready, u - 1)
                for b in range(2):
                    ins = nc.vector.tensor_scalar(DG2[:, u % 2, b, :], const("ident"),
                                                  RSUM[:, 2 * u + b:2 * u + b + 1], None, ALU.mult)
                ins.then_inc(ndg_ready, 1)

            def nsa_copy_output(n):
                r = DH * (n % 2)
                dve.wait_ge(no_ready, n + 1)
                nc.vector.tensor_copy(HN[r:r + DH, n // 2, 0:T], bank[6 + n % 2][r:r + DH, 0:T])\
                    .then_inc(no_out, 1)

            for u in range(2 * H + 4):
                if u < 2 * H:
                    nsa_maxima(u)
                if 1 <= u <= 2 * H:
                    nsa_diagonals(u - 1)
                if u >= 4 and u % 2 == 0:
                    nsa_copy_output((u - 4) // 2)
            drain_plain("nsa_out")
            conv_ffn(1)
            per_layer(1)

        @block.gpsimd
        def _(pool):
            pool.wait_ge(consts_in, 16)

            def load_bias(h):
                if h >= 2:
                    pool.wait_ge(s_max, 2 * h - 2)
                pool.dma_start(RB_T[:, h % 2, :], rpb[h, :, :]).then_inc(bias_in[h % 2], 16)

            load_bias(0)
            for h in range(H):
                if h + 1 < H:
                    load_bias(h + 1)
                pool.wait_ge(bias_in[h % 2], 16 * (h // 2 + 1))
                nc.gpsimd.tensor_tensor(RBT[:, h % 2, :].rearrange("p (u k) -> p u k", u=6),
                                        RB_T[:, h % 2, :].rearrange("p (u k) -> p u k", u=6),
                                        const("window").unsqueeze(1).to_broadcast([P, 6, GRID]),
                                        ALU.add).then_inc(bias_ready, 1)

            pool.wait_ge(h_ready, KC * (norm_no["final"] + 1))
            pool.dma_start(PIN, p_in).then_inc(p_loaded, 16)




def pair_tiles(*parts):
    if len(parts) == 1:
        W = parts[0].reshape(KC, P, -1, 256)
        return W.transpose(2, 1, 0, 3).reshape(-1, P, TILE)
    W = np.stack([p.reshape(KC, P, -1, P) for p in parts], axis=3)
    return W.transpose(2, 1, 0, 3, 4).reshape(-1, P, TILE)


def down_tiles(W):
    return W.reshape(-1, 2, P, 1024).transpose(0, 2, 1, 3).reshape(-1, P, TILE)


def with_mods(tiles, mods):
    return np.stack([tiles, mods], axis=1).reshape(-1, P, TILE)


def columns(v):
    return v.reshape(-1, P).T


def weight_stream(a):
    mods = np.concatenate([pair_tiles(a["mod_w"][i]) for i in range(2)])
    used = [0]

    def take(n):
        used[0] += n
        return mods[used[0] - n:used[0]]

    def ffn(i, j, mods):
        gu = pair_tiles(a["ffn_w_gate"][i, j], a["ffn_w_up"][i, j])
        return [with_mods(gu, take(22)) if mods else gu, down_tiles(a["ffn_w_down"][i, j])]

    def cffn(i):
        up = a["ffn_w_up_2"][i]
        return [pair_tiles(up[:, :F], up[:, F:]), down_tiles(a["ffn_w_down_2"][i])]

    def ple(i):
        return [a["ple_w_2"][i].reshape(2, P, D).transpose(1, 0, 2).reshape(1, P, TILE),
                pair_tiles(a["ple_w_gate_2"][i])]

    pw1 = a["conv_w_pw1"][0]
    qkv = a["na_w_qkv"][0]
    parts = [take(8)]
    parts += ffn(0, 0, True)
    parts += [with_mods(pair_tiles(pw1[:, :D], pw1[:, D:]), take(8)),
              with_mods(pair_tiles(a["conv_w_pw2"][0]), take(4))]
    parts += ffn(0, 1, True)
    parts += ffn(1, 0, False)
    parts += [with_mods(pair_tiles(qkv[:, :2 * D]), take(8)), pair_tiles(qkv[:, 2 * D:]),
              pair_tiles(a["na_w_o"][0])]
    parts += ffn(1, 1, False)
    parts += [pair_tiles(a["ab_w_in_2"][0][:, :3072]), pair_tiles(a["ab_w_out_2"][0])]
    parts += cffn(0) + ple(0)
    w = a["nsa_w_in_2"][0]
    q = w[:, :1024].reshape(D, 2, 8, DH).transpose(0, 2, 1, 3).reshape(D, 1024)
    kc, vc, ks, vs, kw, vw = (w[:, 1024 + 128 * n:1152 + 128 * n] for n in range(6))

    def twice(m):
        return np.repeat(m.reshape(D, 2, 1, DH), 2, axis=2).reshape(D, 256)

    parts += [pair_tiles(m) for m in (q, twice(kc), twice(vc), np.concatenate([ks, kw], axis=1),
                                      np.concatenate([vs, vw], axis=1))]
    for w1 in ("nsa_cmp_w1k_2", "nsa_cmp_w1v_2"):
        parts.append(a[w1][0].reshape(2, 8, P, 256).transpose(0, 2, 1, 3).reshape(2, P, TILE))
    wo = a["nsa_w_out_2"][0].reshape(2, 8, DH, D).transpose(1, 0, 2, 3).reshape(D, D)
    parts += [pair_tiles(wo)]
    parts += cffn(1) + ple(1)
    return np.concatenate(parts)


def parameters(a):
    two = lambda v: np.concatenate([v, v])
    mod_b = np.repeat(columns(a["mod_b"])[:, :, None], 2, axis=2).reshape(P, 288)
    rows4 = np.zeros((P, 2), np.float32)
    rows4[0:4, 0], rows4[0:4, 1] = a["ab_ig_b_2"][0], a["ab_fg_b_2"][0]
    cmp_pos = lambda v: v[0].reshape(16, P).T
    chunked = lambda w: w.reshape(-1, P, w.shape[-1]).transpose(1, 0, 2).reshape(P, -1)
    by_name = {
        "cond": np.stack([columns(a["c"][0]), columns(a["c_ctx"])], axis=2).reshape(P, 2 * KC),
        "mod_b": mod_b, "norm_g": columns(a["norm_g"]), "b_pw1": columns(a["conv_b_pw1"]),
        "w_dw": columns(a["conv_w_dw"]), "b_dw": columns(a["conv_b_dw"]), "ln_g": columns(a["conv_ln_g"]),
        "ln_b": columns(a["conv_ln_b"]), "b_pw2": columns(a["conv_b_pw2"]), "b_qkv": columns(a["na_b_qkv"]),
        "b_o": columns(a["na_b_o"]), "final_g": columns(a["final_g"]), "ab_norm_g": columns(a["ab_norm_g_2"]),
        "ab_conv_w": columns(a["ab_conv_w_2"]), "ab_conv_b": columns(a["ab_conv_b_2"]),
        "ret_g": columns(a["ab_ret_norm_g_2"]), "m_g": columns(a["ab_m_norm_g_2"]), "gate_bias": rows4,
        "ab_wgate": chunked(a["ab_w_in_2"][0][:, 3072:]), "nsa_norm_g": columns(a["nsa_norm_g_2"]),
        "q_g": two(a["nsa_q_norm_g_2"][0])[:, None],
        "k_g": np.concatenate([a["nsa_k_norm_g_2"][0]] * 2, axis=1).T,
        "pos_k": cmp_pos(a["nsa_cmp_pos_k_2"]), "pos_v": cmp_pos(a["nsa_cmp_pos_v_2"]),
        "gate_b": np.repeat(a["nsa_gate_b_2"], P, axis=0),
        "nsa_wgate": chunked(a["nsa_w_in_2"][0][:, 1792:]),
        "w2k": chunked(a["nsa_cmp_w2k_2"][0]), "w2v": chunked(a["nsa_cmp_w2v_2"][0]),
        "ffn_norm_g": columns(a["ffn_norm_g_2"]), "ffn_conv_w": columns(a["ffn_conv_w_2"]),
        "ffn_conv_b": columns(a["ffn_conv_b_2"]), "ple_norm_g": columns(a["ple_norm_g_2"]),
        "ple_gate_norm_g": columns(a["ple_gate_norm_g_2"]),
    }
    for name, v in by_name.items():
        assert v.shape == (P, COLS[name][1]), (name, v.shape)
    return np.concatenate([by_name[name] for name in COLS], axis=1)


def constants():
    p = np.arange(P)
    t = np.arange(T)
    block64 = (p[:, None] // 64 == p[None, :] // 64) / 64
    rot = np.zeros((P, P))
    for m in range(P):
        rot[m + 32 if m % 64 < 32 else m - 32, m] = -1.0 if m % 64 < 32 else 1.0
    inv = (np.float32(10000.0) ** (-np.arange(32, dtype=np.float32) / np.float32(32))).astype(np.float32)
    ang = (t.astype(np.float32)[None, :] * inv[p % 32][:, None]).astype(np.float32)
    log_g = np.log1p(-np.exp2(-5.0 - np.arange(4)))
    diff = t[None, :] - p[:, None]
    decay = [np.where(diff >= 0, np.exp(np.maximum(diff, 0) * g), 0.0) for g in log_g]
    c, kc = p[:, None] % GRID, np.arange(GRID)[None, :]
    start = np.clip(c - 8, 0, GRID - 16)
    q = p[:, None, None] + P * np.arange(2)[None, :, None]
    n = np.arange(16)[None, None, :]
    cmp_valid = (16 * n + 31 <= q) & (n < NC_CMP)
    sel = np.zeros((P, 4, P))
    for h in range(4):
        sel[h, h, :] = 1.0
    by_name = {
        "ident": np.eye(P), "mean_all": np.full((P, P), 1 / D), "ones": np.ones((P, P)),
        "mean64": block64, "mean128": np.full((P, P), 1 / P), "rot": rot,
        "cos": np.cos(ang.astype(np.float64)), "sin": np.sin(ang.astype(np.float64)),
        "causal": np.where(p[None, :] <= p[:, None], 0.0, MASKED),
        "causal_t": np.where(p[:, None] <= p[None, :], 0.0, MASKED),
        "decay": np.concatenate(decay, axis=1),
        "window": np.where((kc >= start) & (kc < start + 16), 0.0, MASKED),
        "cmp_add": np.where(cmp_valid, 0.0, MASKED).reshape(P, 32),
        "cmp_valid": cmp_valid.reshape(P, 32), "sel": sel.reshape(P, 4 * P),
        "eps6": np.full((P, 1), 1e-6), "eps5": np.full((P, 1), 1e-5), "one": np.ones((P, 1)),
    }
    return np.concatenate([by_name[name] for name in CONST], axis=1).astype(np.float32)


def relative_bias(rpb):
    c, kc = np.arange(GRID)[:, None], np.arange(GRID)[None, :]
    col = np.clip(kc - c, -(CB // 2), CB // 2) + CB // 2
    rows = [rpb[:, 5 - r:11 - r][:, :, col].transpose(0, 2, 1, 3) for r in range(2)]
    return np.concatenate(rows, axis=1).reshape(H, P, 6 * GRID)


def kernel(**a):
    import concourse.bacc as bacc
    from concourse.bass_utils import run_bass_kernel_spmd

    a = {n: np.asarray(v) for n, v in a.items()}
    tokens = np.concatenate([a["x"][0], a["ctx"][0]])
    arrays = {
        "x_in": tokens.reshape(T + C, KC, P).transpose(2, 1, 0),
        "params": parameters(a),
        "consts": constants(),
        "weights": weight_stream(a),
        "rpb": relative_bias(a["na_rpb"][0]),
        "p_in": a["p_2"][:, 0].reshape(2, T, 2, P).transpose(3, 0, 2, 1),
    }
    arrays = {n: np.ascontiguousarray(v) for n, v in arrays.items()}
    nc = bacc.Bacc("TRN2", target_bir_lowering=False, num_devices=1)
    args = [nc.dram_tensor(n, v.shape, F32, kind="ExternalInput").ap() for n, v in arrays.items()]
    out = nc.dram_tensor("out", (P, KC, T), F32, kind="ExternalOutput").ap()
    build(nc, *args, out)
    r = run_bass_kernel_spmd(nc, [arrays], core_ids=[0])
    got = r.results[0]["out"]
    return got.transpose(2, 1, 0).reshape(1, T, D)
```

```python
from contextlib import ExitStack

import numpy as np

import concourse.bass as bass
from concourse import mybir

F32 = mybir.dt.float32
F32R = mybir.dt.float32r
ALU = mybir.AluOpType
ACT = mybir.ActivationFunctionType
AX = mybir.AxisListType

P = 128
D = 1024
KC = D // P
T = 256
C = 256
F = 2816
FC = F // P
RAW = 6
SPLIT = 4
TILE = KC * P
GROUP = 8
GJ = GROUP + 4
BODY = 2 * GJ
LAST = 6
TAPS_PE = 11
TAPS = 31
PAD = TAPS // 2
SEG = T + PAD
UP = 2 * SEG + PAD
H = 16
DH = 64
GRID = 64
CB = 31
MASKED = -1e30
NC_CMP = 15
PLE = 256
assert FC == 2 * GROUP + LAST and BODY % RAW == 0 and BODY % SPLIT == 0
FFN_JOBS = 2 * GJ + LAST + 4


class Stage:
    def __init__(self, w, j, m, part, a, q):
        self.w, self.j, self.m, self.part, self.a, self.q = w, j, m, part, a, q


def plan():
    stages, at = {}, [0] * 6
    ffn = (2 * FFN_JOBS, FFN_JOBS)
    for name, (tiles, jobs), mods, parts, acts, hidden in (
        ("mod", (0, 0), 16, 0, 0, 0), ("ffn0", ffn, 44, 0, FC, FC),
        ("pw1", (16, 8), 8, 0, 8, 0), ("pw2", (8, 4), 0, 0, 0, 0),
        ("ffn1", ffn, 44, 0, FC, FC), ("ffn2", ffn, 32, 0, FC, FC),
        ("na_qk", (16, 8), 0, 0, 0, 0), ("na_v", (8, 4), 0, 0, 0, 0), ("na_o", (8, 4), 0, 0, 0, 0),
        ("ffn3", ffn, 0, 0, FC, FC),
        ("ab_in", (24, 12), 0, 0, 0, 0), ("ab_out", (8, 4), 0, 0, 0, 0),
        ("ffn4", ffn, 0, 0, FC, FC),
        ("ple_e0", (2, 4), 0, 2, 0, 0), ("ple_g0", (8, 4), 0, 0, 4, 0),
        ("nsa_in", (16, 8), 0, 0, 0, 0), ("nsa_mlp", (8, 2), 0, 0, 0, 0), ("nsa_out", (8, 4), 0, 0, 0, 0),
        ("ffn5", ffn, 0, 0, FC, FC),
        ("ple_e1", (2, 4), 0, 2, 0, 0), ("ple_g1", (8, 4), 0, 0, 4, 0),
    ):
        stages[name] = Stage(*at)
        at = [x + y for x, y in zip(at, (tiles, jobs, mods, parts, acts, hidden))]
    assert at[2] == 144
    return stages, at[0], at[1]


STAGES, NTILES, NJOBS = plan()

COLS = {}
_at = 0
for _name, _n in (
    ("mod_b", 288), ("norm_g", 6 * KC), ("b_pw1", 2 * KC), ("w_dw", TAPS * KC),
    ("b_dw", KC), ("ln_g", KC), ("ln_b", KC), ("b_pw2", KC), ("b_qkv", 3 * KC), ("b_o", KC),
    ("final_g", KC), ("ab_norm_g", KC), ("ab_conv_w", 4 * 4), ("ab_conv_b", 4), ("ret_g", 4),
    ("m_g", 4), ("gate_bias", 2), ("ab_wgate", 8 * KC), ("nsa_norm_g", KC), ("q_g", 1), ("k_g", 3),
    ("pos_k", 16), ("pos_v", 16), ("gate_b", 48), ("nsa_wgate", 48 * KC), ("w2k", 2 * DH),
    ("w2v", 2 * DH), ("ffn_norm_g", 2 * KC), ("ffn_conv_w", 2 * 3 * FC), ("ffn_conv_b", 2 * FC),
    ("ple_norm_g", 2 * KC), ("ple_gate_norm_g", 2 * KC),
):
    COLS[_name] = (_at, _n)
    _at += _n
NCOLS = _at

CONST = {}
_at = 0
for _name, _n in (
    ("ident", P), ("mean_all", P), ("ones", P), ("mean64", P), ("mean128", P), ("rot", P),
    ("cos", T), ("sin", T), ("causal", P), ("causal_t", P), ("decay", 4 * T), ("window", GRID),
    ("cmp_add", 2 * 16), ("cmp_valid", 2 * 16), ("sel", 4 * P), ("eps6", 1), ("eps5", 1), ("one", 1),
):
    CONST[_name] = (_at, _n)
    _at += _n
NCONST = _at


def build(nc, x_in, params, consts, cond, weights, mod_w, rpb, p_in, out):
    ctx = ExitStack()
    with ctx:
        def sb(name, shape, dt=F32):
            return ctx.enter_context(nc.sbuf_tensor(name, shape, dt))

        def sem(name):
            return ctx.enter_context(nc.semaphore(name))

        raw = [sb(f"raw{n}", [P, TILE]) for n in range(RAW)]
        wh = [sb(f"wh{n}", [P, TILE], F32R) for n in range(SPLIT)]
        wl = [sb(f"wl{n}", [P, TILE], F32R) for n in range(SPLIT)]
        X = sb("X", [P, KC, T + C])
        HNH = sb("HNH", [P, KC, T + C], F32R)
        HNL = sb("HNL", [P, KC, T + C], F32R)
        with nc.sbuf_tensor("arena", [P, KC * UP + KC * (T + C)], F32) as hid:
            pass
        with nc.sbuf_tensor("HDH", [P, GROUP, T + C], F32R) as HDH:
            with nc.sbuf_tensor("HDL", [P, GROUP, T + C], F32R) as HDL:
                pass
        arena_end = sb("arena_all", [P, KC * UP + KC * (T + C)])
        with nc.sbuf_tensor("arena2", [P, 5 * TILE], F32) as hid2:
            pass
        mod_ring = sb("mod_ring", [P, 2, TILE])
        CB = sb("CB", [P, 2, TILE])
        junk = sb("junk", [P, TILE])
        H32 = hid[:, 0:KC * (T + C)].rearrange("p (c t) -> p c t", c=KC)
        G = sb("G", [P, 3, T + C])
        SQ = sb("SQ", [P, 2, T + C])
        STD = sb("STD", [P, T + C])
        cols = sb("cols", [P, NCOLS])
        con = sb("con", [P, NCONST])
        PBUF = [sb(f"embedding{n}", [P, 512], F32R) for n in range(2)]
        with nc.sbuf_tensor("blocks0", [P, 960], F32R) as b0:
            with nc.sbuf_tensor("blocks1", [P, 960], F32R) as b1:
                BBUF = [b0, b1]
        RB_T = sb("bias_rows", [P, 2, 6 * GRID])
        RBT = sb("bias_masked", [P, 2, 6 * GRID])
        bias_rest = sb("bias_rest", [P, 2 * 960 - 4 * 6 * GRID])
        MOD = sb("MOD", [P, 144, 2])
        MA = sb("MA", [P, 2, 2])
        A = sb("A", [P, KC, 2])
        GT = sb("GT", [P, KC, 2])
        bank = [ctx.enter_context(nc.psum_tensor(f"bank{b}", [P, 512], F32)) for b in range(8)]

        def col(name, a=0, n=1):
            return cols[:, COLS[name][0] + a:COLS[name][0] + a + n]

        def const(name, a=0, n=None):
            at, size = CONST[name]
            return con[:, at + a:at + a + (size - a if n is None else n)]

        def mod(layer, n):
            a = layer * 72 + n * KC
            return MOD[:, a:a + KC, :]

        nU = KC * UP
        U = hid[:, 0:nU].rearrange("p (c t) -> p c t", c=KC)
        CV = hid[:, nU:nU + KC * 512].rearrange("p (c t) -> p c t", c=KC)
        DIAG = sb("DIAG", [P, 4, P])

        def both(k, at):
            ap = U[:, k, at:at + T]
            return bass.AP(ap.tensor, ap.offset, [ap.ap[0], [SEG, 2], [1, T]])

        NQ = hid[:, 0:2048].rearrange("p (c t) -> p c t", c=KC)
        NK = hid[:, 2048:6144].rearrange("p (c t) -> p c t", c=KC)
        NV = [hid[:, 6144:8192].rearrange("p (s d) -> p s d", s=2),
              hid2[:, 0:2048].rearrange("p (s d) -> p s d", s=2)]
        O32 = hid2[:, 2048:4096].rearrange("p (c t) -> p c t", c=KC)
        NP = hid2[:, 4096:5120].rearrange("p (b k) -> p b k", b=2)
        MODB = cols[:, COLS["mod_b"][0]:COLS["mod_b"][0] + 288].rearrange("p (m x) -> p m x", x=2)

        landed = [sem(f"landed{s}") for s in range(RAW)]
        w_hi = sem("w_hi")
        w_lo = sem("w_lo")
        tile_used = sem("tile_used")
        params_in = sem("params_in")
        consts_in = sem("consts_in")
        x_loaded = sem("x_loaded")
        cond_in = sem("cond_in")
        cond_ready = sem("cond_ready")
        part_done = sem("part_done")
        drained = sem("drained")
        act_out = sem("act_out")
        mod_landed = [sem(f"mod_landed{n}") for n in range(2)]
        mod_acc = sem("mod_acc")
        mod_done = sem("mod_done")
        gt_ready = sem("gt_ready")
        hid_ready = sem("hid_ready")
        diag_ready = sem("diag_ready")
        taps_done = sem("taps_done")
        o_split = sem("o_split")
        sq_ready = sem("sq_ready")
        sq_used = sem("sq_used")
        std_ready = sem("std_ready")
        scaled = sem("scaled")
        h_hi = sem("h_hi")
        h_lo = sem("h_lo")
        x_normed = sem("x_normed")
        v_step = sem("v_step")
        a_step = sem("a_step")
        out_sent = sem("out_sent")
        conv_out = sem("conv_out")
        gelu_out = sem("gelu_out")
        cv_ready = sem("cv_ready")
        mu_ready = sem("mu_ready")
        cv_centred = sem("cv_centred")
        cvn_ready = sem("cvn_ready")
        bias_in = [sem(f"bias_in{b}") for b in range(2)]
        bias_ready = sem("bias_ready")
        s_ready = sem("s_ready")
        s_max = sem("s_max")
        p_ready = sem("p_ready")
        dg_ready = sem("dg_ready")
        pt_ready = sem("pt_ready")
        pts_ready = sem("pts_ready")
        o_ready = sem("o_ready")
        o_out = sem("o_out")

        DG = sb("DG", [P, 2, P])
        PTS = G[:, 0:2, :].rearrange("p a b -> p (a b)").rearrange("p (k q) -> p k q", k=4)
        PTS2 = SQ[:, :, :].rearrange("p a b -> p (a b)").rearrange("p (k q) -> p k q", k=4)
        NM = sb("NM", [P, 64])
        SUM = sb("SUM", [P, 64])
        RSUM = sb("RSUM", [P, 64])

        norm_no = {n: i for i, n in enumerate(
            ("ffn0", "conv", "ln", "ffn1", "ffn2", "na", "ffn3", "final",
             "ab", "ffn4", "e0", "pg0", "nsa", "ffn5", "e1", "pg1"))}
        split_no = {n: i for i, n in enumerate(n for n in norm_no if n not in ("final", "e0", "e1"))}
        plain_no = {"final": 0, "e0": 1, "e1": 2}
        scaled_no = {n: i for i, n in enumerate(n for n in split_no if n != "ln")}

        PIN = X[:, 0:4, T:2 * T]
        EMT = hid2[:, 0:1024].rearrange("p (c t) -> p c t", c=4)
        DEN = hid2[:, 1024:1536].rearrange("p (c t) -> p c t", c=2)
        E = hid[:, KC * (T + C):KC * (T + C) + KC * T].rearrange("p (c t) -> p c t", c=KC)
        RQK = hid[:, 0:1024].rearrange("p (c t) -> p c t", c=4)
        MQK = hid[:, 1024:2048].rearrange("p (c t) -> p c t", c=4)
        RG = hid[:, 2048:3072].rearrange("p (c t) -> p c t", c=4)
        MO = hid[:, 3072:4096].rearrange("p (c t) -> p c t", c=4)
        RV = hid[:, 4096:5120].rearrange("p (s d) -> p s d", s=2)
        MV = hid[:, 5120:6144].rearrange("p (s d) -> p s d", s=2)
        MPAD = hid[:, 6144:6144 + 4 * 260].rearrange("p (c t) -> p c t", c=4)
        SW = hid[:, 7200:7200 + 768].rearrange("p (e t) -> p e t", e=2)
        IG, XF, LROW, BROW = (hid2[:, 4096 + T * n:4096 + T * (n + 1)] for n in range(4))
        AROW, MROW = (hid2[:, 1536 + T * n:1536 + T * (n + 1)] for n in range(2))
        NMT = hid[:, 7968:7968 + T]
        ACOL = hid[:, 8224:8232]
        WT = G[:, :, :].rearrange("p a b -> p (a b)").rearrange("p (h t) -> p h t", h=4)
        ones_row = con[0:4, CONST["ones"][0]:CONST["ones"][0] + 1].to_broadcast([4, T])
        sel = const("sel").rearrange("p (h q) -> p h q", h=4)
        ab_wgate = col("ab_wgate", 0, 8 * KC).rearrange("p (k n) -> p k n", k=KC)
        gb = COLS["gate_bias"][0]
        AB_SRC = [(RQK[:, c, :], RQK[:, 2 + c, :], RV) for c in range(2)] + \
                 [(MQK[:, c, :], MQK[:, 2 + c, :], MV) for c in range(2)]
        AB_BASE = [0, 7, 14, 22, 30]
        ffn_conv_w = col("ffn_conv_w", 0, 6 * FC).rearrange("p (j f o) -> p j f o", j=6, o=1)
        ffn_conv_b = col("ffn_conv_b", 0, 2 * FC).rearrange("p (j f o) -> p j f o", j=2, o=1)
        QK = hid[:, 0:2560].rearrange("p (c t) -> p c t", c=10)
        BLK = hid[:, 2560:3520].rearrange("p (m k n) -> p m k n", m=2, k=16)
        SV = hid[:, 3520:4032].rearrange("p (s d) -> p s d", s=2)
        GATE = hid[:, 4032:4128]
        HC = hid[:, 4128:4248].rearrange("p (m f n) -> p m f n", m=2, f=2)
        KCN = hid[:, 4248:4263]
        VCS = hid[:, 4264:4392]
        PC = hid[:, 4392:4904].rearrange("p (t h n) -> p t h n", t=2, h=H)
        CM = hid[:, 4904:4936].rearrange("p (t h) -> p t h", t=2)
        QG = hid[:, 4936:4937]
        PTC = hid[:, 4944:5456].rearrange("p (n q) -> p n q", n=2)
        NP2 = hid[:, 5456:6480].rearrange("p (b k) -> p b k", b=2)
        DG2 = hid[:, 6480:6992].rearrange("p (u b q) -> p u b q", u=2, b=2)
        nsa_wgate = col("nsa_wgate", 0, 48 * KC).rearrange("p (k n) -> p k n", k=KC)
        w2k = col("w2k", 0, 2 * DH).rearrange("p (f n) -> p f n", f=2)
        w2v = col("w2v", 0, 2 * DH).rearrange("p (f n) -> p f n", f=2)
        cmp_add = const("cmp_add").rearrange("p (t n) -> p t n", t=2)
        cmp_valid = const("cmp_valid").rearrange("p (t n) -> p t n", t=2)
        PSPLIT = [PBUF[n][:, :].rearrange("p (k t) -> p k t", k=2) for n in range(2)]
        BSPLIT = [BBUF[n][:, :].rearrange("p (m k n) -> p m k n", m=2, k=16) for n in range(2)]
        p_loaded = sem("p_loaded")
        p_hi = sem("p_hi")
        p_split = sem("p_split")
        blk_hi = sem("blk_hi")
        blk_split = sem("blk_split")
        hid_hi = sem("hid_hi")
        o_hi = sem("o_hi")
        gate_step = sem("gate_step")
        ab_step = sem("ab_step")
        nsa_step = sem("nsa_step")
        rotated = sem("rotated")
        rope_done = sem("rope_done")
        mconv_ready = sem("mconv_ready")
        mqk_ready = sem("mqk_ready")
        rg_ready = sem("rg_ready")
        mo_ready = sem("mo_ready")
        tap_out = sem("tap_out")
        qsq_ready = sem("qsq_ready")
        qmean_ready = sem("qmean_ready")
        qstd_ready = sem("qstd_ready")
        qn_ready = sem("qn_ready")
        ngate_ready = sem("ngate_ready")
        pc_exp = sem("pc_exp")
        ns_ready = sem("ns_ready")
        ns_max = sem("ns_max")
        np_ready = sem("np_ready")
        ndg_ready = sem("ndg_ready")
        npt_ready = sem("npt_ready")
        npts_ready = sem("npts_ready")
        no_ready = sem("no_ready")
        no_out = sem("no_out")

        block = ctx.enter_context(nc.Block())

        @block.sync
        def _(sp):
            sp.dma_start(cols[:, :], params).then_inc(params_in, 16)
            sp.dma_start(con[:, :], consts).then_inc(consts_in, 16)
            sp.dma_start(CB[:, :, :], bass.AP(cond.tensor, cond.offset, [[0, P], [1, 2 * D]])
                         .rearrange("p (s d) -> p s d", s=2)).then_inc(cond_in, 16)

            def load(n, i=0, first=False):
                slot = n % RAW
                if not first:
                    sp.wait_ge(w_lo, n - RAW + 1 + RAW * i)
                sp.dma_start(raw[slot][:, :], weights[n + RAW * i, :, :]).then_inc(landed[slot], 16)

            for n in range(RAW):
                load(n, first=True)
            sp.dma_start(X[:, :, :], x_in).then_inc(x_loaded, 16)
            laps = (NTILES - RAW) // RAW
            with sp.Fori(0, laps) as i:
                for n in range(RAW):
                    load(RAW + n, i)
            for n in range(RAW * (laps + 1), NTILES):
                load(n)

            sp.wait_ge(drained, NJOBS)
            sp.dma_start(out, X[:, :, 0:T]).then_inc(out_sent, 16)
            sp.wait_ge(out_sent, 16)

        def pair_banks(pair):
            return bank[2 + 2 * (pair % 3)], bank[3 + 2 * (pair % 3)]

        @block.tensor
        def _(pe):
            def tiles(w, i=0):
                pe.wait_ge(w_lo, w + 2 + BODY * i)
                return [(wh[t % SPLIT][:, :].rearrange("p (k n) -> p k n", k=KC),
                         wl[t % SPLIT][:, :].rearrange("p (k n) -> p k n", k=KC)) for t in (w, w + 1)]

            def banks_free(j, i=0):
                if j >= 2:
                    pe.wait_ge(drained, j - 1 + GJ * i)

            def job(j, w, n, src=None, ks=KC, norm=None, hidden=None, i=0):
                W = tiles(w, i)
                banks_free(j, i)
                xh, xl = src or (HNH, HNL)
                ps = pair_banks(j)
                for k in range(ks):
                    if norm is not None:
                        pe.wait_ge(h_hi, KC * split_no[norm] + k + 1)
                    if hidden is not None:
                        pe.wait_ge(hid_ready, hidden + k + 1 + GROUP * i)
                    for f in range(2):
                        for part in range(2):
                            nc.tensor.matmul(ps[f][:, 0:n], W[f][part][:, k, :], xh[:, k, 0:n],
                                             start=(k == 0 and part == 0), stop=False)
                for k in range(ks):
                    if norm is not None:
                        pe.wait_ge(h_lo, KC * split_no[norm] + k + 1)
                    for f in range(2):
                        mm = nc.tensor.matmul(ps[f][:, 0:n], W[f][0][:, k, :], xl[:, k, 0:n],
                                              start=False, stop=(k == ks - 1))
                        if k == ks - 1:
                            mm.then_inc(tile_used, 1)

            def token_job(j, w, n):
                W = tiles(w)
                banks_free(j)
                for f, ps in enumerate(pair_banks(j)):
                    for s in range(n):
                        t = slice(s * P, (s + 1) * P)
                        for k in range(KC):
                            for a, b in ((HNH, 0), (HNH, 1), (HNL, 0)):
                                mm = nc.tensor.matmul(ps[:, t], a[:, k, t], W[f][b][:, k, :],
                                                      start=(k == 0 and (a, b) == (HNH, 0)),
                                                      stop=(k == KC - 1 and a is HNL))
                    mm.then_inc(tile_used, 1)

            def ffn(name, n):
                S = STAGES[name]
                with pe.Fori(0, 2) as i:
                    for k in range(GROUP):
                        job(S.j + k, S.w + 2 * k, n, norm=name, i=i)
                    for k in range(4):
                        job(S.j + GROUP + k, S.w + 2 * (GROUP + k), n, (HDH, HDL), hidden=S.q, i=i)
                j, w = S.j + 2 * GJ, S.w + 2 * BODY
                for k in range(LAST):
                    job(j + k, w + 2 * k, n)
                for k in range(4):
                    job(j + LAST + k, w + 2 * (LAST + k), n, (HDH, HDL), ks=LAST, hidden=S.q + 2 * GROUP)

            def stats(name, n):
                for c in range(KC):
                    pe.wait_ge(sq_ready, KC * norm_no[name] + c + 1)
                    nc.tensor.matmul(bank[0][:, 0:n], const("mean_all"), SQ[:, c % 2, 0:n],
                                     start=(c == 0), stop=(c == KC - 1)).then_inc(sq_used, 1)

            def per_layer(i):
                S = STAGES[f"ple_e{i}"]
                W = tiles(S.w)
                pe.wait_ge(p_split, i + 1)
                for j in range(4):
                    banks_free(S.j + j)
                    for f, ps in enumerate(pair_banks(S.j + j)):
                        for k in range(2):
                            at = 2 * (j % 2) + f
                            wk = [W[j // 2][b][:, :, :].rearrange("p (k c) n -> p k c n", k=2)[:, k, at, :]
                                  for b in range(2)]
                            for a, b in ((0, 0), (0, 1), (1, 0)):
                                mm = nc.tensor.matmul(ps[:, 0:T], wk[b], PSPLIT[a][:, k, :],
                                                      start=(k == 0 and (a, b) == (0, 0)),
                                                      stop=(k == 1 and a == 1))
                    mm.then_inc(part_done if j % 2 == 0 else tile_used, 1)
                stats(f"e{i}", T)
                stats(f"pg{i}", T)
                S = STAGES[f"ple_g{i}"]
                for k in range(4):
                    job(S.j + k, S.w + 2 * k, T, norm=f"pg{i}")

            pe.wait_ge(consts_in, 16)
            stats("ffn0", T + C)
            ffn("ffn0", T + C)
            stats("conv", T + C)
            S = STAGES["pw1"]
            for k in range(9):
                if k < 8:
                    job(S.j + k, S.w + 2 * k, T + C, norm="conv")
                if k >= 1:
                    c = k - 1
                    pe.wait_ge(drained, S.j + c + 1)
                    if c >= 2:
                        pe.wait_ge(cv_ready, c - 1)
                    for tap in range(TAPS_PE):
                        d = c * TAPS_PE + tap
                        pe.wait_ge(diag_ready, d + 1)
                        nc.tensor.matmul(bank[c % 2][:, :], DIAG[:, d % 4, :], both(c, TAPS - TAPS_PE + tap),
                                         start=(tap == 0), stop=(tap == TAPS_PE - 1)).then_inc(taps_done, 1)
            pe.wait_ge(cv_ready, KC)
            for c in range(KC):
                pe.wait_ge(cv_ready, c + 1)
                mm = nc.tensor.matmul(bank[1][:, :], const("mean_all"), CV[:, c, :],
                                      start=(c == 0), stop=(c == KC - 1))
            mm.then_inc(mu_ready, 1)
            stats("ln", T + C)
            S = STAGES["pw2"]
            for k in range(4):
                job(S.j + k, S.w + 2 * k, T + C, norm="ln")
            stats("ffn1", T + C)
            ffn("ffn1", T + C)
            stats("ffn2", T + C)
            ffn("ffn2", T + C)
            stats("na", T + C)
            S = STAGES["na_qk"]
            for k in range(8):
                job(S.j + k, S.w + 2 * k, T if k < 4 else T + C, norm="na")
            S = STAGES["na_v"]
            for k in range(4):
                token_job(S.j + k, S.w + 2 * k, 4)
            pe.wait_ge(drained, STAGES["na_o"].j)

            def scores(u):
                h, t = u // 2, u % 2
                r = DH * (h % 2)
                if u >= 4:
                    pe.wait_ge(p_ready, u - 3)
                nc.tensor.matmul(bank[u % 4][:, :], NQ[r:r + DH, h // 2, t * P:(t + 1) * P],
                                 NK[r:r + DH, h // 2, :], start=True, stop=True).then_inc(s_ready, 1)

            def transposed(u):
                pe.wait_ge(dg_ready, u + 1)
                if u >= 2:
                    pe.wait_ge(pts_ready, u - 1)
                for k in range(4):
                    mm = nc.tensor.matmul(bank[4 + u % 2][:, k * P:(k + 1) * P],
                                          NP[:, u % 2, k * P:(k + 1) * P], DG[:, u % 2, :],
                                          start=True, stop=True)
                mm.then_inc(pt_ready, 1)

            def outputs(h):
                r = DH * (h % 2)
                pe.wait_ge(pts_ready, 2 * h + 2)
                if h >= 2:
                    pe.wait_ge(o_out, h - 1)
                pt = (PTS, PTS2)[h % 2]
                for k in range(4):
                    mm = nc.tensor.matmul(bank[6 + h % 2][r:r + DH, 0:T], NV[k // 2][:, k % 2, h * DH:(h + 1) * DH],
                                          pt[:, k, :], start=(k == 0), stop=(k == 3))
                mm.then_inc(o_ready, 1)

            for u in range(2 * H + 3):
                if u < 2 * H:
                    scores(u)
                if 1 <= u <= 2 * H:
                    transposed(u - 1)
                if u >= 3 and u % 2 == 1:
                    outputs((u - 3) // 2)
            S = STAGES["na_o"]
            pe.wait_ge(o_split, KC)
            for k in range(4):
                job(S.j + k, S.w + 2 * k, T)
            stats("ffn3", T)
            ffn("ffn3", T)
            stats("final", T)

            stats("ab", T)
            S = STAGES["ab_in"]
            for k in range(KC):
                pe.wait_ge(scaled, KC * scaled_no["ab"] + k + 1)
                for b in range(2):
                    mm = nc.tensor.matmul(bank[2 + b][0:4, 0:T], ab_wgate[:, k, 4 * b:4 * b + 4],
                                          H32[:, k, 0:T], start=(k == 0), stop=(k == KC - 1))
            mm.then_inc(gate_step, 1)
            pe.wait_ge(gate_step, 2)
            for k in range(12):
                if k in (2, 3, 8, 9):
                    token_job(S.j + k, S.w + 2 * k, 2)
                else:
                    job(S.j + k, S.w + 2 * k, T, norm="ab")
            pe.wait_ge(drained, S.j + 12)
            for c in range(4):
                nc.tensor.matmul(bank[4 + c][:, 0:T], const("rot"), RQK[:, c, :], start=True, stop=True)\
                    .then_inc(rotated, 1)
            pe.wait_ge(gate_step, 4)
            for s in range(2):
                nc.tensor.matmul(bank[0][:, 4 * s:4 * s + 4], AROW[0:4, s * P:(s + 1) * P], con[0:4, 0:4],
                                 start=True, stop=True)
            for h in range(4):
                nc.tensor.matmul(bank[2 + h // 2][:, (h % 2) * T:(h % 2 + 1) * T], sel[0:4, h, :],
                                 MROW[0:4, :], start=True, stop=True)
            pe.wait_ge(rope_done, 4)
            for h in range(4):
                mm = nc.tensor.matmul(bank[4 + h // 2][:, (h % 2) * T:(h % 2 + 1) * T], sel[0:4, h, :],
                                      NMT[0:4, :], start=True, stop=True)
            mm.then_inc(gate_step, 1)
            pe.wait_ge(gate_step, 7)
            for pr in range(4):
                q, k, v = AB_SRC[pr]
                base = AB_BASE[pr]
                if pr:
                    pe.wait_ge(ab_step, base)
                else:
                    pe.wait_ge(mqk_ready, 4)
                for e in range(2):
                    r = slice(DH * e, DH * e + DH)
                    nc.tensor.matmul(bank[2 + e][:, 0:T], k[r, 0:P], q[r, :], start=True, stop=True)
                    mm = nc.tensor.matmul(bank[2 + e][:, T:T + P], k[r, P:T], q[r, P:T],
                                          start=True, stop=True)
                mm.then_inc(ab_step, 1)
                pe.wait_ge(ab_step, base + 2)
                for e in range(2):
                    h = 2 * (pr % 2) + e
                    for ps, w0, w1 in ((bank[6], v[:, 0, h * P:(h + 1) * P], v[:, 1, h * P:(h + 1) * P]),
                                       (bank[7], const("ones"), const("ones")))[:1 + pr // 2]:
                        nc.tensor.matmul(ps[:, e * T:(e + 1) * T], w0, SW[:, e, 0:T], start=True, stop=False)
                        mm = nc.tensor.matmul(ps[:, e * T + P:(e + 1) * T], w1, SW[:, e, T:T + P],
                                              start=False, stop=True)
                mm.then_inc(ab_step, 1)
                pe.wait_ge(ab_step, base + 4 + pr // 2)
                nc.tensor.matmul(bank[0][:, :], const("mean128"), SQ[:, 0, :], start=True, stop=True)\
                    .then_inc(ab_step, 1)
            S = STAGES["ab_out"]
            pe.wait_ge(o_split, 2 * KC)
            for k in range(4):
                job(S.j + k, S.w + 2 * k, T)
            stats("ffn4", T)
            ffn("ffn4", T)
            per_layer(0)
            stats("nsa", T)
            S = STAGES["nsa_in"]
            pe.wait_ge(scaled, KC * (scaled_no["nsa"] + 1))
            for s in range(2):
                for k in range(KC):
                    mm = nc.tensor.matmul(bank[0][:, s * 48:(s + 1) * 48], H32[:, k, s * P:(s + 1) * P],
                                          nsa_wgate[:, k, :], start=(k == 0), stop=(k == KC - 1))
            mm.then_inc(nsa_step, 1)
            for k in range(7):
                job(S.j + k, S.w + 2 * k, T, norm="nsa")
            token_job(S.j + 7, S.w + 14, 2)
            for n in range(5):
                pe.wait_ge(qsq_ready, n + 1)
                if n >= 1:
                    pe.wait_ge(qstd_ready, n)
                nc.tensor.matmul(bank[1][:, :], const("mean64"), SQ[:, n % 2, :], start=True, stop=True)\
                    .then_inc(qmean_ready, 1)
            S = STAGES["nsa_mlp"]
            pe.wait_ge(blk_split, 1)
            pe.wait_ge(drained, S.j)
            for m in range(2):
                banks_free(S.j + m)
                for t in range(2):
                    W = tiles(S.w + 4 * m + 2 * t)
                    for f, ps in enumerate(pair_banks(S.j + m)):
                        for k in range(KC):
                            for a, b in ((0, 0), (0, 1), (1, 0)):
                                mm = nc.tensor.matmul(ps[:, 0:30], W[f][b][:, k, :],
                                                      BSPLIT[a][:, m, 8 * t + k, :],
                                                      start=(t == 0 and k == 0 and (a, b) == (0, 0)),
                                                      stop=(t == 1 and k == KC - 1 and a == 1))
                        mm.then_inc(tile_used, 1)
            pe.wait_ge(nsa_step, 3)
            for g in range(2):
                for f in range(2):
                    nc.tensor.matmul(bank[1][g * DH:(g + 1) * DH, 0:15], w2k[:, f, :],
                                     HC[:, 0, f, g * 15:(g + 1) * 15], start=(f == 0), stop=(f == 1))
            for g in range(2):
                for f in range(2):
                    mm = nc.tensor.matmul(bank[0][0:15, g * DH:(g + 1) * DH], HC[:, 1, f, g * 15:(g + 1) * 15],
                                          w2v[:, f, :], start=(f == 0), stop=(f == 1))
            mm.then_inc(nsa_step, 1)
            pe.wait_ge(nsa_step, 5)
            nc.tensor.matmul(bank[2][:, 0:15], const("mean64"), SQ[:, 0, 0:15], start=True, stop=True)\
                .then_inc(nsa_step, 1)
            pe.wait_ge(nsa_step, 8)
            for t in range(2):
                for h in range(H):
                    r = DH * (h // 8)
                    mm = nc.tensor.matmul(bank[2 + 2 * t + h // 8][:, 16 * (h % 8):16 * (h % 8) + 15],
                                          QK[r:r + DH, h % 8, t * P:(t + 1) * P], KCN[r:r + DH, :],
                                          start=True, stop=True)
            mm.then_inc(nsa_step, 1)

            def nsa_scores(u):
                c, g, t = u // 4, u // 2 % 2, u % 2
                r, n = DH * g, P * (t + 1)
                if u >= 3:
                    pe.wait_ge(np_ready, u - 2)
                for b in range(2):
                    mm = nc.tensor.matmul(bank[u % 3][:, b * n:(b + 1) * n],
                                          QK[r:r + DH, c, t * P:(t + 1) * P], QK[r:r + DH, 8 + b, 0:n],
                                          start=True, stop=True)
                mm.then_inc(ns_ready, 1)

            def nsa_transposed(u):
                h, t = u // 4 + 8 * (u // 2 % 2), u % 2
                pe.wait_ge(ndg_ready, u + 1)
                if u >= 2:
                    pe.wait_ge(npts_ready, u - 1)
                ps = bank[3 + u % 2]
                for b in range(2):
                    for k in range(t + 1):
                        n = b * (t + 1) + k
                        mm = nc.tensor.matmul(ps[:, n * P:(n + 1) * P], NP2[:, u % 2, n * P:(n + 1) * P],
                                              DG2[:, u % 2, b, :], start=True, stop=True)
                if t == 0:
                    for s in range(2):
                        mm = nc.tensor.matmul(ps[0:15, (2 + s) * P:(3 + s) * P], PC[:, s, h, 0:15],
                                              const("ident"), start=True, stop=True)
                mm.then_inc(npt_ready, 1)

            def nsa_outputs(n):
                g = n % 2
                r = DH * g
                pe.wait_ge(npts_ready, 2 * n + 2)
                if n >= 2:
                    pe.wait_ge(no_out, n - 1)
                ps = bank[6 + n % 2]
                pt = (PTS, PTS2)[n % 2]
                nc.tensor.matmul(ps[r:r + DH, 0:T], VCS[0:15, g * DH:(g + 1) * DH], PTC[0:15, n % 2, :],
                                 start=True, stop=False)
                for b in range(2):
                    v = SV[:, :, 2 * b * DH + g * DH:2 * b * DH + (g + 1) * DH]
                    nc.tensor.matmul(ps[r:r + DH, 0:T], v[:, 0, :], pt[:, 2 * b, :], start=False, stop=False)
                    mm = nc.tensor.matmul(ps[r:r + DH, P:T], v[:, 1, :], pt[:, 2 * b + 1, P:T],
                                          start=False, stop=(b == 1))
                mm.then_inc(no_ready, 1)

            pe.wait_ge(nsa_step, 11)
            for u in range(2 * H + 3):
                if u < 2 * H:
                    nsa_scores(u)
                if 1 <= u <= 2 * H:
                    nsa_transposed(u - 1)
                if u >= 3 and u % 2 == 1:
                    nsa_outputs((u - 3) // 2)
            S = STAGES["nsa_out"]
            pe.wait_ge(o_split, 3 * KC)
            for k in range(4):
                job(S.j + k, S.w + 2 * k, T)
            stats("ffn5", T)
            ffn("ffn5", T)
            per_layer(1)

        @block.scalar
        def _(act):
            chain = [0]

            def link(ins):
                chain[0] += 1
                ins.then_inc(a_step, 1)
                act.wait_ge(a_step, chain[0])

            def hi(t, i=0):
                if t < NTILES:
                    act.wait_ge(landed[t % RAW], 16 * (t // RAW + 1) + 16 * (BODY // RAW) * i)
                    nc.scalar.activation(wh[t % SPLIT][:, :], raw[t % RAW][:, :], ACT.Copy).then_inc(w_hi, 1)

            def feed(w, i=0):
                if w > 0:
                    act.wait_ge(tile_used, w + BODY * i)
                hi(w + 2, i)
                hi(w + 3, i)

            def load_mod(m, i=0):
                if m >= 2:
                    act.wait_ge(mod_acc, m - 1 + 2 * GROUP * i)
                act.dma_start(mod_ring[:, m % 2, :], mod_w[m + 2 * GROUP * i, :, :])\
                    .then_inc(mod_landed[m % 2], 16)

            def norm(name, n, ready, shift=None, src=X, eps="eps6"):
                m = norm_no[name]
                for c in range(KC):
                    ready(c)
                    if m > 0 or c >= 2:
                        act.wait_ge(sq_used, KC * m + c - 1)
                    nc.scalar.activation(SQ[:, c % 2, 0:n], src[:, c, 0:n], ACT.Square)\
                        .then_inc(sq_ready, 1)
                act.wait_ge(sq_used, KC * (m + 1))
                nc.scalar.activation(STD[:, 0:n], bank[0][:, 0:n], ACT.Sqrt, bias=const(eps))\
                    .then_inc(std_ready, 1)
                if name in scaled_no:
                    for c in range(KC):
                        act.wait_ge(scaled, KC * scaled_no[name] + c + 1)
                        if shift is None:
                            ins = nc.scalar.activation(HNH[:, c, 0:n], H32[:, c, 0:n], ACT.Copy)
                        else:
                            for s in range(n // T):
                                t = slice(s * T, (s + 1) * T)
                                ins = nc.scalar.activation(HNH[:, c, t], H32[:, c, t], ACT.Identity,
                                                           bias=shift[:, c, s:s + 1])
                        ins.then_inc(h_hi, 1)

            def x_from(name, per=1):
                return lambda c: act.wait_ge(drained, STAGES[name].j + c // per + 1)

            def after(name):
                return lambda c: act.wait_ge(drained, STAGES[name].j + FFN_JOBS - 4 + c // 2 + 1)

            def ffn(name, n, mods=0, causal=None):
                S = STAGES[name]

                def group(j, w, a, q, m, chunks, f0, i=0, last=False):
                    for k in range(chunks):
                        if m is not None:
                            load_mod(m + 2 * k, i)
                            load_mod(m + 2 * k + 1, i)
                        act.wait_ge(tile_used, w + 2 * k + 2 + BODY * i)
                        if q + k >= 2:
                            act.wait_ge(hid_ready, q + k - 1 + GROUP * i)
                        g = (j + k) % 3
                        src = pair_banks(j + k)[0][:, 0:n]
                        if causal is None:
                            nc.scalar.activation(G[:, g, 0:n], src, ACT.Silu).then_inc(act_out, 1)
                        else:
                            f = f0 + k + GROUP * i
                            c = FC * causal + f0 + k + 1
                            nc.scalar.activation(G[:, g, 0:T], src, ACT.Identity,
                                                 scale=ffn_conv_w[:, 3 * causal + 2, f],
                                                 bias=ffn_conv_b[:, causal, f]).then_inc(act_out, 1)
                            act.wait_ge(conv_out, c + GROUP * i)
                            nc.scalar.activation(G[:, g, T:2 * T], G[:, g, 0:T], ACT.Gelu_apprx_tanh)\
                                .then_inc(gelu_out, 1)
                        feed(w + 2 * (k + 1), i)
                    for k in range(1, 4 if last else 5):
                        feed(w + 2 * (chunks + k), i)

                feed(S.w)
                with act.Fori(0, 2) as i:
                    group(S.j, S.w, S.a, S.q, S.m if mods else None, GROUP, 0, i)
                group(S.j + 2 * GJ, S.w + 2 * BODY, S.a + 2 * GROUP, S.q + 2 * GROUP,
                      S.m + 4 * GROUP if mods == 3 else None, LAST, 2 * GROUP, last=True)

            def feeds(name, jobs):
                for k in range(jobs):
                    feed(STAGES[name].w + 2 * k)

            def per_layer(i):
                act.wait_ge(p_loaded, 16)
                pin = PIN[:, 2 * i:2 * i + 2, :]
                nc.scalar.activation(PSPLIT[0], pin, ACT.Copy).then_inc(p_hi, 1)
                feed(STAGES[f"ple_e{i}"].w)
                norm(f"e{i}", T, x_from(f"ple_e{i}", 2), src=E)
                act.wait_ge(x_normed, KC * plain_no[f"e{i}"] + 1)
                norm(f"pg{i}", T, after(f"ffn{4 + i}"))
                S = STAGES[f"ple_g{i}"]
                for k in range(4):
                    feed(S.w + 2 * k)
                    act.wait_ge(tile_used, S.w + 2 * k + 2)
                    act.wait_ge(drained, S.j + k - 1)
                    a, b = pair_banks(S.j + k)
                    g = (S.j + k) % 3
                    nc.scalar.activation(G[:, g, 0:T], a[:, 0:T], ACT.Sigmoid)
                    nc.scalar.activation(G[:, g, T:2 * T], b[:, 0:T], ACT.Sigmoid).then_inc(act_out, 1)

            def split_output(c, ready):
                act.wait_ge(*ready)
                nc.scalar.activation(HNH[:, c, 0:T], O32[:, c, :], ACT.Copy).then_inc(o_hi, 1)

            act.wait_ge(params_in, 16)
            act.wait_ge(cond_in, 16)
            nc.scalar.activation(CB[:, :, :], CB[:, :, :], ACT.Silu).then_inc(cond_ready, 1)
            hi(0)
            hi(1)
            act.wait_ge(consts_in, 16)
            for m in range(8):
                load_mod(m)
            norm("ffn0", T + C, lambda c: (act.wait_ge(x_loaded, 16), load_mod(8 + c)), mod(0, 0))
            ffn("ffn0", T + C, 3)
            norm("conv", T + C, after("ffn0"), mod(0, 3))
            S = STAGES["pw1"]
            for k in range(8):
                feed(S.w + 2 * k)
                load_mod(S.m + k)
                act.wait_ge(tile_used, S.w + 2 * k + 2)
                act.wait_ge(drained, S.j + k - 1)
                g = (S.j + k) % 3
                nc.scalar.activation(G[:, g, :], pair_banks(S.j + k)[1][:, :], ACT.Sigmoid,
                                     bias=col("b_pw1", KC + k)).then_inc(act_out, 1)
            norm("ln", T + C, lambda c: act.wait_ge(cv_centred, c + 1), src=CV, eps="eps5")
            for c in range(KC):
                act.wait_ge(cvn_ready, c + 1)
                link(nc.scalar.activation(CV[:, c, :], CV[:, c, :], ACT.Silu, scale=col("ln_g", c),
                                          bias=col("ln_b", c)))
                nc.scalar.activation(HNH[:, c, :], CV[:, c, :], ACT.Copy).then_inc(h_hi, 1)
            feeds("pw2", 4)
            norm("ffn1", T + C, x_from("pw2", 2), mod(0, 6))
            ffn("ffn1", T + C, 3)
            norm("ffn2", T + C, after("ffn1"), mod(1, 0))
            ffn("ffn2", T + C, 2)
            norm("na", T + C, after("ffn2"), mod(1, 3))
            feeds("na_qk", 8)
            feeds("na_v", 4)

            def exponentials(u):
                act.wait_ge(s_max, u + 1)
                if u >= 2:
                    act.wait_ge(pt_ready, u - 1)
                nc.scalar.activation(NP[:, u % 2, :], bank[u % 4][:, :], ACT.Exp, bias=NM[:, u:u + 1],
                                     accum_out=SUM[:, u:u + 1]).then_inc(p_ready, 1)

            def copy_transposed(u):
                h, t = u // 2, u % 2
                act.wait_ge(pt_ready, u + 1)
                if h >= 2:
                    act.wait_ge(o_ready, h - 1)
                nc.scalar.activation((PTS, PTS2)[h % 2][:, :, t * P:(t + 1) * P],
                                     bank[4 + u % 2][:, :].rearrange("p (k q) -> p k q", k=4),
                                     ACT.Copy).then_inc(pts_ready, 1)

            for u in range(2 * H + 5):
                if u < 2 * H:
                    exponentials(u)
                if 1 <= u <= 2 * H:
                    copy_transposed(u - 1)
                if u >= 7 and u % 4 == 3:
                    c = (u - 7) // 4
                    split_output(c, (o_out, 2 * c + 2))
            feeds("na_o", 4)
            norm("ffn3", T, x_from("na_o", 2), mod(1, 6))
            ffn("ffn3", T)
            norm("final", T, after("ffn3"))

            norm("ab", T, lambda c: act.wait_ge(x_normed, c + 1))
            S = STAGES["ab_in"]
            for k in range(12):
                feed(S.w + 2 * k)
            act.wait_ge(drained, S.j + 6)
            nc.scalar.activation(RG[:, :, :], RG[:, :, :], ACT.Silu).then_inc(rg_ready, 1)
            act.wait_ge(drained, S.j + 12)
            nc.scalar.activation(MO[:, :, :], MO[:, :, :], ACT.Sigmoid).then_inc(mo_ready, 1)
            for c in range(4):
                act.wait_ge(mconv_ready, c + 1)
                nc.scalar.activation(MQK[:, c, :], MQK[:, c, :], ACT.Silu).then_inc(mqk_ready, 1)
            act.wait_ge(gate_step, 2)
            link(nc.scalar.activation(LROW[0:4, :], XF[0:4, :], ACT.Abs))
            link(nc.scalar.activation(LROW[0:4, :], LROW[0:4, :], ACT.Exp, scale=-1.0))
            nc.scalar.activation(LROW[0:4, :], LROW[0:4, :], ACT.Ln, bias=con[0:4, CONST["one"][0]:CONST["one"][0] + 1])\
                .then_inc(gate_step, 1)
            act.wait_ge(gate_step, 6)
            for h in range(4):
                nc.scalar.activation(WT[:, h, 0:T], WT[:, h, 0:T], ACT.Exp, bias=ACOL[:, h:h + 1])
                nc.scalar.activation(WT[:, h, T:T + P], WT[:, h, T:T + P], ACT.Exp, bias=ACOL[:, 4 + h:5 + h])
            for b in range(2):
                ins = nc.scalar.activation(EMT[:, 2 * b:2 * b + 2, :],
                                           bank[4 + b][:, :].rearrange("p (e t) -> p e t", e=2), ACT.Exp)
            ins.then_inc(gate_step, 1)
            for pr in range(4):
                base = AB_BASE[pr] + pr // 2
                act.wait_ge(ab_step, base + 3)
                nc.scalar.activation(SQ[:, 0, :], bank[6][:, :], ACT.Square).then_inc(ab_step, 1)
                act.wait_ge(ab_step, base + 5)
                nc.scalar.activation(STD[:, :], bank[0][:, :], ACT.Sqrt, bias=const("eps6")).then_inc(ab_step, 1)
                for e in range(2):
                    split_output(2 * pr + e, (ab_step, AB_BASE[pr + 1]))
            feeds("ab_out", 4)
            norm("ffn4", T, x_from("ab_out", 2))
            ffn("ffn4", T, causal=0)
            per_layer(0)
            norm("nsa", T, x_from("ple_g0", 2))
            for k in range(8):
                feed(STAGES["nsa_in"].w + 2 * k)
            act.wait_ge(drained, STAGES["nsa_in"].j + 6)
            nc.scalar.activation(BSPLIT[0], BLK[:, :, :, :], ACT.Copy).then_inc(blk_hi, 1)
            for n in range(5):
                act.wait_ge(drained, STAGES["nsa_in"].j + (n + 1 if n < 4 else 7))
                if n >= 2:
                    act.wait_ge(qmean_ready, n - 1)
                nc.scalar.activation(SQ[:, n % 2, :], QK[:, 2 * n:2 * n + 2, :].rearrange("p c t -> p (c t)"),
                                     ACT.Square).then_inc(qsq_ready, 1)
                act.wait_ge(qmean_ready, n + 1)
                if n >= 1:
                    act.wait_ge(qn_ready, n)
                nc.scalar.activation(STD[:, :], bank[1][:, :], ACT.Sqrt, bias=const("eps6"))\
                    .then_inc(qstd_ready, 1)
            act.wait_ge(nsa_step, 2)
            nc.scalar.activation(GATE[:, :], GATE[:, :], ACT.Sigmoid).then_inc(ngate_ready, 1)
            for k in range(4):
                feed(STAGES["nsa_mlp"].w + 2 * k)
            act.wait_ge(drained, STAGES["nsa_out"].j)
            nc.scalar.activation(HC[:, :, :, :].rearrange("p a f n -> p (a f n)"),
                                 HC[:, :, :, :].rearrange("p a f n -> p (a f n)"), ACT.Gelu_apprx_tanh)\
                .then_inc(nsa_step, 1)
            act.wait_ge(nsa_step, 4)
            nc.scalar.activation(SQ[:, 0, 0:15], bank[1][:, 0:15], ACT.Square).then_inc(nsa_step, 1)
            act.wait_ge(nsa_step, 6)
            nc.scalar.activation(STD[:, 0:15], bank[2][:, 0:15], ACT.Sqrt, bias=const("eps6"))\
                .then_inc(nsa_step, 1)
            act.wait_ge(nsa_step, 10)
            nc.scalar.activation(PC[:, :, :, 0:15], PC[:, :, :, 0:15], ACT.Exp).then_inc(pc_exp, 1)

            def nsa_exponentials(u):
                n = P * (u % 2 + 1)
                act.wait_ge(ns_max, u + 1)
                if u >= 2:
                    act.wait_ge(npt_ready, u - 1)
                for b in range(2):
                    ins = nc.scalar.activation(NP2[:, u % 2, b * n:(b + 1) * n], bank[u % 3][:, b * n:(b + 1) * n],
                                               ACT.Exp, bias=NM[:, 2 * u + b:2 * u + b + 1],
                                               accum_out=SUM[:, 2 * u + b:2 * u + b + 1])
                ins.then_inc(np_ready, 1)

            def nsa_copy_transposed(u):
                n, t = u // 2, u % 2
                act.wait_ge(npt_ready, u + 1)
                if n >= 2:
                    act.wait_ge(no_ready, n - 1)
                pt = (PTS, PTS2)[n % 2]
                ps = bank[3 + u % 2]
                if t == 0:
                    nc.scalar.activation(pt[:, 0:4:2, 0:P], ps[:, 0:2 * P].rearrange("p (b q) -> p b q", b=2),
                                         ACT.Copy)
                    nc.scalar.activation(PTC[0:15, n % 2, :], ps[0:15, 2 * P:4 * P], ACT.Copy)\
                        .then_inc(npts_ready, 1)
                else:
                    nc.scalar.activation(pt[:, :, P:T], ps[:, :].rearrange("p (b q) -> p b q", b=4), ACT.Copy)\
                        .then_inc(npts_ready, 1)

            for u in range(2 * H + 5):
                if u < 2 * H:
                    nsa_exponentials(u)
                if 1 <= u <= 2 * H:
                    nsa_copy_transposed(u - 1)
                if u >= 7 and u % 4 == 3:
                    c = (u - 7) // 4
                    split_output(c, (no_out, 2 * c + 2))
            feeds("nsa_out", 4)
            norm("ffn5", T, x_from("nsa_out", 2))
            ffn("ffn5", T, causal=1)
            per_layer(1)

        @block.vector
        def _(dve):
            chain = [0]

            def link(ins):
                chain[0] += 1
                ins.then_inc(v_step, 1)
                dve.wait_ge(v_step, chain[0])

            def gain(name, layer, n, g):
                link(nc.vector.scalar_tensor_tensor(
                    out=A[:, :, :], in0=mod(layer, n), scalar=1.0,
                    in1=col("norm_g", g * KC, KC).unsqueeze(2).to_broadcast([P, KC, 2]),
                    op0=ALU.add, op1=ALU.mult))

            def lo(t, i=0):
                if t >= NTILES:
                    return
                dve.wait_ge(w_hi, t + 1 + BODY * i)
                nc.vector.tensor_tensor(wl[t % SPLIT][:, :], raw[t % RAW][:, :],
                                        wh[t % SPLIT][:, :].bitcast(F32), ALU.subtract).then_inc(w_lo, 1)

            def feed(w, i=0):
                lo(w + 2, i)
                lo(w + 3, i)

            def feeds(name, jobs):
                for k in range(jobs):
                    feed(STAGES[name].w + 2 * k)

            def norm(name, n, gains, src=X, dst=None, shift=None):
                dve.wait_ge(std_ready, norm_no[name] + 1)
                link(nc.vector.reciprocal(bank[1][:, 0:n], STD[:, 0:n]))
                for c in range(KC):
                    for s in range(n // T):
                        ins = nc.vector.scalar_tensor_tensor(
                            out=(dst or H32)[:, c, s * T:(s + 1) * T], in0=src[:, c, s * T:(s + 1) * T],
                            scalar=gains(c, s), in1=bank[1][:, s * T:(s + 1) * T],
                            op0=ALU.mult, op1=ALU.mult)
                    ins.then_inc(x_normed if dst else scaled, 1)
                if not dst:
                    for c in range(KC):
                        dve.wait_ge(h_hi, KC * split_no[name] + c + 1)
                        if shift is None:
                            ins = nc.vector.tensor_tensor(HNL[:, c, 0:n], H32[:, c, 0:n],
                                                          HNH[:, c, 0:n].bitcast(F32), ALU.subtract)
                        else:
                            for s in range(n // T):
                                t = slice(s * T, (s + 1) * T)
                                ins = nc.vector.scalar_tensor_tensor(
                                    out=HNL[:, c, t], in0=H32[:, c, t], scalar=shift[:, c, s:s + 1],
                                    in1=HNH[:, c, t].bitcast(F32), op0=ALU.add, op1=ALU.subtract)
                        ins.then_inc(h_lo, 1)

            def split_output(c):
                dve.wait_ge(o_hi, c + 1)
                nc.vector.tensor_tensor(HNL[:, c % KC, 0:T], O32[:, c % KC, :],
                                        HNH[:, c % KC, 0:T].bitcast(F32), ALU.subtract).then_inc(o_split, 1)

            def mod_unit(m, i=0):
                per = 2 * GROUP * i
                dve.wait_ge(mod_landed[m % 2], 16 * (m // 2 + 1) + 16 * GROUP * i)
                if m >= 1:
                    dve.wait_ge(mod_done, m + per)
                nc.vector.tensor_tensor_reduce(junk[:, :], mod_ring[:, m % 2, :], CB[:, 0, :], 1.0, 0.0,
                                               ALU.mult, ALU.add, MA[:, m % 2, 0:1])
                nc.vector.tensor_tensor_reduce(mod_ring[:, m % 2, :], mod_ring[:, m % 2, :], CB[:, 1, :],
                                               1.0, 0.0, ALU.mult, ALU.add, MA[:, m % 2, 1:2])\
                    .then_inc(mod_acc, 1)
                dve.wait_ge(mod_acc, m + 1 + per)
                nc.vector.tensor_tensor(MOD[:, m + per, :], MA[:, m % 2, :], MODB[:, m + per, :], ALU.add)\
                    .then_inc(mod_done, 1)

            def ffn(name, n, mods=0, gate=None, causal=None):
                S = STAGES[name]

                def group(j, w, a, q, m, chunks, f0, i=0, first=True):
                    for k in range(chunks):
                        feed(w + 2 * k, i)
                        g = (j + k) % 3
                        A_, B_ = pair_banks(j + k)
                        dve.wait_ge(act_out, a + k + 1 + GROUP * i)
                        gg = G[:, g, 0:n]
                        if causal is not None:
                            c = FC * causal + f0 + k + 1
                            f = f0 + k + GROUP * i
                            nc.vector.scalar_tensor_tensor(
                                out=G[:, g, 1:T], in0=A_[:, 0:T - 1], scalar=ffn_conv_w[:, 3 * causal + 1, f],
                                in1=G[:, g, 1:T], op0=ALU.mult, op1=ALU.add).then_inc(tap_out, 1)
                            dve.wait_ge(tap_out, c + GROUP * i)
                            nc.vector.scalar_tensor_tensor(
                                out=G[:, g, 2:T], in0=A_[:, 0:T - 2], scalar=ffn_conv_w[:, 3 * causal, f],
                                in1=G[:, g, 2:T], op0=ALU.mult, op1=ALU.add).then_inc(conv_out, 1)
                            dve.wait_ge(gelu_out, c + GROUP * i)
                            gg = G[:, g, T:2 * T]
                        nc.vector.tensor_tensor(gg, gg, B_[:, 0:n], ALU.mult).then_inc(drained, 1)
                        if m is not None:
                            mod_unit(m + 2 * k, i)
                            mod_unit(m + 2 * k + 1, i)
                    if gate is not None and first:
                        (layer, nn), before = gate
                        if m is not None:
                            dve.wait_ge(mod_done, m + 2 * chunks + 2 * GROUP * i)
                        nc.vector.tensor_scalar(GT[:, :, :], mod(layer, nn), 0.5, None, ALU.mult)\
                            .then_inc(gt_ready, 1)
                        dve.wait_ge(gt_ready, before + 1 + i)
                    for k in range(4):
                        feed(w + 2 * (chunks + k), i)
                        dve.wait_ge(tile_used, w + 2 * (chunks + k) + 2 + BODY * i)
                        for f, ps in enumerate(pair_banks(j + chunks + k)):
                            c = 2 * k + f
                            for s in range(n // T):
                                t = slice(s * T, (s + 1) * T)
                                if gate is None:
                                    ins = nc.vector.tensor_tensor(X[:, c, t], X[:, c, t], ps[:, t], ALU.add)
                                else:
                                    ins = nc.vector.scalar_tensor_tensor(
                                        out=X[:, c, t], in0=ps[:, t], scalar=GT[:, c, s:s + 1],
                                        in1=X[:, c, t], op0=ALU.mult, op1=ALU.add)
                        ins.then_inc(drained, 1)

                with dve.Fori(0, 2) as i:
                    group(S.j, S.w, S.a, S.q, S.m if mods else None, GROUP, 0, i)
                group(S.j + 2 * GJ, S.w + 2 * BODY, S.a + 2 * GROUP, S.q + 2 * GROUP,
                      S.m + 4 * GROUP if mods == 3 else None, LAST, 2 * GROUP, first=False)

            def drain_biased(name, n, layer, bias):
                S = STAGES[name]
                for k in range(4):
                    feed(S.w + 2 * k)
                    dve.wait_ge(tile_used, S.w + 2 * k + 2)
                    for f, ps in enumerate(pair_banks(S.j + k)):
                        c = 2 * k + f
                        for s in range(n // T):
                            t = slice(s * T, (s + 1) * T)
                            ins = nc.vector.tensor_scalar(ps[:, t], ps[:, t], col(bias, c),
                                                          mod(layer, 5)[:, c, s:s + 1], ALU.add, ALU.mult)
                        link(ins)
                        ins = nc.vector.tensor_tensor(X[:, c, 0:n], X[:, c, 0:n], ps[:, 0:n], ALU.add)
                    ins.then_inc(drained, 1)

            def by_mod(c, s):
                return A[:, c, s:s + 1]

            def drain_plain(name):
                S = STAGES[name]
                for k in range(4):
                    feed(S.w + 2 * k)
                    dve.wait_ge(tile_used, S.w + 2 * k + 2)
                    for f, ps in enumerate(pair_banks(S.j + k)):
                        c = 2 * k + f
                        ins = nc.vector.tensor_tensor(X[:, c, 0:T], X[:, c, 0:T], ps[:, 0:T], ALU.add)
                    ins.then_inc(drained, 1)

            def per_layer(i):
                S = STAGES[f"ple_e{i}"]
                dve.wait_ge(p_hi, i + 1)
                pin = PIN[:, 2 * i:2 * i + 2, :]
                nc.vector.tensor_tensor(PSPLIT[1], pin, PSPLIT[0].bitcast(F32), ALU.subtract)\
                    .then_inc(p_split, 1)
                feed(S.w)
                for j in range(4):
                    if j % 2 == 0:
                        dve.wait_ge(part_done, S.part + j // 2 + 1)
                    else:
                        dve.wait_ge(tile_used, S.w + j // 2 + 1)
                    for f, ps in enumerate(pair_banks(S.j + j)):
                        ins = nc.vector.tensor_copy(E[:, 2 * j + f, :], ps[:, 0:T])
                    ins.then_inc(drained, 1)
                norm(f"e{i}", T, lambda c, s: col("ple_norm_g", i * KC + c), src=E, dst=E)
                dve.wait_ge(x_normed, KC * (plain_no[f"e{i}"] + 1))
                norm(f"pg{i}", T, lambda c, s: col("ple_gate_norm_g", i * KC + c))
                S = STAGES[f"ple_g{i}"]
                for k in range(4):
                    feed(S.w + 2 * k)
                    dve.wait_ge(act_out, S.a + k + 1)
                    g = G[:, (S.j + k) % 3, :].rearrange("p (f t) -> p f t", f=2)
                    link(nc.vector.tensor_tensor(g, g, E[:, 2 * k:2 * k + 2, :], ALU.mult))
                    nc.vector.tensor_tensor(X[:, 2 * k:2 * k + 2, 0:T], X[:, 2 * k:2 * k + 2, 0:T], g, ALU.add)\
                        .then_inc(drained, 1)

            dve.wait_ge(params_in, 16)
            def add_taps(k):
                dve.wait_ge(taps_done, TAPS_PE * (k + 1))
                nc.vector.tensor_tensor(CV[:, k, :], CV[:, k, :], bank[k % 2][:, :], ALU.add)\
                    .then_inc(cv_ready, 1)

            dve.wait_ge(cond_ready, 1)
            lo(0)
            lo(1)
            for m in range(16):
                mod_unit(m)
            dve.wait_ge(mod_done, 16)
            gain("ffn0", 0, 1, 0)
            norm("ffn0", T + C, by_mod, shift=mod(0, 0))
            ffn("ffn0", T + C, 3, ((0, 2), 0))
            gain("conv", 0, 4, 1)
            norm("conv", T + C, by_mod, shift=mod(0, 3))
            dve.wait_ge(h_lo, KC * (split_no["conv"] + 1))
            for s in range(3):
                nc.vector.memset(U[:, :, s * SEG:s * SEG + PAD], 0.0)
            S = STAGES["pw1"]
            for k in range(8):
                feed(S.w + 2 * k)
                dve.wait_ge(act_out, S.a + k + 1)
                nc.vector.scalar_tensor_tensor(
                    out=both(k, PAD), in0=pair_banks(S.j + k)[0][:, :].rearrange("p (s t) -> p s t", s=2),
                    scalar=col("b_pw1", k), in1=G[:, (S.j + k) % 3, :].rearrange("p (s t) -> p s t", s=2),
                    op0=ALU.add, op1=ALU.mult).then_inc(drained, 1)
                mod_unit(S.m + k)
                dve.wait_ge(drained, S.j + k + 1)
                cv = CV[:, k, :].rearrange("p (s t) -> p s t", s=2)
                link(nc.vector.tensor_scalar(cv, both(k, 0), col("w_dw", k), col("b_dw", k),
                                             ALU.mult, ALU.add))
                for tap in range(1, TAPS - TAPS_PE):
                    link(nc.vector.scalar_tensor_tensor(
                        out=cv, in0=both(k, tap), scalar=col("w_dw", tap * KC + k), in1=cv,
                        op0=ALU.mult, op1=ALU.add))
                if k >= 1:
                    add_taps(k - 1)
            add_taps(KC - 1)
            dve.wait_ge(mu_ready, 1)
            for c in range(KC):
                nc.vector.tensor_tensor(CV[:, c, :], CV[:, c, :], bank[1][:, :], ALU.subtract)\
                    .then_inc(cv_centred, 1)
            dve.wait_ge(std_ready, norm_no["ln"] + 1)
            link(nc.vector.reciprocal(bank[1][:, :], STD[:, :]))
            for c in range(KC):
                nc.vector.tensor_tensor(CV[:, c, :], CV[:, c, :], bank[1][:, :], ALU.mult)\
                    .then_inc(cvn_ready, 1)
            for c in range(KC):
                dve.wait_ge(h_hi, KC * split_no["ln"] + c + 1)
                nc.vector.tensor_tensor(HNL[:, c, :], CV[:, c, :], HNH[:, c, :].bitcast(F32), ALU.subtract)\
                    .then_inc(h_lo, 1)
            drain_biased("pw2", T + C, 0, "b_pw2")
            dve.wait_ge(mod_done, 68)
            gain("ffn1", 0, 7, 2)
            norm("ffn1", T + C, by_mod, shift=mod(0, 6))
            ffn("ffn1", T + C, 3, ((0, 8), 2))
            gain("ffn2", 1, 1, 3)
            norm("ffn2", T + C, by_mod, shift=mod(1, 0))
            ffn("ffn2", T + C, 2, ((1, 2), 4))
            dve.wait_ge(mod_done, 144)
            gain("na", 1, 4, 4)
            norm("na", T + C, by_mod, shift=mod(1, 3))
            dve.wait_ge(h_lo, KC * (split_no["na"] + 1))
            S = STAGES["na_qk"]
            for k in range(8):
                feed(S.w + 2 * k)
                dve.wait_ge(tile_used, S.w + 2 * k + 2)
                for f, ps in enumerate(pair_banks(S.j + k)):
                    c = 2 * k + f
                    if k < 4:
                        ins = nc.vector.tensor_scalar(NQ[:, c, :], ps[:, 0:T], col("b_qkv", c), DH ** -0.5,
                                                      ALU.add, ALU.mult)
                    else:
                        ins = nc.vector.tensor_scalar(NK[:, c - KC, :], ps[:, :], col("b_qkv", c), None,
                                                      ALU.add)
                ins.then_inc(drained, 1)
            S = STAGES["na_v"]
            for k in range(4):
                feed(S.w + 2 * k)
                dve.wait_ge(tile_used, S.w + 2 * k + 2)
                for f, ps in enumerate(pair_banks(S.j + k)):
                    for h in range(2):
                        c = 2 * k + f
                        ins = nc.vector.tensor_copy(NV[h][:, :, c * P:(c + 1) * P],
                                                    ps[:, h * T:(h + 1) * T].rearrange("p (s d) -> p s d", s=2))
                ins.then_inc(drained, 1)

            def maxima(u):
                h, t = u // 2, u % 2
                dve.wait_ge(s_ready, u + 1)
                dve.wait_ge(bias_ready, h + 1)
                ps = bank[u % 4]
                at = (2 - 2 * t) * GRID
                link(nc.vector.tensor_tensor(ps[:, 0:T], ps[:, 0:T], RBT[:, h % 2, at:at + T], ALU.add))
                nc.vector.tensor_reduce(NM[:, u:u + 1], ps[:, :], AX.X, ALU.max, negate=True)\
                    .then_inc(s_max, 1)

            def diagonal(u):
                dve.wait_ge(p_ready, u + 1)
                link(nc.vector.reciprocal(RSUM[:, u:u + 1], SUM[:, u:u + 1]))
                if u >= 2:
                    dve.wait_ge(pt_ready, u - 1)
                nc.vector.tensor_scalar(DG[:, u % 2, :], const("ident"), RSUM[:, u:u + 1], None, ALU.mult)\
                    .then_inc(dg_ready, 1)

            def copy_output(h):
                r = DH * (h % 2)
                dve.wait_ge(o_ready, h + 1)
                nc.vector.tensor_scalar(O32[r:r + DH, h // 2, :], bank[6 + h % 2][r:r + DH, 0:T],
                                        cols[r:r + DH, COLS["b_qkv"][0] + 2 * KC + h // 2:
                                             COLS["b_qkv"][0] + 2 * KC + h // 2 + 1],
                                        None, ALU.add).then_inc(o_out, 1)

            for u in range(2 * H + 5):
                if u < 2 * H:
                    maxima(u)
                if 1 <= u <= 2 * H:
                    diagonal(u - 1)
                if 4 <= u <= 2 * H + 2 and u % 2 == 0:
                    copy_output((u - 4) // 2)
                if u >= 8 and u % 4 == 0:
                    split_output((u - 8) // 4)
            drain_biased("na_o", T, 1, "b_o")
            gain("ffn3", 1, 7, 5)
            norm("ffn3", T, by_mod, shift=mod(1, 6))
            ffn("ffn3", T, 0, ((1, 8), 6))
            norm("final", T, lambda c, s: col("final_g", c), dst=X)

            norm("ab", T, lambda c, s: col("ab_norm_g", c))
            dve.wait_ge(gate_step, 1)
            nc.vector.tensor_scalar(IG[0:4, :], bank[2][0:4, 0:T], cols[0:4, gb:gb + 1], None, ALU.add)
            nc.vector.tensor_scalar(XF[0:4, :], bank[3][0:4, 0:T], cols[0:4, gb + 1:gb + 2], None, ALU.add)\
                .then_inc(gate_step, 1)
            S = STAGES["ab_in"]
            nc.vector.memset(MPAD[:, :, 0:3], 0.0)
            for k in range(12):
                feed(S.w + 2 * k)
                dve.wait_ge(tile_used, S.w + 2 * k + 2)
                for f, ps in enumerate(pair_banks(S.j + k)):
                    if k < 2:
                        ins = nc.vector.tensor_scalar(RQK[:, 2 * k + f, :], ps[:, 0:T],
                                                      1.0 if k == 0 else DH ** -0.5, None, ALU.mult)
                    elif k in (2, 3, 8, 9):
                        v = RV if k < 4 else MV
                        c = 2 * (k % 2) + f
                        ins = nc.vector.tensor_copy(v[:, :, c * P:(c + 1) * P],
                                                    ps[:, 0:T].rearrange("p (s d) -> p s d", s=2))
                    elif k in (6, 7):
                        ins = nc.vector.tensor_copy(MPAD[:, 2 * (k - 6) + f, 3:3 + T], ps[:, 0:T])
                    else:
                        dst = RG if k < 6 else MO
                        ins = nc.vector.tensor_copy(dst[:, 2 * (k % 2) + f, :], ps[:, 0:T])
                ins.then_inc(drained, 1)
            dve.wait_ge(drained, S.j + 12)
            for c in range(4):
                link(nc.vector.tensor_scalar(MQK[:, c, :], MPAD[:, c, 0:T], col("ab_conv_w", c),
                                             col("ab_conv_b", c), ALU.mult, ALU.add))
                for tap in range(1, 4):
                    ins = nc.vector.scalar_tensor_tensor(out=MQK[:, c, :], in0=MPAD[:, c, tap:tap + T],
                                                         scalar=col("ab_conv_w", 4 * tap + c), in1=MQK[:, c, :],
                                                         op0=ALU.mult, op1=ALU.add)
                    if tap < 3:
                        link(ins)
                ins.then_inc(mconv_ready, 1)
            for c in range(4):
                dve.wait_ge(rotated, c + 1)
                nc.vector.tensor_tensor(RQK[:, c, :], RQK[:, c, :], const("cos"), ALU.mult)
                link(nc.vector.tensor_tensor(bank[4 + c][:, 0:T], bank[4 + c][:, 0:T], const("sin"), ALU.mult))
                nc.vector.tensor_tensor(RQK[:, c, :], RQK[:, c, :], bank[4 + c][:, 0:T], ALU.add)\
                    .then_inc(rope_done, 1)
            dve.wait_ge(gate_step, 3)
            link(nc.vector.tensor_scalar(XF[0:4, :], XF[0:4, :], 0.0, None, ALU.min))
            link(nc.vector.tensor_tensor(LROW[0:4, :], XF[0:4, :], LROW[0:4, :], ALU.subtract))
            link(nc.vector.tensor_tensor_scan(BROW[0:4, :], ones_row, LROW[0:4, :], 0.0, ALU.mult, ALU.add))
            link(nc.vector.tensor_tensor(AROW[0:4, :], IG[0:4, :], BROW[0:4, :], ALU.subtract))
            link(nc.vector.tensor_tensor_scan(MROW[0:4, :], AROW[0:4, :], AROW[0:4, :], 0.0, ALU.max, ALU.max))
            nc.vector.scalar_tensor_tensor(out=NMT[0:4, :], in0=BROW[0:4, :], scalar=-1.0, in1=MROW[0:4, :],
                                           op0=ALU.mult, op1=ALU.subtract).then_inc(gate_step, 1)
            dve.wait_ge(gate_step, 5)
            nc.vector.tensor_copy(ACOL[:, :], bank[0][:, 0:8])
            for b in range(2):
                ps = bank[2 + b][:, :].rearrange("p (e t) -> p e t", e=2)
                mask = const("causal_t").unsqueeze(1).to_broadcast([P, 2, P])
                w = WT[:, 2 * b:2 * b + 2, :]
                nc.vector.tensor_tensor(w[:, :, 0:P], mask, ps[:, :, 0:P], ALU.subtract)
                nc.vector.tensor_scalar(w[:, :, P:T], ps[:, :, P:T], -1.0, None, ALU.mult)
                ins = nc.vector.tensor_tensor(w[:, :, T:T + P], mask, ps[:, :, P:T], ALU.subtract)
            ins.then_inc(gate_step, 1)
            dve.wait_ge(rg_ready, 1)
            dve.wait_ge(mo_ready, 1)
            for pr in range(4):
                base = AB_BASE[pr]
                mlstm = pr // 2
                dve.wait_ge(ab_step, base + 1)
                for e in range(2):
                    h = 2 * (pr % 2) + e
                    for a, b in ((0, T), (T, T + P)):
                        if mlstm:
                            ins = nc.vector.scalar_tensor_tensor(
                                out=SW[:, e, a:b], in0=bank[2 + e][:, a:b], scalar=DH ** -0.5,
                                in1=WT[:, h, a:b], op0=ALU.mult, op1=ALU.mult)
                        else:
                            ins = nc.vector.tensor_tensor(SW[:, e, a:b], bank[2 + e][:, a:b],
                                                          const("decay", h * T, b - a), ALU.mult)
                ins.then_inc(ab_step, 1)
                if mlstm:
                    dve.wait_ge(ab_step, base + 3)
                    h = 2 * (pr % 2)
                    den = bank[7][:, :].rearrange("p (e t) -> p e t", e=2)
                    link(nc.vector.tensor_tensor(DEN, den, EMT[:, h:h + 2, :], ALU.max))
                    link(nc.vector.scalar_tensor_tensor(out=DEN, in0=den, scalar=-1.0, in1=DEN,
                                                        op0=ALU.mult, op1=ALU.max))
                    link(nc.vector.reciprocal(DEN, DEN))
                    num = bank[6][:, :].rearrange("p (e t) -> p e t", e=2)
                    nc.vector.tensor_tensor(num, num, DEN, ALU.mult).then_inc(ab_step, 1)
                base += mlstm
                dve.wait_ge(ab_step, base + 6)
                link(nc.vector.reciprocal(STD[:, :], STD[:, :]))
                for e in range(2):
                    h = 2 * (pr % 2) + e
                    t = slice(e * T, (e + 1) * T)
                    link(nc.vector.scalar_tensor_tensor(
                        out=O32[:, 2 * pr + e, :], in0=bank[6][:, t],
                        scalar=col("m_g" if mlstm else "ret_g", h), in1=STD[:, t], op0=ALU.mult, op1=ALU.mult))
                    ins = nc.vector.tensor_tensor(O32[:, 2 * pr + e, :], O32[:, 2 * pr + e, :],
                                                  (MO if mlstm else RG)[:, h, :], ALU.mult)
                ins.then_inc(ab_step, 1)
            for c in range(KC, 2 * KC):
                split_output(c)
            drain_plain("ab_out")
            norm("ffn4", T, lambda c, s: col("ffn_norm_g", c))
            ffn("ffn4", T, causal=0)
            per_layer(0)
            norm("nsa", T, lambda c, s: col("nsa_norm_g", c))
            dve.wait_ge(nsa_step, 1)
            S = STAGES["nsa_in"]
            for k in range(8):
                feed(S.w + 2 * k)
                dve.wait_ge(tile_used, S.w + 2 * k + 2)
                for f, ps in enumerate(pair_banks(S.j + k)):
                    if k in (4, 5):
                        pos = col("pos_k" if k == 4 else "pos_v", 0, 16)
                        for lp in range(2):
                            r = slice(DH * lp, DH * lp + DH)
                            rows = ps[r, lp:lp + 255]
                            rows = bass.AP(rows.tensor, rows.offset, [rows.ap[0], [2, 16], [16, NC_CMP]])
                            ins = nc.vector.tensor_tensor(
                                BLK[r, k - 4, :, f * 15:(f + 1) * 15], rows,
                                pos[r, :].unsqueeze(2).to_broadcast([DH, 16, NC_CMP]), ALU.add)
                    elif k == 7:
                        ins = nc.vector.tensor_copy(SV[:, :, f * P:(f + 1) * P],
                                                    ps[:, 0:T].rearrange("p (s d) -> p s d", s=2))
                    else:
                        ins = nc.vector.tensor_copy(QK[:, 2 * min(k, 4) + f, :], ps[:, 0:T])
                ins.then_inc(drained, 1)
                if k == 3:
                    link(nc.vector.tensor_scalar(QG[:, :], col("q_g"), DH ** -0.5, None, ALU.mult))
            dve.wait_ge(blk_hi, 1)
            nc.vector.tensor_tensor(BSPLIT[1], BLK[:, :, :, :], BSPLIT[0].bitcast(F32), ALU.subtract)\
                .then_inc(blk_split, 1)
            nc.vector.tensor_tensor(GATE[:, :].rearrange("p (s n) -> p s n", s=2),
                                    bank[0][:, 0:96].rearrange("p (s n) -> p s n", s=2),
                                    col("gate_b", 0, 48).unsqueeze(1).to_broadcast([P, 2, 48]), ALU.add)\
                .then_inc(nsa_step, 1)
            for n in range(5):
                dve.wait_ge(qstd_ready, n + 1)
                link(nc.vector.reciprocal(STD[:, :], STD[:, :]))
                for f in range(2):
                    c = 2 * n + f
                    g = QG[:, :] if c < 8 else col("k_g", c - 7)
                    ins = nc.vector.scalar_tensor_tensor(out=QK[:, c, :], in0=QK[:, c, :], scalar=g,
                                                         in1=STD[:, f * T:(f + 1) * T],
                                                         op0=ALU.mult, op1=ALU.mult)
                ins.then_inc(qn_ready, 1)
            S = STAGES["nsa_mlp"]
            for m in range(2):
                feed(S.w + 4 * m)
                feed(S.w + 4 * m + 2)
                dve.wait_ge(tile_used, S.w + 4 * m + 4)
                for f, ps in enumerate(pair_banks(S.j + m)):
                    ins = nc.vector.tensor_copy(HC[:, m, f, :], ps[:, 0:30])
                ins.then_inc(drained, 1)
            dve.wait_ge(nsa_step, 7)
            nc.vector.tensor_copy(VCS[0:15, :], bank[0][0:15, 0:P])
            link(nc.vector.reciprocal(STD[:, 0:15], STD[:, 0:15]))
            nc.vector.scalar_tensor_tensor(out=KCN[:, :], in0=bank[1][:, 0:15], scalar=col("k_g", 0),
                                           in1=STD[:, 0:15], op0=ALU.mult, op1=ALU.mult)\
                .then_inc(nsa_step, 1)
            dve.wait_ge(nsa_step, 9)
            for t in range(2):
                pc = PC[:, t, :, 0:15]
                for g in range(2):
                    ps = bank[2 + 2 * t + g][:, 0:128].rearrange("p (h n) -> p h n", h=8)[:, :, 0:15]
                    ins = nc.vector.tensor_tensor(pc[:, 8 * g:8 * g + 8, :], ps,
                                                  cmp_add[:, t:t + 1, 0:15].to_broadcast([P, 8, 15]), ALU.add)
                link(ins)
                link(nc.vector.tensor_reduce(CM[:, t, :], pc, AX.X, ALU.max))
                ins = nc.vector.tensor_tensor(pc, pc, CM[:, t, :].unsqueeze(2).to_broadcast([P, H, 15]),
                                              ALU.subtract)
            ins.then_inc(nsa_step, 1)
            dve.wait_ge(pc_exp, 1)
            dve.wait_ge(ngate_ready, 1)
            gates = GATE[:, :].rearrange("p (s h b) -> p s h b", s=2, b=3)
            for t in range(2):
                pc = PC[:, t, :, 0:15]
                link(nc.vector.tensor_reduce(CM[:, t, :], pc, AX.X, ALU.add))
                link(nc.vector.reciprocal(CM[:, t, :], CM[:, t, :]))
                link(nc.vector.tensor_tensor(CM[:, t, :], CM[:, t, :], gates[:, t, :, 0], ALU.mult))
                link(nc.vector.tensor_tensor(pc, pc, cmp_valid[:, t:t + 1, 0:15].to_broadcast([P, H, 15]),
                                             ALU.mult))
                ins = nc.vector.tensor_tensor(pc, pc, CM[:, t, :].unsqueeze(2).to_broadcast([P, H, 15]), ALU.mult)
            ins.then_inc(nsa_step, 1)

            def nsa_maxima(u):
                t = u % 2
                dve.wait_ge(ns_ready, u + 1)
                ps = bank[u % 3][:, 0:2 * P * (t + 1)].rearrange("p (b k) -> p b k", b=2)
                link(nc.vector.tensor_tensor(ps[:, :, t * P:(t + 1) * P], ps[:, :, t * P:(t + 1) * P],
                                             const("causal").unsqueeze(1).to_broadcast([P, 2, P]), ALU.add))
                nc.vector.tensor_reduce(NM[:, 2 * u:2 * u + 2], ps, AX.X, ALU.max, negate=True)\
                    .then_inc(ns_max, 1)

            def nsa_diagonals(u):
                h, t = u // 4 + 8 * (u // 2 % 2), u % 2
                dve.wait_ge(np_ready, u + 1)
                link(nc.vector.reciprocal(RSUM[:, 2 * u:2 * u + 2], SUM[:, 2 * u:2 * u + 2]))
                link(nc.vector.tensor_tensor(RSUM[:, 2 * u:2 * u + 2], RSUM[:, 2 * u:2 * u + 2],
                                             gates[:, t, h, 1:3], ALU.mult))
                if u >= 2:
                    dve.wait_ge(npt_ready, u - 1)
                for b in range(2):
                    ins = nc.vector.tensor_scalar(DG2[:, u % 2, b, :], const("ident"),
                                                  RSUM[:, 2 * u + b:2 * u + b + 1], None, ALU.mult)
                ins.then_inc(ndg_ready, 1)

            def nsa_copy_output(n):
                r = DH * (n % 2)
                dve.wait_ge(no_ready, n + 1)
                nc.vector.tensor_copy(O32[r:r + DH, n // 2, :], bank[6 + n % 2][r:r + DH, 0:T])\
                    .then_inc(no_out, 1)

            for u in range(2 * H + 5):
                if u < 2 * H:
                    nsa_maxima(u)
                if 1 <= u <= 2 * H:
                    nsa_diagonals(u - 1)
                if 4 <= u <= 2 * H + 2 and u % 2 == 0:
                    nsa_copy_output((u - 4) // 2)
                if u >= 8 and u % 4 == 0:
                    split_output(2 * KC + (u - 8) // 4)
            drain_plain("nsa_out")
            norm("ffn5", T, lambda c, s: col("ffn_norm_g", KC + c))
            ffn("ffn5", T, causal=1)
            per_layer(1)

        @block.gpsimd
        def _(pool):
            pool.wait_ge(consts_in, 16)

            def ffn(name, n, gelu=False):
                S = STAGES[name]
                a = T if gelu else 0

                def group(j, q, chunks, i=0):
                    for k in range(chunks):
                        src = G[:, (j + k) % 3, a:a + n]
                        pool.wait_ge(drained, j + k + 1 + GJ * i)
                        nc.gpsimd.tensor_tensor(HDH[:, k, 0:n], src, const("one").to_broadcast([P, n]),
                                                ALU.mult).then_inc(hid_hi, 1)
                        pool.wait_ge(hid_hi, q + k + 1 + GROUP * i)
                        nc.gpsimd.tensor_tensor(HDL[:, k, 0:n], src, HDH[:, k, 0:n].bitcast(F32),
                                                ALU.subtract).then_inc(hid_ready, 1)

                with pool.Fori(0, 2) as i:
                    group(S.j, S.q, GROUP, i)
                group(S.j + 2 * GJ, S.q + 2 * GROUP, LAST)

            ffn("ffn0", T + C)
            for d in range(KC * TAPS_PE):
                c, tap = d // TAPS_PE, TAPS - TAPS_PE + d % TAPS_PE
                if d >= 4:
                    pool.wait_ge(taps_done, d - 3)
                nc.gpsimd.tensor_scalar(DIAG[:, d % 4, :], const("ident"), col("w_dw", tap * KC + c), 1.0,
                                        ALU.mult, ALU.mult).then_inc(diag_ready, 1)
            ffn("ffn1", T + C)
            ffn("ffn2", T + C)

            def load_bias(h):
                if h >= 2:
                    pool.wait_ge(s_max, 2 * h - 2)
                pool.dma_start(RB_T[:, h % 2, :], rpb[h, :, :]).then_inc(bias_in[h % 2], 16)

            load_bias(0)
            for h in range(H):
                if h + 1 < H:
                    load_bias(h + 1)
                pool.wait_ge(bias_in[h % 2], 16 * (h // 2 + 1))
                nc.gpsimd.tensor_tensor(RBT[:, h % 2, :].rearrange("p (u k) -> p u k", u=6),
                                        RB_T[:, h % 2, :].rearrange("p (u k) -> p u k", u=6),
                                        const("window").unsqueeze(1).to_broadcast([P, 6, GRID]),
                                        ALU.add).then_inc(bias_ready, 1)

            ffn("ffn3", T)
            pool.wait_ge(x_normed, KC)
            pool.dma_start(PIN, p_in).then_inc(p_loaded, 16)
            ffn("ffn4", T, True)
            ffn("ffn5", T, True)




def tiles(W):
    k = W.shape[0] // P
    out = np.zeros((W.shape[1] // P, P, KC, P), W.dtype)
    out[:, :, :k] = W.reshape(k, P, -1, P).transpose(2, 1, 0, 3)
    return out.reshape(-1, P, TILE)


def alternate(a, b):
    return np.stack([a, b], axis=1).reshape(-1, P, TILE)


def columns(v):
    return v.reshape(-1, P).T


def weight_stream(a):
    def ffn(gate, up, down):
        parts, f = [], 0
        for n in (GROUP, GROUP, LAST):
            s = slice(f * P, (f + n) * P)
            parts += [alternate(tiles(gate[:, s]), tiles(up[:, s])), tiles(down[s])]
            f += n
        return parts

    def cffn(i):
        up = a["ffn_w_up_2"][i]
        return ffn(up[:, :F], up[:, F:], a["ffn_w_down_2"][i])

    def ple(i):
        w = a["ple_w_2"][i].reshape(2, P, 2, 512).transpose(2, 1, 0, 3)
        return [w.reshape(2, P, TILE), tiles(a["ple_w_gate_2"][i])]

    def first_ffn(i, j):
        return ffn(a["ffn_w_gate"][i, j], a["ffn_w_up"][i, j], a["ffn_w_down"][i, j])

    pw1 = a["conv_w_pw1"][0]
    parts = first_ffn(0, 0) + [alternate(tiles(pw1[:, :D]), tiles(pw1[:, D:])), tiles(a["conv_w_pw2"][0])]
    parts += first_ffn(0, 1) + first_ffn(1, 0) + [tiles(a["na_w_qkv"][0]), tiles(a["na_w_o"][0])]
    parts += first_ffn(1, 1)
    parts += [tiles(a["ab_w_in_2"][0][:, :3072]), tiles(a["ab_w_out_2"][0])]
    parts += cffn(0) + ple(0)
    w = a["nsa_w_in_2"][0]
    q = w[:, :1024].reshape(D, 2, 8, DH).transpose(0, 2, 1, 3).reshape(D, 1024)
    kc, vc, ks, vs, kw, vw = (w[:, 1024 + 128 * n:1152 + 128 * n] for n in range(6))

    def twice(m):
        return np.repeat(m.reshape(D, 2, 1, DH), 2, axis=2).reshape(D, 256)

    parts += [tiles(m) for m in (q, twice(kc), twice(vc), ks, kw, vs, vw)]
    for w1 in ("nsa_cmp_w1k_2", "nsa_cmp_w1v_2"):
        parts += [tiles(a[w1][0][:1024]), tiles(a[w1][0][1024:])]
    wo = a["nsa_w_out_2"][0].reshape(2, 8, DH, D).transpose(1, 0, 2, 3).reshape(D, D)
    parts += [tiles(wo)] + cffn(1) + ple(1)
    return np.concatenate(parts)


def parameters(a):
    two = lambda v: np.concatenate([v, v])
    mod_b = np.repeat(columns(a["mod_b"])[:, :, None], 2, axis=2).reshape(P, 288)
    rows4 = np.zeros((P, 2), np.float32)
    rows4[0:4, 0], rows4[0:4, 1] = a["ab_ig_b_2"][0], a["ab_fg_b_2"][0]
    cmp_pos = lambda v: v[0].reshape(16, P).T
    chunked = lambda w: w.reshape(-1, P, w.shape[-1]).transpose(1, 0, 2).reshape(P, -1)
    by_name = {
        "mod_b": mod_b, "norm_g": columns(a["norm_g"]), "b_pw1": columns(a["conv_b_pw1"]),
        "w_dw": columns(a["conv_w_dw"]), "b_dw": columns(a["conv_b_dw"]), "ln_g": columns(a["conv_ln_g"]),
        "ln_b": columns(a["conv_ln_b"]), "b_pw2": columns(a["conv_b_pw2"]), "b_qkv": columns(a["na_b_qkv"]),
        "b_o": columns(a["na_b_o"]), "final_g": columns(a["final_g"]), "ab_norm_g": columns(a["ab_norm_g_2"]),
        "ab_conv_w": columns(a["ab_conv_w_2"]), "ab_conv_b": columns(a["ab_conv_b_2"]),
        "ret_g": columns(a["ab_ret_norm_g_2"]), "m_g": columns(a["ab_m_norm_g_2"]), "gate_bias": rows4,
        "ab_wgate": chunked(a["ab_w_in_2"][0][:, 3072:]), "nsa_norm_g": columns(a["nsa_norm_g_2"]),
        "q_g": two(a["nsa_q_norm_g_2"][0])[:, None],
        "k_g": np.concatenate([a["nsa_k_norm_g_2"][0]] * 2, axis=1).T,
        "pos_k": cmp_pos(a["nsa_cmp_pos_k_2"]), "pos_v": cmp_pos(a["nsa_cmp_pos_v_2"]),
        "gate_b": np.repeat(a["nsa_gate_b_2"], P, axis=0),
        "nsa_wgate": chunked(a["nsa_w_in_2"][0][:, 1792:]),
        "w2k": chunked(a["nsa_cmp_w2k_2"][0]), "w2v": chunked(a["nsa_cmp_w2v_2"][0]),
        "ffn_norm_g": columns(a["ffn_norm_g_2"]), "ffn_conv_w": columns(a["ffn_conv_w_2"]),
        "ffn_conv_b": columns(a["ffn_conv_b_2"]), "ple_norm_g": columns(a["ple_norm_g_2"]),
        "ple_gate_norm_g": columns(a["ple_gate_norm_g_2"]),
    }
    for name, v in by_name.items():
        assert v.shape == (P, COLS[name][1]), (name, v.shape)
    return np.concatenate([by_name[name] for name in COLS], axis=1)


def constants():
    p = np.arange(P)
    t = np.arange(T)
    block64 = (p[:, None] // 64 == p[None, :] // 64) / 64
    rot = np.zeros((P, P))
    for m in range(P):
        rot[m + 32 if m % 64 < 32 else m - 32, m] = -1.0 if m % 64 < 32 else 1.0
    inv = (np.float32(10000.0) ** (-np.arange(32, dtype=np.float32) / np.float32(32))).astype(np.float32)
    ang = (t.astype(np.float32)[None, :] * inv[p % 32][:, None]).astype(np.float32)
    log_g = np.log1p(-np.exp2(-5.0 - np.arange(4)))
    diff = t[None, :] - p[:, None]
    decay = [np.where(diff >= 0, np.exp(np.maximum(diff, 0) * g), 0.0) for g in log_g]
    c, kc = p[:, None] % GRID, np.arange(GRID)[None, :]
    start = np.clip(c - 8, 0, GRID - 16)
    q = p[:, None, None] + P * np.arange(2)[None, :, None]
    n = np.arange(16)[None, None, :]
    cmp_valid = (16 * n + 31 <= q) & (n < NC_CMP)
    sel = np.zeros((P, 4, P))
    for h in range(4):
        sel[h, h, :] = 1.0
    by_name = {
        "ident": np.eye(P), "mean_all": np.full((P, P), 1 / D), "ones": np.ones((P, P)),
        "mean64": block64, "mean128": np.full((P, P), 1 / P), "rot": rot,
        "cos": np.cos(ang.astype(np.float64)), "sin": np.sin(ang.astype(np.float64)),
        "causal": np.where(p[None, :] <= p[:, None], 0.0, MASKED),
        "causal_t": np.where(p[:, None] <= p[None, :], 0.0, MASKED),
        "decay": np.concatenate(decay, axis=1),
        "window": np.where((kc >= start) & (kc < start + 16), 0.0, MASKED),
        "cmp_add": np.where(cmp_valid, 0.0, MASKED).reshape(P, 32),
        "cmp_valid": cmp_valid.reshape(P, 32), "sel": sel.reshape(P, 4 * P),
        "eps6": np.full((P, 1), 1e-6), "eps5": np.full((P, 1), 1e-5), "one": np.ones((P, 1)),
    }
    return np.concatenate([by_name[name] for name in CONST], axis=1).astype(np.float32)


def relative_bias(rpb):
    c, kc = np.arange(GRID)[:, None], np.arange(GRID)[None, :]
    col = np.clip(kc - c, -(CB // 2), CB // 2) + CB // 2
    rows = [rpb[:, 5 - r:11 - r][:, :, col].transpose(0, 2, 1, 3) for r in range(2)]
    return np.concatenate(rows, axis=1).reshape(H, P, 6 * GRID)


def kernel(**a):
    import concourse.bacc as bacc
    from concourse.bass_utils import run_bass_kernel_spmd

    a = {n: np.asarray(v) for n, v in a.items()}
    tokens = np.concatenate([a["x"][0], a["ctx"][0]])
    arrays = {
        "x_in": tokens.reshape(T + C, KC, P).transpose(2, 1, 0),
        "params": parameters(a),
        "consts": constants(),
        "cond": np.stack([a["c"][0], a["c_ctx"]]),
        "weights": weight_stream(a),
        "mod_w": a["mod_w"].transpose(0, 2, 1).reshape(-1, P, D),
        "rpb": relative_bias(a["na_rpb"][0]),
        "p_in": a["p_2"][:, 0].reshape(2, T, 2, P).transpose(3, 0, 2, 1),
    }
    arrays = {n: np.ascontiguousarray(v) for n, v in arrays.items()}
    nc = bacc.Bacc("TRN2", target_bir_lowering=False, num_devices=1)
    args = [nc.dram_tensor(n, v.shape, F32, kind="ExternalInput").ap() for n, v in arrays.items()]
    out = nc.dram_tensor("out", (P, KC, T), F32, kind="ExternalOutput").ap()
    build(nc, *args, out)
    r = run_bass_kernel_spmd(nc, [arrays], core_ids=[0])
    got = r.results[0]["out"]
    return got.transpose(2, 1, 0).reshape(1, T, D)
```

```python
from contextlib import ExitStack

import numpy as np

import concourse.bass as bass
from concourse import mybir

F32 = mybir.dt.float32
F32R = mybir.dt.float32r
ALU = mybir.AluOpType
ACT = mybir.ActivationFunctionType
AX = mybir.AxisListType

P = 128
D = 1024
KC = D // P
T = 256
C = 256
F = 2816
FC = F // P
RAW = 6
SPLIT = 4
TILE = KC * P
GROUP = 8
GJ = GROUP + 4
BODY = 2 * GJ
LAST = 6
TAPS_PE = 11
TAPS = 31
PAD = TAPS // 2
SEG = T + PAD
UP = 2 * SEG + PAD
H = 16
DH = 64
GRID = 64
CB = 31
MASKED = -1e30
NC_CMP = 15
PLE = 256
assert FC == 2 * GROUP + LAST and BODY % RAW == 0 and BODY % SPLIT == 0
FFN_JOBS = 2 * GJ + LAST + 4


class Stage:
    def __init__(self, w, j, m, part, a, q):
        self.w, self.j, self.m, self.part, self.a, self.q = w, j, m, part, a, q


def plan():
    stages, at = {}, [0] * 6
    ffn = (2 * FFN_JOBS, FFN_JOBS)
    for name, (tiles, jobs), mods, parts, acts, hidden in (
        ("mod", (0, 0), 16, 0, 0, 0), ("ffn0", ffn, 44, 0, FC, FC),
        ("pw1", (16, 8), 4, 0, 8, 0), ("pw2", (8, 4), 0, 0, 0, 0),
        ("ffn1", ffn, 44, 0, FC, FC), ("ffn2", ffn, 36, 0, FC, FC),
        ("na_qk", (16, 8), 0, 0, 0, 0), ("na_v", (8, 4), 0, 0, 0, 0), ("na_o", (8, 4), 0, 0, 0, 0),
        ("ffn3", ffn, 0, 0, FC, FC),
        ("ab_in", (24, 12), 0, 0, 0, 0), ("ab_out", (8, 4), 0, 0, 0, 0),
        ("ffn4", ffn, 0, 0, FC, FC),
        ("ple_e0", (2, 4), 0, 2, 0, 0), ("ple_g0", (8, 4), 0, 0, 4, 0),
        ("nsa_in", (16, 8), 0, 0, 0, 0), ("nsa_mlp", (8, 2), 0, 0, 0, 0), ("nsa_out", (8, 4), 0, 0, 0, 0),
        ("ffn5", ffn, 0, 0, FC, FC),
        ("ple_e1", (2, 4), 0, 2, 0, 0), ("ple_g1", (8, 4), 0, 0, 4, 0),
    ):
        stages[name] = Stage(*at)
        at = [x + y for x, y in zip(at, (tiles, jobs, mods, parts, acts, hidden))]
    assert at[2] == 144
    return stages, at[0], at[1]


STAGES, NTILES, NJOBS = plan()

COLS = {}
_at = 0
for _name, _n in (
    ("mod_b", 288), ("norm_g", 6 * KC), ("b_pw1", 2 * KC), ("w_dw", TAPS * KC),
    ("b_dw", KC), ("ln_g", KC), ("ln_b", KC), ("b_pw2", KC), ("b_qkv", 3 * KC), ("b_o", KC),
    ("final_g", KC), ("ab_norm_g", KC), ("ab_conv_w", 4 * 4), ("ab_conv_b", 4), ("ret_g", 4),
    ("m_g", 4), ("gate_bias", 2), ("ab_wgate", 8 * KC), ("nsa_norm_g", KC), ("q_g", 1), ("k_g", 3),
    ("pos_k", 16), ("pos_v", 16), ("gate_b", 48), ("nsa_wgate", 48 * KC), ("w2k", 2 * DH),
    ("w2v", 2 * DH), ("ffn_norm_g", 2 * KC), ("ffn_conv_w", 2 * 3 * FC), ("ffn_conv_b", 2 * FC),
    ("ple_norm_g", 2 * KC), ("ple_gate_norm_g", 2 * KC),
):
    COLS[_name] = (_at, _n)
    _at += _n
NCOLS = _at

CONST = {}
_at = 0
for _name, _n in (
    ("ident", P), ("mean_all", P), ("ones", P), ("mean64", P), ("mean128", P), ("rot", P),
    ("cos", T), ("sin", T), ("causal", P), ("causal_t", P), ("decay", 4 * T), ("window", GRID),
    ("cmp_add", 2 * 16), ("cmp_valid", 2 * 16), ("sel", 4 * P), ("eps6", 1), ("eps5", 1), ("one", 1),
):
    CONST[_name] = (_at, _n)
    _at += _n
NCONST = _at


def build(nc, x_in, params, consts, cond, weights, mod_w, rpb, p_in, out):
    ctx = ExitStack()
    with ctx:
        def sb(name, shape, dt=F32):
            return ctx.enter_context(nc.sbuf_tensor(name, shape, dt))

        def sem(name):
            return ctx.enter_context(nc.semaphore(name))

        raw = [sb(f"raw{n}", [P, TILE]) for n in range(RAW)]
        wh = [sb(f"wh{n}", [P, TILE], F32R) for n in range(SPLIT)]
        wl = [sb(f"wl{n}", [P, TILE], F32R) for n in range(SPLIT)]
        X = sb("X", [P, KC, T + C])
        HNH = sb("HNH", [P, KC, T + C], F32R)
        HNL = sb("HNL", [P, KC, T + C], F32R)
        with nc.sbuf_tensor("arena", [P, KC * UP + KC * (T + C)], F32) as hid:
            pass
        with nc.sbuf_tensor("HDH", [P, GROUP, T + C], F32R) as HDH:
            with nc.sbuf_tensor("HDL", [P, GROUP, T + C], F32R) as HDL:
                pass
        sb("arena_room", [P, KC * UP + KC * (T + C)])
        with nc.sbuf_tensor("arena2", [P, 5 * TILE], F32) as hid2:
            pass
        mod_ring = sb("mod_ring", [P, 2, TILE])
        CB = sb("CB", [P, 2, TILE])
        junk = sb("junk", [P, TILE])
        H32 = hid[:, 0:KC * (T + C)].rearrange("p (c t) -> p c t", c=KC)
        G = sb("G", [P, 3, T + C])
        SQ = sb("SQ", [P, 2, T + C])
        STD = sb("STD", [P, T + C])
        cols = sb("cols", [P, NCOLS])
        con = sb("con", [P, NCONST])
        PBUF = [sb(f"embedding{n}", [P, 512], F32R) for n in range(2)]
        with nc.sbuf_tensor("blocks", [P, 2 * 960], F32R) as BBUF:
            pass
        RB_T = sb("bias_rows", [P, 2, 6 * GRID])
        RBT = sb("bias_masked", [P, 2, 6 * GRID])
        sb("bias_rest", [P, 2 * 960 - 4 * 6 * GRID])
        MOD = sb("MOD", [P, 144, 2])
        MA = sb("MA", [P, 2, 2])
        warm = sb("warm", [P, 16])
        A = sb("A", [P, KC, 2])
        GT = sb("GT", [P, KC, 2])
        bank = [ctx.enter_context(nc.psum_tensor(f"bank{b}", [P, 512], F32)) for b in range(8)]

        def col(name, a=0, n=1):
            return cols[:, COLS[name][0] + a:COLS[name][0] + a + n]

        def const(name, a=0, n=None):
            at, size = CONST[name]
            return con[:, at + a:at + a + (size - a if n is None else n)]

        def mod(layer, n):
            a = layer * 72 + n * KC
            return MOD[:, a:a + KC, :]

        nU = KC * UP
        U = hid[:, 0:nU].rearrange("p (c t) -> p c t", c=KC)
        CV = hid[:, nU:nU + KC * 512].rearrange("p (c t) -> p c t", c=KC)
        DIAG = sb("DIAG", [P, 4, P])

        def both(k, at):
            ap = U[:, k, at:at + T]
            return bass.AP(ap.tensor, ap.offset, [ap.ap[0], [SEG, 2], [1, T]])

        NQ = hid[:, 0:2048].rearrange("p (c t) -> p c t", c=KC)
        NK = hid[:, 2048:6144].rearrange("p (c t) -> p c t", c=KC)
        NV = [hid[:, 6144:8192].rearrange("p (s d) -> p s d", s=2),
              hid2[:, 0:2048].rearrange("p (s d) -> p s d", s=2)]
        O32 = hid2[:, 2048:4096].rearrange("p (c t) -> p c t", c=KC)
        NP = hid2[:, 4096:5120].rearrange("p (b k) -> p b k", b=2)
        MODB = cols[:, COLS["mod_b"][0]:COLS["mod_b"][0] + 288].rearrange("p (m x) -> p m x", x=2)

        landed = [sem(f"landed{s}") for s in range(RAW)]
        w_hi = sem("w_hi")
        w_lo = sem("w_lo")
        tile_used = sem("tile_used")
        params_in = sem("params_in")
        consts_in = sem("consts_in")
        x_loaded = sem("x_loaded")
        cond_in = sem("cond_in")
        cond_ready = sem("cond_ready")
        part_done = sem("part_done")
        drained = sem("drained")
        act_out = sem("act_out")
        mod_landed = [sem(f"mod_landed{n}") for n in range(2)]
        mod_acc = sem("mod_acc")
        mod_done = sem("mod_done")
        gt_ready = sem("gt_ready")
        hid_ready = sem("hid_ready")
        diag_ready = sem("diag_ready")
        taps_done = sem("taps_done")
        o_split = sem("o_split")
        sq_ready = sem("sq_ready")
        sq_used = sem("sq_used")
        sq_added = sem("sq_added")
        std_ready = sem("std_ready")
        scaled = sem("scaled")
        h_hi = sem("h_hi")
        h_lo = sem("h_lo")
        x_normed = sem("x_normed")
        v_step = sem("v_step")
        a_step = sem("a_step")
        out_sent = sem("out_sent")
        conv_out = sem("conv_out")
        gelu_out = sem("gelu_out")
        cv_ready = sem("cv_ready")
        mu_ready = sem("mu_ready")
        cv_centred = sem("cv_centred")
        cvn_ready = sem("cvn_ready")
        bias_in = [sem(f"bias_in{b}") for b in range(2)]
        bias_ready = sem("bias_ready")
        s_ready = sem("s_ready")
        s_max = sem("s_max")
        p_ready = sem("p_ready")
        dg_ready = sem("dg_ready")
        pt_ready = sem("pt_ready")
        pts_ready = sem("pts_ready")
        o_ready = sem("o_ready")
        o_out = sem("o_out")

        DG = sb("DG", [P, 2, P])
        PTS = G[:, 0:2, :].rearrange("p a b -> p (a b)").rearrange("p (k q) -> p k q", k=4)
        PTS2 = SQ[:, :, :].rearrange("p a b -> p (a b)").rearrange("p (k q) -> p k q", k=4)
        NM = sb("NM", [P, 64])
        SUM = sb("SUM", [P, 64])
        RSUM = sb("RSUM", [P, 64])

        norm_no = {n: i for i, n in enumerate(
            ("ffn0", "conv", "ln", "ffn1", "ffn2", "na", "ffn3", "final",
             "ab", "ffn4", "pg0", "e0", "nsa", "ffn5", "pg1", "e1"))}
        summed = ("conv", "ffn1", "ffn2", "na", "ffn3", "final", "ffn4", "pg0", "ffn5", "pg1")
        squares_used, squares_added = {}, {}
        used = added = 0
        for n in norm_no:
            squares_used[n], squares_added[n] = used, added
            used += 3 if n in summed else KC
            added += KC - 3 if n in summed else 0
        split_no = {n: i for i, n in enumerate(n for n in norm_no if n not in ("final", "e0", "e1"))}
        plain_no = {"final": 0, "e0": 1, "e1": 2}
        scaled_no = {n: i for i, n in enumerate(n for n in split_no if n != "ln")}

        PIN = X[:, 0:4, T:2 * T]
        EMT = hid2[:, 0:1024].rearrange("p (c t) -> p c t", c=4)
        DEN = hid2[:, 1024:1536].rearrange("p (c t) -> p c t", c=2)
        E = hid[:, KC * (T + C):KC * (T + C) + KC * T].rearrange("p (c t) -> p c t", c=KC)
        RQK = hid[:, 0:1024].rearrange("p (c t) -> p c t", c=4)
        MQK = hid[:, 1024:2048].rearrange("p (c t) -> p c t", c=4)
        RG = hid[:, 2048:3072].rearrange("p (c t) -> p c t", c=4)
        MO = hid[:, 3072:4096].rearrange("p (c t) -> p c t", c=4)
        RV = hid[:, 4096:5120].rearrange("p (s d) -> p s d", s=2)
        MV = hid[:, 5120:6144].rearrange("p (s d) -> p s d", s=2)
        MPAD = hid[:, 6144:6144 + 4 * 260].rearrange("p (c t) -> p c t", c=4)
        SW = [hid[:, 7200:7200 + 768].rearrange("p (e t) -> p e t", e=2),
              hid2[:, 4096:4096 + 768].rearrange("p (e t) -> p e t", e=2)]
        IG, XF, LROW, BROW = (hid2[:, 4096 + T * n:4096 + T * (n + 1)] for n in range(4))
        AROW, MROW = (hid2[:, 1536 + T * n:1536 + T * (n + 1)] for n in range(2))
        NMT = hid[:, 7968:7968 + T]
        ACOL = hid[:, 8224:8232]
        WT = G[:, :, :].rearrange("p a b -> p (a b)").rearrange("p (h t) -> p h t", h=4)
        ones_row = con[0:4, CONST["ones"][0]:CONST["ones"][0] + 1].to_broadcast([4, T])
        sel = const("sel").rearrange("p (h q) -> p h q", h=4)
        ab_wgate = col("ab_wgate", 0, 8 * KC).rearrange("p (k n) -> p k n", k=KC)
        gb = COLS["gate_bias"][0]
        AB_SRC = [(RQK[:, c, :], RQK[:, 2 + c, :], RV) for c in range(2)] + \
                 [(MQK[:, c, :], MQK[:, 2 + c, :], MV) for c in range(2)]
        AB_NUM, AB_DEN = (6, 1, 3, 5), (None, None, 2, 4)
        ffn_conv_w = col("ffn_conv_w", 0, 6 * FC).rearrange("p (j f o) -> p j f o", j=6, o=1)
        ffn_conv_b = col("ffn_conv_b", 0, 2 * FC).rearrange("p (j f o) -> p j f o", j=2, o=1)
        QK = hid[:, 0:2560].rearrange("p (c t) -> p c t", c=10)
        BLK = hid[:, 2560:3520].rearrange("p (m k n) -> p m k n", m=2, k=16)
        SV = hid[:, 3520:4032].rearrange("p (s d) -> p s d", s=2)
        GATE = hid[:, 4032:4128]
        HC = hid[:, 4128:4248].rearrange("p (m f n) -> p m f n", m=2, f=2)
        KCN = hid[:, 4248:4263]
        VCS = hid[:, 4264:4392]
        PC = hid[:, 4392:4904].rearrange("p (t h n) -> p t h n", t=2, h=H)
        CM = hid[:, 4904:4936].rearrange("p (t h) -> p t h", t=2)
        QG = hid[:, 4936:4937]
        PTC = hid[:, 4944:5456].rearrange("p (n q) -> p n q", n=2)
        NP2 = hid[:, 5456:6480].rearrange("p (b k) -> p b k", b=2)
        DG2 = hid[:, 6480:6992].rearrange("p (u b q) -> p u b q", u=2, b=2)
        nsa_wgate = col("nsa_wgate", 0, 48 * KC).rearrange("p (k n) -> p k n", k=KC)
        w2k = col("w2k", 0, 2 * DH).rearrange("p (f n) -> p f n", f=2)
        w2v = col("w2v", 0, 2 * DH).rearrange("p (f n) -> p f n", f=2)
        cmp_add = const("cmp_add").rearrange("p (t n) -> p t n", t=2)
        cmp_valid = const("cmp_valid").rearrange("p (t n) -> p t n", t=2)
        PSPLIT = [PBUF[n][:, :].rearrange("p (k t) -> p k t", k=2) for n in range(2)]
        BSPLIT = BBUF[:, :].rearrange("p (m k s n) -> p m k s n", m=2, k=16, s=2)
        p_loaded = sem("p_loaded")
        p_hi = sem("p_hi")
        p_split = sem("p_split")
        blk_hi = sem("blk_hi")
        blk_split = sem("blk_split")
        hid_hi = sem("hid_hi")
        o_hi = sem("o_hi")
        gate_step = sem("gate_step")
        ab_scores = sem("ab_scores")
        ab_weighted = sem("ab_weighted")
        ab_values = sem("ab_values")
        ab_divided = sem("ab_divided")
        ab_squares = sem("ab_squares")
        ab_mean = sem("ab_mean")
        ab_root = sem("ab_root")
        ab_out = sem("ab_out")
        nsa_step = sem("nsa_step")
        rotated = sem("rotated")
        rope_done = sem("rope_done")
        mconv_ready = sem("mconv_ready")
        mqk_ready = sem("mqk_ready")
        rg_ready = sem("rg_ready")
        mo_ready = sem("mo_ready")
        tap_out = sem("tap_out")
        qsq_ready = sem("qsq_ready")
        qmean_ready = sem("qmean_ready")
        qstd_ready = sem("qstd_ready")
        qn_ready = sem("qn_ready")
        ngate_ready = sem("ngate_ready")
        pc_exp = sem("pc_exp")
        ns_ready = sem("ns_ready")
        ns_max = sem("ns_max")
        np_ready = sem("np_ready")
        ndg_ready = sem("ndg_ready")
        npt_ready = sem("npt_ready")
        npts_ready = sem("npts_ready")
        no_ready = sem("no_ready")
        no_out = sem("no_out")

        block = ctx.enter_context(nc.Block())

        @block.sync
        def _(sp):
            sp.dma_start(CB[:, :, :], bass.AP(cond.tensor, cond.offset, [[0, P], [1, 2 * D]])
                         .rearrange("p (s d) -> p s d", s=2)).then_inc(cond_in, 16)
            sp.dma_start(cols[:, :], params).then_inc(params_in, 16)
            sp.dma_start(con[:, :], consts).then_inc(consts_in, 16)
            sp.dma_start(X[:, :, :], x_in).then_inc(x_loaded, 16)

            def load(n, i=0, first=False):
                slot = n % RAW
                if not first:
                    sp.wait_ge(w_lo, n - RAW + 1 + RAW * i)
                sp.dma_start(raw[slot][:, :], weights[n + RAW * i, :, :]).then_inc(landed[slot], 16)

            sp.wait_ge(mod_acc, 4)
            for n in range(RAW):
                load(n, first=True)
            laps = (NTILES - RAW) // RAW
            with sp.Fori(0, laps) as i:
                for n in range(RAW):
                    load(RAW + n, i)
            for n in range(RAW * (laps + 1), NTILES):
                load(n)

            sp.wait_ge(drained, NJOBS)
            sp.dma_start(out, X[:, :, 0:T]).then_inc(out_sent, 16)
            sp.wait_ge(out_sent, 16)

        def pair_banks(pair):
            return bank[2 + 2 * (pair % 3)], bank[3 + 2 * (pair % 3)]

        @block.tensor
        def _(pe):
            def tiles(w, i=0):
                pe.wait_ge(w_lo, w + 2 + BODY * i)
                return [(wh[t % SPLIT][:, :].rearrange("p (k n) -> p k n", k=KC),
                         wl[t % SPLIT][:, :].rearrange("p (k n) -> p k n", k=KC)) for t in (w, w + 1)]

            def banks_free(j, i=0):
                if j >= 2:
                    pe.wait_ge(drained, j - 1 + GJ * i)

            def job(j, w, n, src=None, ks=KC, norm=None, hidden=None, i=0):
                W = tiles(w, i)
                banks_free(j, i)
                xh, xl = src or (HNH, HNL)
                ps = pair_banks(j)
                for k in range(ks):
                    if norm is not None:
                        pe.wait_ge(h_hi, KC * split_no[norm] + k + 1)
                    if hidden is not None:
                        pe.wait_ge(hid_ready, hidden + k + 1 + GROUP * i)
                    for f in range(2):
                        for part in range(2):
                            nc.tensor.matmul(ps[f][:, 0:n], W[f][part][:, k, :], xh[:, k, 0:n],
                                             start=(k == 0 and part == 0), stop=False)
                for k in range(ks):
                    if norm is not None:
                        pe.wait_ge(h_lo, KC * split_no[norm] + k + 1)
                    for f in range(2):
                        mm = nc.tensor.matmul(ps[f][:, 0:n], W[f][0][:, k, :], xl[:, k, 0:n],
                                              start=False, stop=(k == ks - 1))
                        if k == ks - 1:
                            mm.then_inc(tile_used, 1)

            def token_job(j, w, n):
                W = [[part.rearrange("p (k m) n -> p k (m n)", k=4) for part in t] for t in tiles(w)]
                banks_free(j)
                for s in range(n):
                    ps = pair_banks(j)[s // 2][:, (s % 2) * 2 * P:(s % 2 + 1) * 2 * P]
                    t = slice(s * P, (s + 1) * P)
                    for k in range(KC):
                        for a, b in ((HNH, 0), (HNH, 1), (HNL, 0)):
                            mm = nc.tensor.matmul(ps, a[:, k, t], W[k // 4][b][:, k % 4, :],
                                                  start=(k == 0 and (a, b) == (HNH, 0)),
                                                  stop=(k == KC - 1 and a is HNL))
                mm.then_inc(tile_used, 2)

            def ffn(name, n):
                S = STAGES[name]
                with pe.Fori(0, 2) as i:
                    for k in range(GROUP):
                        job(S.j + k, S.w + 2 * k, n, norm=name, i=i)
                    for k in range(4):
                        job(S.j + GROUP + k, S.w + 2 * (GROUP + k), n, (HDH, HDL), hidden=S.q, i=i)
                j, w = S.j + 2 * GJ, S.w + 2 * BODY
                for k in range(LAST):
                    job(j + k, w + 2 * k, n)
                for k in range(4):
                    job(j + LAST + k, w + 2 * (LAST + k), n, (HDH, HDL), ks=LAST, hidden=S.q + 2 * GROUP)

            def stats(name, n):
                first = 0
                if name in summed:
                    first = KC - 2
                    pe.wait_ge(sq_added, squares_added[name] + KC - 3)
                    nc.tensor.matmul(bank[0][:, 0:n], const("mean_all"), STD[:, 0:n],
                                     start=True, stop=False).then_inc(sq_used, 1)
                for c in range(first, KC):
                    pe.wait_ge(sq_ready, KC * norm_no[name] + c + 1)
                    nc.tensor.matmul(bank[0][:, 0:n], const("mean_all"), SQ[:, c % 2, 0:n],
                                     start=(c == 0), stop=(c == KC - 1)).then_inc(sq_used, 1)

            def per_layer(i):
                S = STAGES[f"ple_e{i}"]
                W = tiles(S.w)
                pe.wait_ge(p_split, i + 1)
                for j in range(4):
                    banks_free(S.j + j)
                    for f, ps in enumerate(pair_banks(S.j + j)):
                        for k in range(2):
                            at = 2 * (j % 2) + f
                            wk = [W[j // 2][b][:, :, :].rearrange("p (k c) n -> p k c n", k=2)[:, k, at, :]
                                  for b in range(2)]
                            for a, b in ((0, 0), (0, 1), (1, 0)):
                                mm = nc.tensor.matmul(ps[:, 0:T], wk[b], PSPLIT[a][:, k, :],
                                                      start=(k == 0 and (a, b) == (0, 0)),
                                                      stop=(k == 1 and a == 1))
                    mm.then_inc(part_done if j % 2 == 0 else tile_used, 1)
                stats(f"pg{i}", T)
                S = STAGES[f"ple_g{i}"]
                for k in range(4):
                    job(S.j + k, S.w + 2 * k, T, norm=f"pg{i}")
                    if k == 0:
                        stats(f"e{i}", T)

            pe.wait_ge(consts_in, 16)
            stats("ffn0", T + C)
            ffn("ffn0", T + C)
            stats("conv", T + C)
            S = STAGES["pw1"]
            for k in range(9):
                if k < 8:
                    job(S.j + k, S.w + 2 * k, T + C, norm="conv")
                if k >= 1:
                    c = k - 1
                    pe.wait_ge(drained, S.j + c + 1)
                    if c >= 2:
                        pe.wait_ge(cv_ready, c - 1)
                    for tap in range(TAPS_PE):
                        d = c * TAPS_PE + tap
                        pe.wait_ge(diag_ready, d + 1)
                        nc.tensor.matmul(bank[c % 2][:, :], DIAG[:, d % 4, :], both(c, TAPS - TAPS_PE + tap),
                                         start=(tap == 0), stop=(tap == TAPS_PE - 1)).then_inc(taps_done, 1)
            for c in range(KC):
                pe.wait_ge(cv_ready, c + 1)
                mm = nc.tensor.matmul(pair_banks(S.j + KC)[0][:, :], const("mean_all"), CV[:, c, :],
                                      start=(c == 0), stop=(c == KC - 1))
            mm.then_inc(mu_ready, 1)
            stats("ln", T + C)
            S = STAGES["pw2"]
            for k in range(4):
                job(S.j + k, S.w + 2 * k, T + C, norm="ln")
            stats("ffn1", T + C)
            ffn("ffn1", T + C)
            stats("ffn2", T + C)
            ffn("ffn2", T + C)
            stats("na", T + C)
            S = STAGES["na_qk"]
            for k in range(8):
                job(S.j + k, S.w + 2 * k, T if k < 4 else T + C, norm="na")
            S = STAGES["na_v"]
            for k in range(4):
                token_job(S.j + k, S.w + 2 * k, 4)
            pe.wait_ge(drained, STAGES["na_o"].j)

            def scores(u):
                h, t = u // 2, u % 2
                r = DH * (h % 2)
                if u >= 4:
                    pe.wait_ge(p_ready, u - 3)
                nc.tensor.matmul(bank[u % 4][:, :], NQ[r:r + DH, h // 2, t * P:(t + 1) * P],
                                 NK[r:r + DH, h // 2, :], start=True, stop=True).then_inc(s_ready, 1)

            def transposed(u):
                pe.wait_ge(dg_ready, u + 1)
                if u >= 2:
                    pe.wait_ge(pts_ready, u - 1)
                for k in range(4):
                    mm = nc.tensor.matmul(bank[4 + u % 2][:, k * P:(k + 1) * P],
                                          NP[:, u % 2, k * P:(k + 1) * P], DG[:, u % 2, :],
                                          start=True, stop=True)
                mm.then_inc(pt_ready, 1)

            def outputs(h):
                r = DH * (h % 2)
                pe.wait_ge(pts_ready, 2 * h + 2)
                if h >= 2:
                    pe.wait_ge(o_out, h - 1)
                pt = (PTS, PTS2)[h % 2]
                for k in range(4):
                    mm = nc.tensor.matmul(bank[6 + h % 2][r:r + DH, 0:T], NV[k // 2][:, k % 2, h * DH:(h + 1) * DH],
                                          pt[:, k, :], start=(k == 0), stop=(k == 3))
                mm.then_inc(o_ready, 1)

            for u in range(2 * H + 4):
                if u < 2 * H:
                    scores(u)
                if 2 <= u <= 2 * H + 1:
                    transposed(u - 2)
                if u >= 5 and u % 2 == 1:
                    outputs((u - 5) // 2)
            S = STAGES["na_o"]
            pe.wait_ge(o_split, KC)
            for k in range(4):
                job(S.j + k, S.w + 2 * k, T)
            stats("ffn3", T)
            ffn("ffn3", T)
            stats("final", T)

            stats("ab", T)
            S = STAGES["ab_in"]
            for k in range(KC):
                pe.wait_ge(scaled, KC * scaled_no["ab"] + k + 1)
                for b in range(2):
                    mm = nc.tensor.matmul(bank[2 + b][0:4, 0:T], ab_wgate[:, k, 4 * b:4 * b + 4],
                                          H32[:, k, 0:T], start=(k == 0), stop=(k == KC - 1))
            mm.then_inc(gate_step, 1)
            pe.wait_ge(gate_step, 2)
            for k in range(12):
                if k in (2, 3, 8, 9):
                    token_job(S.j + k, S.w + 2 * k, 2)
                else:
                    job(S.j + k, S.w + 2 * k, T, norm="ab")
                if k == 3:
                    pe.wait_ge(drained, S.j + 2)
                    for c in range(4):
                        nc.tensor.matmul(bank[c // 2][:, (c % 2) * T:(c % 2 + 1) * T], const("rot"), RQK[:, c, :],
                                         start=True, stop=True).then_inc(rotated, 1)
            pe.wait_ge(drained, S.j + 12)
            pe.wait_ge(gate_step, 4)
            pe.wait_ge(rope_done, 4)
            for s in range(2):
                nc.tensor.matmul(bank[0][:, 4 * s:4 * s + 4], AROW[0:4, s * P:(s + 1) * P], con[0:4, 0:4],
                                 start=True, stop=True)
            for h in range(4):
                nc.tensor.matmul(bank[2 + h // 2][:, (h % 2) * T:(h % 2 + 1) * T], sel[0:4, h, :],
                                 MROW[0:4, :], start=True, stop=True)
            for h in range(4):
                mm = nc.tensor.matmul(bank[4 + h // 2][:, (h % 2) * T:(h % 2 + 1) * T], sel[0:4, h, :],
                                      NMT[0:4, :], start=True, stop=True)
            mm.then_inc(gate_step, 1)
            pe.wait_ge(gate_step, 7)
            pe.wait_ge(mqk_ready, 4)

            def pair_scores(pr):
                q, k, v = AB_SRC[pr]
                if pr >= 2:
                    pe.wait_ge(ab_weighted, pr - 1)
                for e in range(2):
                    r = slice(DH * e, DH * e + DH)
                    ps = bank[2 + 2 * (pr % 2) + e]
                    nc.tensor.matmul(ps[:, 0:T], k[r, 0:P], q[r, :], start=True, stop=True)
                    mm = nc.tensor.matmul(ps[:, T:T + P], k[r, P:T], q[r, P:T], start=True, stop=True)
                mm.then_inc(ab_scores, 1)

            def pair_values(pr):
                q, k, v = AB_SRC[pr]
                pe.wait_ge(ab_weighted, pr + 1)
                for e in range(2):
                    h = 2 * (pr % 2) + e
                    sums = [(bank[AB_NUM[pr]], v[:, 0, h * P:(h + 1) * P], v[:, 1, h * P:(h + 1) * P])]
                    if pr >= 2:
                        sums.append((bank[AB_DEN[pr]], const("ones"), const("ones")))
                    for ps, w0, w1 in sums:
                        nc.tensor.matmul(ps[:, e * T:(e + 1) * T], w0, SW[pr % 2][:, e, 0:T],
                                         start=True, stop=False)
                        mm = nc.tensor.matmul(ps[:, e * T + P:(e + 1) * T], w1, SW[pr % 2][:, e, T:T + P],
                                              start=False, stop=True)
                mm.then_inc(ab_values, 1)

            def pair_mean(pr):
                pe.wait_ge(ab_squares, pr + 1)
                if pr >= 1:
                    pe.wait_ge(ab_root, pr)
                nc.tensor.matmul(bank[0][:, :], const("mean128"), SQ[:, pr % 2, :], start=True, stop=True)\
                    .then_inc(ab_mean, 1)

            pair_scores(0)
            pair_scores(1)
            for pr in range(5):
                if pr < 4:
                    pair_values(pr)
                if pr < 2:
                    pair_scores(pr + 2)
                if pr >= 1:
                    pair_mean(pr - 1)
            S = STAGES["ab_out"]
            pe.wait_ge(o_split, 2 * KC)
            for k in range(4):
                job(S.j + k, S.w + 2 * k, T)
            stats("ffn4", T)
            ffn("ffn4", T)
            per_layer(0)
            stats("nsa", T)
            S = STAGES["nsa_in"]
            pe.wait_ge(scaled, KC * (scaled_no["nsa"] + 1))
            for s in range(2):
                for k in range(KC):
                    mm = nc.tensor.matmul(bank[0][:, s * 48:(s + 1) * 48], H32[:, k, s * P:(s + 1) * P],
                                          nsa_wgate[:, k, :], start=(k == 0), stop=(k == KC - 1))
            mm.then_inc(nsa_step, 1)
            for k in range(7):
                job(S.j + k, S.w + 2 * k, T, norm="nsa")
            token_job(S.j + 7, S.w + 14, 2)
            S = STAGES["nsa_mlp"]

            def compress(m, t):
                if t == 0:
                    banks_free(S.j + m)
                W = tiles(S.w + 4 * m + 2 * t)
                for f, ps in enumerate(pair_banks(S.j + m)):
                    for k in range(KC):
                        x = BSPLIT[:, m, 8 * t + k, :, :]
                        nc.tensor.matmul(ps[:, 0:60], W[f][0][:, k, :], x.rearrange("p s n -> p (s n)"),
                                         start=(t == 0 and k == 0), stop=False)
                        mm = nc.tensor.matmul(ps[:, 0:30], W[f][1][:, k, :], x[:, 0, :],
                                              start=False, stop=(t == 1 and k == KC - 1))
                    mm.then_inc(tile_used, 1)

            for n in range(5):
                pe.wait_ge(qsq_ready, n + 1)
                if n >= 1:
                    pe.wait_ge(qstd_ready, n)
                nc.tensor.matmul(bank[1][:, :], const("mean64"), SQ[:, n % 2, :], start=True, stop=True)\
                    .then_inc(qmean_ready, 1)
                if n == 0:
                    pe.wait_ge(blk_split, 1)
                if n < 4:
                    compress(n // 2, n % 2)
            pe.wait_ge(nsa_step, 3)
            for g in range(2):
                for f in range(2):
                    nc.tensor.matmul(bank[1][g * DH:(g + 1) * DH, 0:15], w2k[:, f, :],
                                     HC[:, 0, f, g * 15:(g + 1) * 15], start=(f == 0), stop=(f == 1))
            for g in range(2):
                for f in range(2):
                    mm = nc.tensor.matmul(bank[0][0:15, g * DH:(g + 1) * DH], HC[:, 1, f, g * 15:(g + 1) * 15],
                                          w2v[:, f, :], start=(f == 0), stop=(f == 1))
            mm.then_inc(nsa_step, 1)
            pe.wait_ge(nsa_step, 5)
            nc.tensor.matmul(bank[2][:, 0:15], const("mean64"), SQ[:, 0, 0:15], start=True, stop=True)\
                .then_inc(nsa_step, 1)
            pe.wait_ge(nsa_step, 8)
            for t in range(2):
                for h in range(H):
                    r = DH * (h // 8)
                    mm = nc.tensor.matmul(bank[2 + 2 * t + h // 8][:, 16 * (h % 8):16 * (h % 8) + 15],
                                          QK[r:r + DH, h % 8, t * P:(t + 1) * P], KCN[r:r + DH, :],
                                          start=True, stop=True)
            mm.then_inc(nsa_step, 1)

            def nsa_scores(u):
                c, g, t = u // 4, u // 2 % 2, u % 2
                r, n = DH * g, P * (t + 1)
                if u >= 3:
                    pe.wait_ge(np_ready, u - 2)
                for b in range(2):
                    mm = nc.tensor.matmul(bank[u % 3][:, b * n:(b + 1) * n],
                                          QK[r:r + DH, c, t * P:(t + 1) * P], QK[r:r + DH, 8 + b, 0:n],
                                          start=True, stop=True)
                mm.then_inc(ns_ready, 1)

            def nsa_transposed(u):
                h, t = u // 4 + 8 * (u // 2 % 2), u % 2
                pe.wait_ge(ndg_ready, u + 1)
                if u >= 2:
                    pe.wait_ge(npts_ready, u - 1)
                ps = bank[3 + u % 2]
                for b in range(2):
                    for k in range(t + 1):
                        n = b * (t + 1) + k
                        mm = nc.tensor.matmul(ps[:, n * P:(n + 1) * P], NP2[:, u % 2, n * P:(n + 1) * P],
                                              DG2[:, u % 2, b, :], start=True, stop=True)
                if t == 0:
                    for s in range(2):
                        mm = nc.tensor.matmul(ps[0:15, (2 + s) * P:(3 + s) * P], PC[:, s, h, 0:15],
                                              const("ident"), start=True, stop=True)
                mm.then_inc(npt_ready, 1)

            def nsa_outputs(n):
                g = n % 2
                r = DH * g
                pe.wait_ge(npts_ready, 2 * n + 2)
                if n >= 2:
                    pe.wait_ge(no_out, n - 1)
                ps = bank[6 + n % 2]
                pt = (PTS, PTS2)[n % 2]
                nc.tensor.matmul(ps[r:r + DH, 0:T], VCS[0:15, g * DH:(g + 1) * DH], PTC[0:15, n % 2, :],
                                 start=True, stop=False)
                for b in range(2):
                    v = SV[:, :, 2 * b * DH + g * DH:2 * b * DH + (g + 1) * DH]
                    nc.tensor.matmul(ps[r:r + DH, 0:T], v[:, 0, :], pt[:, 2 * b, :], start=False, stop=False)
                    mm = nc.tensor.matmul(ps[r:r + DH, P:T], v[:, 1, :], pt[:, 2 * b + 1, P:T],
                                          start=False, stop=(b == 1))
                mm.then_inc(no_ready, 1)

            pe.wait_ge(nsa_step, 11)
            for u in range(2 * H + 4):
                if u < 2 * H:
                    nsa_scores(u)
                if 2 <= u <= 2 * H + 1:
                    nsa_transposed(u - 2)
                if u >= 5 and u % 2 == 1:
                    nsa_outputs((u - 5) // 2)
            S = STAGES["nsa_out"]
            pe.wait_ge(o_split, 3 * KC)
            for k in range(4):
                job(S.j + k, S.w + 2 * k, T)
            stats("ffn5", T)
            ffn("ffn5", T)
            per_layer(1)

        @block.scalar
        def _(act):
            chain = [0]

            def link(ins):
                chain[0] += 1
                ins.then_inc(a_step, 1)
                act.wait_ge(a_step, chain[0])

            def hi(t, i=0):
                if t < NTILES:
                    act.wait_ge(landed[t % RAW], 16 * (t // RAW + 1) + 16 * (BODY // RAW) * i)
                    nc.scalar.activation(wh[t % SPLIT][:, :], raw[t % RAW][:, :], ACT.Copy).then_inc(w_hi, 1)

            def feed(w, i=0):
                if w > 0:
                    act.wait_ge(tile_used, w + BODY * i)
                hi(w + 2, i)
                hi(w + 3, i)

            def load_mod(m, i=0):
                if m >= 2:
                    act.wait_ge(mod_acc, m - 1 + 2 * GROUP * i)
                act.dma_start(mod_ring[:, m % 2, :], mod_w[m + 2 * GROUP * i, :, :])\
                    .then_inc(mod_landed[m % 2], 16)

            def squares(name, n, c, ready, src=X):
                m = norm_no[name]
                ready(c)
                if name in summed:
                    act.wait_ge(*((sq_used, squares_used[name]) if c < 2 else
                                  (sq_added, squares_added[name] + max(c - 2, 1))))
                elif m > 0 or c >= 2:
                    act.wait_ge(sq_used, squares_used[name] + c - 1)
                nc.scalar.activation(SQ[:, c % 2, 0:n], src[:, c, 0:n], ACT.Square).then_inc(sq_ready, 1)

            def warm_root(name):
                m = norm_no[name]
                nc.scalar.activation(warm[:, m:m + 1], const("one"), ACT.Sqrt)

            def last_jobs(name, n, w, ready, first=0):
                for k in range(first, 4):
                    feed(w + 2 * k)
                    if k == 1:
                        warm_root(name)
                    if k >= 1:
                        squares(name, n, 2 * k - 2, ready)
                        squares(name, n, 2 * k - 1, ready)

            def norm(name, n, ready, shift=None, src=X, eps="eps6", meanwhile=None):
                if name not in summed:
                    warm_root(name)
                for c in range(KC - 2 if name in summed else 0, KC):
                    squares(name, n, c, ready, src)
                if meanwhile is not None:
                    meanwhile()
                act.wait_ge(sq_used, squares_used[name] + (3 if name in summed else KC))
                nc.scalar.activation(STD[:, 0:n], bank[0][:, 0:n], ACT.Sqrt, bias=const(eps))\
                    .then_inc(std_ready, 1)
                if name in scaled_no:
                    for c in range(KC):
                        act.wait_ge(scaled, KC * scaled_no[name] + c + 1)
                        if shift is None:
                            ins = nc.scalar.activation(HNH[:, c, 0:n], H32[:, c, 0:n], ACT.Copy)
                        else:
                            for s in range(n // T):
                                t = slice(s * T, (s + 1) * T)
                                ins = nc.scalar.activation(HNH[:, c, t], H32[:, c, t], ACT.Identity,
                                                           bias=shift[:, c, s:s + 1])
                        ins.then_inc(h_hi, 1)

            def x_from(name, per=1):
                return lambda c: act.wait_ge(drained, STAGES[name].j + c // per + 1)

            def after(name):
                return lambda c: act.wait_ge(drained, STAGES[name].j + FFN_JOBS - 4 + c // 2 + 1)

            def ffn(name, n, mods=None, causal=None, then=None):
                S = STAGES[name]

                def group(j, w, a, q, m, chunks, f0, i=0, last=False, units=2 * GROUP):
                    for k in range(chunks):
                        if m is not None and 2 * k < units:
                            load_mod(m + 2 * k, i)
                            load_mod(m + 2 * k + 1, i)
                        act.wait_ge(tile_used, w + 2 * k + 2 + BODY * i)
                        if q + k >= 2:
                            act.wait_ge(hid_ready, q + k - 1 + GROUP * i)
                        g = (j + k) % 3
                        src = pair_banks(j + k)[0][:, 0:n]
                        if causal is None:
                            nc.scalar.activation(G[:, g, 0:n], src, ACT.Silu).then_inc(act_out, 1)
                        else:
                            f = f0 + k + GROUP * i
                            c = FC * causal + f0 + k + 1
                            nc.scalar.activation(G[:, g, 0:T], src, ACT.Identity,
                                                 scale=ffn_conv_w[:, 3 * causal + 2, f],
                                                 bias=ffn_conv_b[:, causal, f]).then_inc(act_out, 1)
                            act.wait_ge(conv_out, c + GROUP * i)
                            nc.scalar.activation(G[:, g, T:2 * T], G[:, g, 0:T], ACT.Gelu_apprx_tanh)\
                                .then_inc(gelu_out, 1)
                        feed(w + 2 * (k + 1), i)
                    if last and then is not None:
                        last_jobs(then, n, w + 2 * chunks, after(name), 1)
                    else:
                        for k in range(1, 4 if last else 5):
                            feed(w + 2 * (chunks + k), i)

                feed(S.w)
                with act.Fori(0, 2) as i:
                    group(S.j, S.w, S.a, S.q, S.m if mods is not None else None, GROUP, 0, i)
                group(S.j + 2 * GJ, S.w + 2 * BODY, S.a + 2 * GROUP, S.q + 2 * GROUP,
                      S.m + 4 * GROUP if mods else None, LAST, 2 * GROUP, last=True, units=mods)

            def feeds(name, jobs):
                for k in range(jobs):
                    feed(STAGES[name].w + 2 * k)

            def split_embedding(i):
                act.wait_ge(p_loaded, 16)
                nc.scalar.activation(PSPLIT[0], PIN[:, 2 * i:2 * i + 2, :], ACT.Copy).then_inc(p_hi, 1)

            def per_layer(i):
                norm(f"pg{i}", T, after(f"ffn{4 + i}"), meanwhile=lambda: feed(STAGES[f"ple_e{i}"].w))
                S = STAGES[f"ple_g{i}"]
                feed(S.w)
                norm(f"e{i}", T, x_from(f"ple_e{i}", 2), src=E)
                for k in range(4):
                    if k >= 1:
                        feed(S.w + 2 * k)
                    act.wait_ge(tile_used, S.w + 2 * k + 2)
                    act.wait_ge(drained, S.j + k - 1)
                    a, b = pair_banks(S.j + k)
                    g = (S.j + k) % 3
                    nc.scalar.activation(G[:, g, 0:T], a[:, 0:T], ACT.Sigmoid)
                    nc.scalar.activation(G[:, g, T:2 * T], b[:, 0:T], ACT.Sigmoid).then_inc(act_out, 1)

            def split_output(c, ready):
                act.wait_ge(*ready)
                nc.scalar.activation(HNH[:, c, 0:T], O32[:, c, :], ACT.Copy).then_inc(o_hi, 1)

            load_mod(0)
            load_mod(1)
            act.wait_ge(params_in, 16)
            act.wait_ge(cond_in, 16)
            nc.scalar.activation(CB[:, :, :], CB[:, :, :], ACT.Silu).then_inc(cond_ready, 1)
            for m in range(2, 8):
                load_mod(m)
            act.wait_ge(consts_in, 16)
            hi(0)
            hi(1)
            norm("ffn0", T + C, lambda c: (act.wait_ge(x_loaded, 16), load_mod(8 + c)), mod(0, 0))
            ffn("ffn0", T + C, 12, then="conv")
            norm("conv", T + C, after("ffn0"), mod(0, 3))
            S = STAGES["pw1"]
            for k in range(8):
                feed(S.w + 2 * k)
                if k < 4:
                    load_mod(S.m + k)
                act.wait_ge(tile_used, S.w + 2 * k + 2)
                act.wait_ge(drained, S.j + k - 1)
                g = (S.j + k) % 3
                nc.scalar.activation(G[:, g, :], pair_banks(S.j + k)[1][:, :], ACT.Sigmoid,
                                     bias=col("b_pw1", KC + k)).then_inc(act_out, 1)
            norm("ln", T + C, lambda c: act.wait_ge(cv_centred, c + 1), src=CV, eps="eps5")
            for c in range(KC):
                act.wait_ge(cvn_ready, c + 1)
                link(nc.scalar.activation(CV[:, c, :], CV[:, c, :], ACT.Silu, scale=col("ln_g", c),
                                          bias=col("ln_b", c)))
                nc.scalar.activation(HNH[:, c, :], CV[:, c, :], ACT.Copy).then_inc(h_hi, 1)
            last_jobs("ffn1", T + C, STAGES["pw2"].w, x_from("pw2", 2))
            norm("ffn1", T + C, x_from("pw2", 2), mod(0, 6))
            ffn("ffn1", T + C, 12, then="ffn2")
            norm("ffn2", T + C, after("ffn1"), mod(1, 0))
            ffn("ffn2", T + C, 4, then="na")
            norm("na", T + C, after("ffn2"), mod(1, 3))
            feeds("na_qk", 8)
            feeds("na_v", 4)

            def exponentials(u):
                act.wait_ge(s_max, u + 1)
                if u >= 2:
                    act.wait_ge(pt_ready, u - 1)
                nc.scalar.activation(NP[:, u % 2, :], bank[u % 4][:, :], ACT.Exp, bias=NM[:, u:u + 1],
                                     accum_out=SUM[:, u:u + 1]).then_inc(p_ready, 1)

            def copy_transposed(u):
                h, t = u // 2, u % 2
                act.wait_ge(pt_ready, u + 1)
                if h >= 2:
                    act.wait_ge(o_ready, h - 1)
                nc.scalar.activation((PTS, PTS2)[h % 2][:, :, t * P:(t + 1) * P],
                                     bank[4 + u % 2][:, :].rearrange("p (k q) -> p k q", k=4),
                                     ACT.Copy).then_inc(pts_ready, 1)

            for u in range(2 * H + 6):
                if u < 2 * H:
                    exponentials(u)
                if 2 <= u <= 2 * H + 1:
                    copy_transposed(u - 2)
                if u >= 9 and u % 4 == 1:
                    c = (u - 9) // 4
                    split_output(c, (o_out, 2 * c + 2))
            last_jobs("ffn3", T, STAGES["na_o"].w, x_from("na_o", 2))
            norm("ffn3", T, x_from("na_o", 2), mod(1, 6))
            ffn("ffn3", T, then="final")
            norm("final", T, after("ffn3"))

            norm("ab", T, lambda c: act.wait_ge(x_normed, c + 1))
            S = STAGES["ab_in"]
            feed(S.w)
            act.wait_ge(gate_step, 2)
            link(nc.scalar.activation(LROW[0:4, :], XF[0:4, :], ACT.Abs))
            link(nc.scalar.activation(LROW[0:4, :], LROW[0:4, :], ACT.Exp, scale=-1.0))
            nc.scalar.activation(LROW[0:4, :], LROW[0:4, :], ACT.Ln, bias=con[0:4, CONST["one"][0]:CONST["one"][0] + 1])\
                .then_inc(gate_step, 1)
            for k in range(1, 12):
                feed(S.w + 2 * k)
            act.wait_ge(drained, S.j + 6)
            nc.scalar.activation(RG[:, :, :], RG[:, :, :], ACT.Silu).then_inc(rg_ready, 1)
            act.wait_ge(drained, S.j + 12)
            nc.scalar.activation(MO[:, :, :], MO[:, :, :], ACT.Sigmoid).then_inc(mo_ready, 1)
            for c in range(4):
                act.wait_ge(mconv_ready, c + 1)
                nc.scalar.activation(MQK[:, c, :], MQK[:, c, :], ACT.Silu).then_inc(mqk_ready, 1)
            act.wait_ge(gate_step, 6)
            for h in range(4):
                nc.scalar.activation(WT[:, h, 0:T], WT[:, h, 0:T], ACT.Exp, bias=ACOL[:, h:h + 1])
                nc.scalar.activation(WT[:, h, T:T + P], WT[:, h, T:T + P], ACT.Exp, bias=ACOL[:, 4 + h:5 + h])
            for b in range(2):
                ins = nc.scalar.activation(EMT[:, 2 * b:2 * b + 2, :],
                                           bank[4 + b][:, :].rearrange("p (e t) -> p e t", e=2), ACT.Exp)
            ins.then_inc(gate_step, 1)
            for pr in range(6):
                if pr < 4:
                    act.wait_ge(*((ab_values, pr + 1) if pr < 2 else (ab_divided, pr - 1)))
                    nc.scalar.activation(SQ[:, pr % 2, :], bank[AB_NUM[pr]][:, :], ACT.Square)\
                        .then_inc(ab_squares, 1)
                if 1 <= pr < 5:
                    act.wait_ge(ab_mean, pr)
                    if pr >= 2:
                        act.wait_ge(ab_out, pr - 1)
                    nc.scalar.activation(STD[:, :], bank[0][:, :], ACT.Sqrt, bias=const("eps6"))\
                        .then_inc(ab_root, 1)
                if pr >= 2:
                    for e in range(2):
                        split_output(2 * (pr - 2) + e, (ab_out, pr - 1))
            split_embedding(0)
            last_jobs("ffn4", T, STAGES["ab_out"].w, x_from("ab_out", 2))
            norm("ffn4", T, x_from("ab_out", 2))
            ffn("ffn4", T, causal=0, then="pg0")
            per_layer(0)
            norm("nsa", T, x_from("ple_g0", 2))
            for k in range(8):
                feed(STAGES["nsa_in"].w + 2 * k)
            act.wait_ge(drained, STAGES["nsa_in"].j + 6)
            nc.scalar.activation(BSPLIT[:, :, :, 0, :], BLK[:, :, :, :], ACT.Copy).then_inc(blk_hi, 1)
            for n in range(5):
                act.wait_ge(drained, STAGES["nsa_in"].j + (n + 1 if n < 4 else 7))
                if n >= 2:
                    act.wait_ge(qmean_ready, n - 1)
                nc.scalar.activation(SQ[:, n % 2, :], QK[:, 2 * n:2 * n + 2, :].rearrange("p c t -> p (c t)"),
                                     ACT.Square).then_inc(qsq_ready, 1)
                act.wait_ge(qmean_ready, n + 1)
                if n >= 1:
                    act.wait_ge(qn_ready, n)
                nc.scalar.activation(STD[:, :], bank[1][:, :], ACT.Sqrt, bias=const("eps6"))\
                    .then_inc(qstd_ready, 1)
                if n < 4:
                    feed(STAGES["nsa_mlp"].w + 2 * n)
            act.wait_ge(nsa_step, 2)
            nc.scalar.activation(GATE[:, :], GATE[:, :], ACT.Sigmoid).then_inc(ngate_ready, 1)
            act.wait_ge(drained, STAGES["nsa_out"].j)
            nc.scalar.activation(HC[:, :, :, :].rearrange("p a f n -> p (a f n)"),
                                 HC[:, :, :, :].rearrange("p a f n -> p (a f n)"), ACT.Gelu_apprx_tanh)\
                .then_inc(nsa_step, 1)
            act.wait_ge(nsa_step, 4)
            nc.scalar.activation(SQ[:, 0, 0:15], bank[1][:, 0:15], ACT.Square).then_inc(nsa_step, 1)
            act.wait_ge(nsa_step, 6)
            nc.scalar.activation(STD[:, 0:15], bank[2][:, 0:15], ACT.Sqrt, bias=const("eps6"))\
                .then_inc(nsa_step, 1)
            act.wait_ge(nsa_step, 10)
            nc.scalar.activation(PC[:, :, :, 0:15], PC[:, :, :, 0:15], ACT.Exp).then_inc(pc_exp, 1)

            def nsa_exponentials(u):
                n = P * (u % 2 + 1)
                act.wait_ge(ns_max, u + 1)
                if u >= 2:
                    act.wait_ge(npt_ready, u - 1)
                for b in range(2):
                    ins = nc.scalar.activation(NP2[:, u % 2, b * n:(b + 1) * n], bank[u % 3][:, b * n:(b + 1) * n],
                                               ACT.Exp, bias=NM[:, 2 * u + b:2 * u + b + 1],
                                               accum_out=SUM[:, 2 * u + b:2 * u + b + 1])
                ins.then_inc(np_ready, 1)

            def nsa_copy_transposed(u):
                n, t = u // 2, u % 2
                act.wait_ge(npt_ready, u + 1)
                if n >= 2:
                    act.wait_ge(no_ready, n - 1)
                pt = (PTS, PTS2)[n % 2]
                ps = bank[3 + u % 2]
                if t == 0:
                    nc.scalar.activation(pt[:, 0:4:2, 0:P], ps[:, 0:2 * P].rearrange("p (b q) -> p b q", b=2),
                                         ACT.Copy)
                    nc.scalar.activation(PTC[0:15, n % 2, :], ps[0:15, 2 * P:4 * P], ACT.Copy)\
                        .then_inc(npts_ready, 1)
                else:
                    nc.scalar.activation(pt[:, :, P:T], ps[:, :].rearrange("p (b q) -> p b q", b=4), ACT.Copy)\
                        .then_inc(npts_ready, 1)

            for u in range(2 * H + 6):
                if u < 2 * H:
                    nsa_exponentials(u)
                if 2 <= u <= 2 * H + 1:
                    nsa_copy_transposed(u - 2)
                if u >= 9 and u % 4 == 1:
                    c = (u - 9) // 4
                    split_output(c, (no_out, 2 * c + 2))
            split_embedding(1)
            last_jobs("ffn5", T, STAGES["nsa_out"].w, x_from("nsa_out", 2))
            norm("ffn5", T, x_from("nsa_out", 2))
            ffn("ffn5", T, causal=1, then="pg1")
            per_layer(1)

        @block.vector
        def _(dve):
            chain = [0]

            def link(ins):
                chain[0] += 1
                ins.then_inc(v_step, 1)
                dve.wait_ge(v_step, chain[0])

            def gain(name, layer, n, g):
                link(nc.vector.scalar_tensor_tensor(
                    out=A[:, :, :], in0=mod(layer, n), scalar=1.0,
                    in1=col("norm_g", g * KC, KC).unsqueeze(2).to_broadcast([P, KC, 2]),
                    op0=ALU.add, op1=ALU.mult))

            def lo(t, i=0):
                if t >= NTILES:
                    return
                dve.wait_ge(w_hi, t + 1 + BODY * i)
                nc.vector.tensor_tensor(wl[t % SPLIT][:, :], raw[t % RAW][:, :],
                                        wh[t % SPLIT][:, :].bitcast(F32), ALU.subtract).then_inc(w_lo, 1)

            def feed(w, i=0):
                lo(w + 2, i)
                lo(w + 3, i)

            def feeds(name, jobs):
                for k in range(jobs):
                    feed(STAGES[name].w + 2 * k)

            def norm(name, n, gains, src=X, dst=None, shift=None):
                dve.wait_ge(std_ready, norm_no[name] + 1)
                link(nc.vector.reciprocal(bank[1][:, 0:n], STD[:, 0:n]))
                for c in range(KC):
                    for s in range(n // T):
                        ins = nc.vector.scalar_tensor_tensor(
                            out=(dst or H32)[:, c, s * T:(s + 1) * T], in0=src[:, c, s * T:(s + 1) * T],
                            scalar=gains(c, s), in1=bank[1][:, s * T:(s + 1) * T],
                            op0=ALU.mult, op1=ALU.mult)
                    ins.then_inc(x_normed if dst else scaled, 1)
                if not dst:
                    for c in range(KC):
                        dve.wait_ge(h_hi, KC * split_no[name] + c + 1)
                        if shift is None:
                            ins = nc.vector.tensor_tensor(HNL[:, c, 0:n], H32[:, c, 0:n],
                                                          HNH[:, c, 0:n].bitcast(F32), ALU.subtract)
                        else:
                            for s in range(n // T):
                                t = slice(s * T, (s + 1) * T)
                                ins = nc.vector.scalar_tensor_tensor(
                                    out=HNL[:, c, t], in0=H32[:, c, t], scalar=shift[:, c, s:s + 1],
                                    in1=HNH[:, c, t].bitcast(F32), op0=ALU.add, op1=ALU.subtract)
                        ins.then_inc(h_lo, 1)

            def split_output(c):
                dve.wait_ge(o_hi, c + 1)
                nc.vector.tensor_tensor(HNL[:, c % KC, 0:T], O32[:, c % KC, :],
                                        HNH[:, c % KC, 0:T].bitcast(F32), ALU.subtract).then_inc(o_split, 1)

            def mod_unit(m, i=0):
                per = 2 * GROUP * i
                dve.wait_ge(mod_landed[m % 2], 16 * (m // 2 + 1) + 16 * GROUP * i)
                if m >= 1:
                    dve.wait_ge(mod_done, m + per)
                nc.vector.tensor_tensor_reduce(junk[:, :], mod_ring[:, m % 2, :], CB[:, 0, :], 1.0, 0.0,
                                               ALU.mult, ALU.add, MA[:, m % 2, 0:1])
                nc.vector.tensor_tensor_reduce(mod_ring[:, m % 2, :], mod_ring[:, m % 2, :], CB[:, 1, :],
                                               1.0, 0.0, ALU.mult, ALU.add, MA[:, m % 2, 1:2])\
                    .then_inc(mod_acc, 1)
                dve.wait_ge(mod_acc, m + 1 + per)
                nc.vector.tensor_tensor(MOD[:, m + per, :], MA[:, m % 2, :], MODB[:, m + per, :], ALU.add)\
                    .then_inc(mod_done, 1)

            def ffn(name, n, mods=None, gate=None, causal=None):
                S = STAGES[name]

                def group(j, w, a, q, m, chunks, f0, i=0, first=True, units=2 * GROUP):
                    for k in range(chunks):
                        feed(w + 2 * k, i)
                        g = (j + k) % 3
                        A_, B_ = pair_banks(j + k)
                        dve.wait_ge(act_out, a + k + 1 + GROUP * i)
                        gg = G[:, g, 0:n]
                        if causal is not None:
                            c = FC * causal + f0 + k + 1
                            f = f0 + k + GROUP * i
                            nc.vector.scalar_tensor_tensor(
                                out=G[:, g, 1:T], in0=A_[:, 0:T - 1], scalar=ffn_conv_w[:, 3 * causal + 1, f],
                                in1=G[:, g, 1:T], op0=ALU.mult, op1=ALU.add).then_inc(tap_out, 1)
                            dve.wait_ge(tap_out, c + GROUP * i)
                            nc.vector.scalar_tensor_tensor(
                                out=G[:, g, 2:T], in0=A_[:, 0:T - 2], scalar=ffn_conv_w[:, 3 * causal, f],
                                in1=G[:, g, 2:T], op0=ALU.mult, op1=ALU.add).then_inc(conv_out, 1)
                            dve.wait_ge(gelu_out, c + GROUP * i)
                            gg = G[:, g, T:2 * T]
                        nc.vector.tensor_tensor(gg, gg, B_[:, 0:n], ALU.mult).then_inc(drained, 1)
                        if m is not None and 2 * k < units:
                            mod_unit(m + 2 * k, i)
                            mod_unit(m + 2 * k + 1, i)
                    if gate is not None and first:
                        (layer, nn), before = gate
                        if m is not None:
                            dve.wait_ge(mod_done, m + 2 * chunks + 2 * GROUP * i)
                        nc.vector.tensor_scalar(GT[:, :, :], mod(layer, nn), 0.5, None, ALU.mult)\
                            .then_inc(gt_ready, 1)
                        dve.wait_ge(gt_ready, before + 1 + i)
                    for k in range(4):
                        feed(w + 2 * (chunks + k), i)
                        dve.wait_ge(tile_used, w + 2 * (chunks + k) + 2 + BODY * i)
                        for f, ps in enumerate(pair_banks(j + chunks + k)):
                            c = 2 * k + f
                            for s in range(n // T):
                                t = slice(s * T, (s + 1) * T)
                                if gate is None:
                                    ins = nc.vector.tensor_tensor(X[:, c, t], X[:, c, t], ps[:, t], ALU.add)
                                else:
                                    ins = nc.vector.scalar_tensor_tensor(
                                        out=X[:, c, t], in0=ps[:, t], scalar=GT[:, c, s:s + 1],
                                        in1=X[:, c, t], op0=ALU.mult, op1=ALU.add)
                        ins.then_inc(drained, 1)

                with dve.Fori(0, 2) as i:
                    group(S.j, S.w, S.a, S.q, S.m if mods is not None else None, GROUP, 0, i)
                group(S.j + 2 * GJ, S.w + 2 * BODY, S.a + 2 * GROUP, S.q + 2 * GROUP,
                      S.m + 4 * GROUP if mods else None, LAST, 2 * GROUP, first=False, units=mods)

            def drain_biased(name, n, layer, bias):
                S = STAGES[name]
                for k in range(4):
                    feed(S.w + 2 * k)
                    dve.wait_ge(tile_used, S.w + 2 * k + 2)
                    for f, ps in enumerate(pair_banks(S.j + k)):
                        c = 2 * k + f
                        for s in range(n // T):
                            t = slice(s * T, (s + 1) * T)
                            ins = nc.vector.tensor_scalar(ps[:, t], ps[:, t], col(bias, c),
                                                          mod(layer, 5)[:, c, s:s + 1], ALU.add, ALU.mult)
                        link(ins)
                        ins = nc.vector.tensor_tensor(X[:, c, 0:n], X[:, c, 0:n], ps[:, 0:n], ALU.add)
                    ins.then_inc(drained, 1)

            def by_mod(c, s):
                return A[:, c, s:s + 1]

            def drain_plain(name):
                S = STAGES[name]
                for k in range(4):
                    feed(S.w + 2 * k)
                    dve.wait_ge(tile_used, S.w + 2 * k + 2)
                    for f, ps in enumerate(pair_banks(S.j + k)):
                        c = 2 * k + f
                        ins = nc.vector.tensor_tensor(X[:, c, 0:T], X[:, c, 0:T], ps[:, 0:T], ALU.add)
                    ins.then_inc(drained, 1)

            def split_embedding(i):
                dve.wait_ge(p_hi, i + 1)
                nc.vector.tensor_tensor(PSPLIT[1], PIN[:, 2 * i:2 * i + 2, :], PSPLIT[0].bitcast(F32),
                                        ALU.subtract).then_inc(p_split, 1)

            def per_layer(i):
                S = STAGES[f"ple_e{i}"]
                for j in range(4):
                    if j % 2 == 0:
                        dve.wait_ge(part_done, S.part + j // 2 + 1)
                    else:
                        dve.wait_ge(tile_used, S.w + j // 2 + 1)
                    for f, ps in enumerate(pair_banks(S.j + j)):
                        ins = nc.vector.tensor_copy(E[:, 2 * j + f, :], ps[:, 0:T])
                    ins.then_inc(drained, 1)
                feed(S.w)
                norm(f"pg{i}", T, lambda c, s: col("ple_gate_norm_g", i * KC + c))
                S = STAGES[f"ple_g{i}"]
                feed(S.w)
                norm(f"e{i}", T, lambda c, s: col("ple_norm_g", i * KC + c), src=E, dst=E)
                dve.wait_ge(x_normed, KC * (plain_no[f"e{i}"] + 1))
                for k in range(4):
                    if k >= 1:
                        feed(S.w + 2 * k)
                    dve.wait_ge(act_out, S.a + k + 1)
                    g = G[:, (S.j + k) % 3, :].rearrange("p (f t) -> p f t", f=2)
                    link(nc.vector.tensor_tensor(g, g, E[:, 2 * k:2 * k + 2, :], ALU.mult))
                    nc.vector.tensor_tensor(X[:, 2 * k:2 * k + 2, 0:T], X[:, 2 * k:2 * k + 2, 0:T], g, ALU.add)\
                        .then_inc(drained, 1)

            dve.wait_ge(params_in, 16)
            def add_taps(k):
                dve.wait_ge(taps_done, TAPS_PE * (k + 1))
                nc.vector.tensor_tensor(CV[:, k, :], CV[:, k, :], bank[k % 2][:, :], ALU.add)\
                    .then_inc(cv_ready, 1)

            dve.wait_ge(cond_ready, 1)
            for m in range(16):
                mod_unit(m)
                if m in (9, 10):
                    lo(m - 9)
            dve.wait_ge(mod_done, 16)
            gain("ffn0", 0, 1, 0)
            norm("ffn0", T + C, by_mod, shift=mod(0, 0))
            ffn("ffn0", T + C, 12, ((0, 2), 0))
            gain("conv", 0, 4, 1)
            norm("conv", T + C, by_mod, shift=mod(0, 3))
            dve.wait_ge(h_lo, KC * (split_no["conv"] + 1))
            for s in range(3):
                nc.vector.memset(U[:, :, s * SEG:s * SEG + PAD], 0.0)
            S = STAGES["pw1"]
            for k in range(8):
                feed(S.w + 2 * k)
                dve.wait_ge(act_out, S.a + k + 1)
                nc.vector.scalar_tensor_tensor(
                    out=both(k, PAD), in0=pair_banks(S.j + k)[0][:, :].rearrange("p (s t) -> p s t", s=2),
                    scalar=col("b_pw1", k), in1=G[:, (S.j + k) % 3, :].rearrange("p (s t) -> p s t", s=2),
                    op0=ALU.add, op1=ALU.mult).then_inc(drained, 1)
                if k < 4:
                    mod_unit(S.m + k)
                dve.wait_ge(drained, S.j + k + 1)
                cv = CV[:, k, :].rearrange("p (s t) -> p s t", s=2)
                link(nc.vector.tensor_scalar(cv, both(k, 0), col("w_dw", k), col("b_dw", k),
                                             ALU.mult, ALU.add))
                for tap in range(1, TAPS - TAPS_PE):
                    link(nc.vector.scalar_tensor_tensor(
                        out=cv, in0=both(k, tap), scalar=col("w_dw", tap * KC + k), in1=cv,
                        op0=ALU.mult, op1=ALU.add))
                if k >= 1:
                    add_taps(k - 1)
            add_taps(KC - 1)
            dve.wait_ge(mu_ready, 1)
            for c in range(KC):
                nc.vector.tensor_tensor(CV[:, c, :], CV[:, c, :], pair_banks(S.j + KC)[0][:, :],
                                        ALU.subtract)\
                    .then_inc(cv_centred, 1)
            dve.wait_ge(std_ready, norm_no["ln"] + 1)
            link(nc.vector.reciprocal(bank[1][:, :], STD[:, :]))
            for c in range(KC):
                nc.vector.tensor_tensor(CV[:, c, :], CV[:, c, :], bank[1][:, :], ALU.mult)\
                    .then_inc(cvn_ready, 1)
            for c in range(KC):
                dve.wait_ge(h_hi, KC * split_no["ln"] + c + 1)
                nc.vector.tensor_tensor(HNL[:, c, :], CV[:, c, :], HNH[:, c, :].bitcast(F32), ALU.subtract)\
                    .then_inc(h_lo, 1)
            drain_biased("pw2", T + C, 0, "b_pw2")
            dve.wait_ge(mod_done, STAGES["ffn1"].m)
            gain("ffn1", 0, 7, 2)
            norm("ffn1", T + C, by_mod, shift=mod(0, 6))
            ffn("ffn1", T + C, 12, ((0, 8), 2))
            gain("ffn2", 1, 1, 3)
            norm("ffn2", T + C, by_mod, shift=mod(1, 0))
            ffn("ffn2", T + C, 4, ((1, 2), 4))
            dve.wait_ge(mod_done, STAGES["na_qk"].m)
            gain("na", 1, 4, 4)
            norm("na", T + C, by_mod, shift=mod(1, 3))
            dve.wait_ge(h_lo, KC * (split_no["na"] + 1))
            S = STAGES["na_qk"]
            for k in range(8):
                feed(S.w + 2 * k)
                dve.wait_ge(tile_used, S.w + 2 * k + 2)
                for f, ps in enumerate(pair_banks(S.j + k)):
                    c = 2 * k + f
                    if k < 4:
                        ins = nc.vector.tensor_scalar(NQ[:, c, :], ps[:, 0:T], col("b_qkv", c), DH ** -0.5,
                                                      ALU.add, ALU.mult)
                    else:
                        ins = nc.vector.tensor_scalar(NK[:, c - KC, :], ps[:, :], col("b_qkv", c), None,
                                                      ALU.add)
                ins.then_inc(drained, 1)
            S = STAGES["na_v"]
            for k in range(4):
                feed(S.w + 2 * k)
                dve.wait_ge(tile_used, S.w + 2 * k + 2)
                for h, ps in enumerate(pair_banks(S.j + k)):
                    ins = nc.vector.tensor_copy(NV[h][:, :, 2 * k * P:2 * (k + 1) * P],
                                                ps[:, :].rearrange("p (s d) -> p s d", s=2))
                ins.then_inc(drained, 1)

            def maxima(u):
                h, t = u // 2, u % 2
                dve.wait_ge(s_ready, u + 1)
                dve.wait_ge(bias_ready, h + 1)
                ps = bank[u % 4]
                at = (2 - 2 * t) * GRID
                link(nc.vector.tensor_tensor(ps[:, 0:T], ps[:, 0:T], RBT[:, h % 2, at:at + T], ALU.add))
                nc.vector.tensor_reduce(NM[:, u:u + 1], ps[:, :], AX.X, ALU.max, negate=True)\
                    .then_inc(s_max, 1)

            def diagonal(u):
                dve.wait_ge(p_ready, u + 1)
                link(nc.vector.reciprocal(RSUM[:, u:u + 1], SUM[:, u:u + 1]))
                if u >= 2:
                    dve.wait_ge(pt_ready, u - 1)
                nc.vector.tensor_scalar(DG[:, u % 2, :], const("ident"), RSUM[:, u:u + 1], None, ALU.mult)\
                    .then_inc(dg_ready, 1)

            def copy_output(h):
                r = DH * (h % 2)
                dve.wait_ge(o_ready, h + 1)
                nc.vector.tensor_scalar(O32[r:r + DH, h // 2, :], bank[6 + h % 2][r:r + DH, 0:T],
                                        cols[r:r + DH, COLS["b_qkv"][0] + 2 * KC + h // 2:
                                             COLS["b_qkv"][0] + 2 * KC + h // 2 + 1],
                                        None, ALU.add).then_inc(o_out, 1)

            for u in range(2 * H + 7):
                if u < 2 * H:
                    maxima(u)
                if 1 <= u <= 2 * H:
                    diagonal(u - 1)
                if 6 <= u <= 2 * H + 4 and u % 2 == 0:
                    copy_output((u - 6) // 2)
                if u >= 10 and u % 4 == 2:
                    split_output((u - 10) // 4)
            drain_biased("na_o", T, 1, "b_o")
            gain("ffn3", 1, 7, 5)
            norm("ffn3", T, by_mod, shift=mod(1, 6))
            ffn("ffn3", T, None, ((1, 8), 6))
            norm("final", T, lambda c, s: col("final_g", c), dst=X)

            norm("ab", T, lambda c, s: col("ab_norm_g", c))
            dve.wait_ge(gate_step, 1)
            nc.vector.tensor_scalar(IG[0:4, :], bank[2][0:4, 0:T], cols[0:4, gb:gb + 1], None, ALU.add)
            nc.vector.tensor_scalar(XF[0:4, :], bank[3][0:4, 0:T], cols[0:4, gb + 1:gb + 2], None, ALU.add)\
                .then_inc(gate_step, 1)
            S = STAGES["ab_in"]
            nc.vector.memset(MPAD[:, :, 0:3], 0.0)
            for k in range(12):
                feed(S.w + 2 * k)
                if k == 3:
                    dve.wait_ge(gate_step, 3)
                    link(nc.vector.tensor_scalar(XF[0:4, :], XF[0:4, :], 0.0, None, ALU.min))
                    link(nc.vector.tensor_tensor(LROW[0:4, :], XF[0:4, :], LROW[0:4, :], ALU.subtract))
                    link(nc.vector.tensor_tensor_scan(BROW[0:4, :], ones_row, LROW[0:4, :], 0.0,
                                                      ALU.mult, ALU.add))
                    link(nc.vector.tensor_tensor(AROW[0:4, :], IG[0:4, :], BROW[0:4, :], ALU.subtract))
                    link(nc.vector.tensor_tensor_scan(MROW[0:4, :], AROW[0:4, :], AROW[0:4, :], 0.0,
                                                      ALU.max, ALU.max))
                    nc.vector.scalar_tensor_tensor(out=NMT[0:4, :], in0=BROW[0:4, :], scalar=-1.0,
                                                   in1=MROW[0:4, :], op0=ALU.mult, op1=ALU.subtract)\
                        .then_inc(gate_step, 1)
                if k in (4, 5):
                    for c in (2 * (k - 4), 2 * (k - 4) + 1):
                        dve.wait_ge(rotated, 2 * (c // 2) + 2)
                        rx = bank[c // 2][:, (c % 2) * T:(c % 2 + 1) * T]
                        nc.vector.tensor_tensor(RQK[:, c, :], RQK[:, c, :], const("cos"), ALU.mult)
                        link(nc.vector.tensor_tensor(rx, rx, const("sin"), ALU.mult))
                        nc.vector.tensor_tensor(RQK[:, c, :], RQK[:, c, :], rx, ALU.add).then_inc(rope_done, 1)
                if k >= 8:
                    c = k - 8
                    dve.wait_ge(drained, S.j + 8)
                    link(nc.vector.tensor_scalar(MQK[:, c, :], MPAD[:, c, 0:T], col("ab_conv_w", c),
                                                 col("ab_conv_b", c), ALU.mult, ALU.add))
                    for tap in range(1, 4):
                        ins = nc.vector.scalar_tensor_tensor(out=MQK[:, c, :], in0=MPAD[:, c, tap:tap + T],
                                                             scalar=col("ab_conv_w", 4 * tap + c),
                                                             in1=MQK[:, c, :], op0=ALU.mult, op1=ALU.add)
                        if tap < 3:
                            link(ins)
                    ins.then_inc(mconv_ready, 1)
                dve.wait_ge(tile_used, S.w + 2 * k + 2)
                if k in (2, 3, 8, 9):
                    ins = nc.vector.tensor_copy((RV if k < 4 else MV)[:, :, (k % 2) * T:(k % 2 + 1) * T],
                                                pair_banks(S.j + k)[0][:, :].rearrange("p (s d) -> p s d", s=2))
                    ins.then_inc(drained, 1)
                    continue
                for f, ps in enumerate(pair_banks(S.j + k)):
                    if k < 2:
                        ins = nc.vector.tensor_scalar(RQK[:, 2 * k + f, :], ps[:, 0:T],
                                                      1.0 if k == 0 else DH ** -0.5, None, ALU.mult)
                    elif k in (6, 7):
                        ins = nc.vector.tensor_copy(MPAD[:, 2 * (k - 6) + f, 3:3 + T], ps[:, 0:T])
                    else:
                        dst = RG if k < 6 else MO
                        ins = nc.vector.tensor_copy(dst[:, 2 * (k % 2) + f, :], ps[:, 0:T])
                ins.then_inc(drained, 1)
            dve.wait_ge(gate_step, 5)
            nc.vector.tensor_copy(ACOL[:, :], bank[0][:, 0:8])
            for b in range(2):
                ps = bank[2 + b][:, :].rearrange("p (e t) -> p e t", e=2)
                mask = const("causal_t").unsqueeze(1).to_broadcast([P, 2, P])
                w = WT[:, 2 * b:2 * b + 2, :]
                nc.vector.tensor_tensor(w[:, :, 0:P], mask, ps[:, :, 0:P], ALU.subtract)
                nc.vector.tensor_scalar(w[:, :, P:T], ps[:, :, P:T], -1.0, None, ALU.mult)
                ins = nc.vector.tensor_tensor(w[:, :, T:T + P], mask, ps[:, :, P:T], ALU.subtract)
            ins.then_inc(gate_step, 1)
            dve.wait_ge(rg_ready, 1)
            dve.wait_ge(mo_ready, 1)

            def weighted(pr):
                dve.wait_ge(ab_scores, pr + 1)
                if pr >= 2:
                    dve.wait_ge(ab_values, pr - 1)
                for e in range(2):
                    h = 2 * (pr % 2) + e
                    ps = bank[2 + 2 * (pr % 2) + e]
                    for a, b in ((0, T), (T, T + P)):
                        if pr >= 2:
                            ins = nc.vector.scalar_tensor_tensor(
                                out=SW[pr % 2][:, e, a:b], in0=ps[:, a:b], scalar=DH ** -0.5,
                                in1=WT[:, h, a:b], op0=ALU.mult, op1=ALU.mult)
                        else:
                            ins = nc.vector.tensor_tensor(SW[pr % 2][:, e, a:b], ps[:, a:b],
                                                          const("decay", h * T, b - a), ALU.mult)
                ins.then_inc(ab_weighted, 1)

            def divide(pr):
                dve.wait_ge(ab_values, pr + 1)
                h = 2 * (pr % 2)
                den = bank[AB_DEN[pr]][:, :].rearrange("p (e t) -> p e t", e=2)
                link(nc.vector.tensor_tensor(DEN, den, EMT[:, h:h + 2, :], ALU.max))
                link(nc.vector.scalar_tensor_tensor(out=DEN, in0=den, scalar=-1.0, in1=DEN,
                                                    op0=ALU.mult, op1=ALU.max))
                link(nc.vector.reciprocal(DEN, DEN))
                num = bank[AB_NUM[pr]][:, :].rearrange("p (e t) -> p e t", e=2)
                nc.vector.tensor_tensor(num, num, DEN, ALU.mult).then_inc(ab_divided, 1)

            def normed(pr):
                dve.wait_ge(ab_root, pr + 1)
                link(nc.vector.reciprocal(STD[:, :], STD[:, :]))
                for e in range(2):
                    h = 2 * (pr % 2) + e
                    t = slice(e * T, (e + 1) * T)
                    link(nc.vector.scalar_tensor_tensor(
                        out=O32[:, 2 * pr + e, :], in0=bank[AB_NUM[pr]][:, t],
                        scalar=col("m_g" if pr >= 2 else "ret_g", h), in1=STD[:, t],
                        op0=ALU.mult, op1=ALU.mult))
                    ins = nc.vector.tensor_tensor(O32[:, 2 * pr + e, :], O32[:, 2 * pr + e, :],
                                                  (MO if pr >= 2 else RG)[:, h, :], ALU.mult)
                ins.then_inc(ab_out, 1)

            for pr in range(6):
                if pr < 4:
                    weighted(pr)
                if pr in (3, 4):
                    divide(pr - 1)
                if pr >= 2:
                    normed(pr - 2)
                if pr >= 3:
                    for c in (2 * (pr - 3), 2 * (pr - 3) + 1):
                        split_output(KC + c)
            for c in (6, 7):
                split_output(KC + c)
            split_embedding(0)
            drain_plain("ab_out")
            norm("ffn4", T, lambda c, s: col("ffn_norm_g", c))
            ffn("ffn4", T, causal=0)
            per_layer(0)
            norm("nsa", T, lambda c, s: col("nsa_norm_g", c))
            dve.wait_ge(nsa_step, 1)
            S = STAGES["nsa_in"]
            for k in range(8):
                feed(S.w + 2 * k)
                dve.wait_ge(tile_used, S.w + 2 * k + 2)
                for f, ps in enumerate(pair_banks(S.j + k)):
                    if k in (4, 5):
                        pos = col("pos_k" if k == 4 else "pos_v", 0, 16)
                        for lp in range(2):
                            r = slice(DH * lp, DH * lp + DH)
                            rows = ps[r, lp:lp + 255]
                            rows = bass.AP(rows.tensor, rows.offset, [rows.ap[0], [2, 16], [16, NC_CMP]])
                            ins = nc.vector.tensor_tensor(
                                BLK[r, k - 4, :, f * 15:(f + 1) * 15], rows,
                                pos[r, :].unsqueeze(2).to_broadcast([DH, 16, NC_CMP]), ALU.add)
                    elif k == 7:
                        if f == 0:
                            ins = nc.vector.tensor_copy(SV, ps[:, :].rearrange("p (s d) -> p s d", s=2))
                    else:
                        ins = nc.vector.tensor_copy(QK[:, 2 * min(k, 4) + f, :], ps[:, 0:T])
                ins.then_inc(drained, 1)
                if k == 3:
                    link(nc.vector.tensor_scalar(QG[:, :], col("q_g"), DH ** -0.5, None, ALU.mult))
            dve.wait_ge(blk_hi, 1)
            nc.vector.tensor_tensor(BSPLIT[:, :, :, 1, :], BLK[:, :, :, :], BSPLIT[:, :, :, 0, :].bitcast(F32),
                                    ALU.subtract)\
                .then_inc(blk_split, 1)
            nc.vector.tensor_tensor(GATE[:, :].rearrange("p (s n) -> p s n", s=2),
                                    bank[0][:, 0:96].rearrange("p (s n) -> p s n", s=2),
                                    col("gate_b", 0, 48).unsqueeze(1).to_broadcast([P, 2, 48]), ALU.add)\
                .then_inc(nsa_step, 1)
            S = STAGES["nsa_mlp"]

            def drain_compressed(m):
                dve.wait_ge(tile_used, S.w + 4 * m + 4)
                for f, ps in enumerate(pair_banks(S.j + m)):
                    link(nc.vector.tensor_copy(HC[:, m, f, :], ps[:, 0:30]))
                    ins = nc.vector.tensor_tensor(HC[:, m, f, :], HC[:, m, f, :], ps[:, 30:60], ALU.add)
                ins.then_inc(drained, 1)

            for n in range(5):
                dve.wait_ge(qstd_ready, n + 1)
                link(nc.vector.reciprocal(STD[:, :], STD[:, :]))
                for f in range(2):
                    c = 2 * n + f
                    g = QG[:, :] if c < 8 else col("k_g", c - 7)
                    ins = nc.vector.scalar_tensor_tensor(out=QK[:, c, :], in0=QK[:, c, :], scalar=g,
                                                         in1=STD[:, f * T:(f + 1) * T],
                                                         op0=ALU.mult, op1=ALU.mult)
                ins.then_inc(qn_ready, 1)
                if n < 4:
                    feed(S.w + 2 * n)
                if n >= 2 and n % 2 == 0:
                    drain_compressed(n // 2 - 1)
            dve.wait_ge(nsa_step, 7)
            nc.vector.tensor_copy(VCS[0:15, :], bank[0][0:15, 0:P])
            link(nc.vector.reciprocal(STD[:, 0:15], STD[:, 0:15]))
            nc.vector.scalar_tensor_tensor(out=KCN[:, :], in0=bank[1][:, 0:15], scalar=col("k_g", 0),
                                           in1=STD[:, 0:15], op0=ALU.mult, op1=ALU.mult)\
                .then_inc(nsa_step, 1)
            dve.wait_ge(nsa_step, 9)
            for t in range(2):
                pc = PC[:, t, :, 0:15]
                for g in range(2):
                    ps = bank[2 + 2 * t + g][:, 0:128].rearrange("p (h n) -> p h n", h=8)[:, :, 0:15]
                    ins = nc.vector.tensor_tensor(pc[:, 8 * g:8 * g + 8, :], ps,
                                                  cmp_add[:, t:t + 1, 0:15].to_broadcast([P, 8, 15]), ALU.add)
                link(ins)
                link(nc.vector.tensor_reduce(CM[:, t, :], pc, AX.X, ALU.max))
                ins = nc.vector.tensor_tensor(pc, pc, CM[:, t, :].unsqueeze(2).to_broadcast([P, H, 15]),
                                              ALU.subtract)
            ins.then_inc(nsa_step, 1)
            dve.wait_ge(pc_exp, 1)
            dve.wait_ge(ngate_ready, 1)
            gates = GATE[:, :].rearrange("p (s h b) -> p s h b", s=2, b=3)
            for t in range(2):
                pc = PC[:, t, :, 0:15]
                link(nc.vector.tensor_reduce(CM[:, t, :], pc, AX.X, ALU.add))
                link(nc.vector.reciprocal(CM[:, t, :], CM[:, t, :]))
                link(nc.vector.tensor_tensor(CM[:, t, :], CM[:, t, :], gates[:, t, :, 0], ALU.mult))
                link(nc.vector.tensor_tensor(pc, pc, cmp_valid[:, t:t + 1, 0:15].to_broadcast([P, H, 15]),
                                             ALU.mult))
                ins = nc.vector.tensor_tensor(pc, pc, CM[:, t, :].unsqueeze(2).to_broadcast([P, H, 15]), ALU.mult)
            ins.then_inc(nsa_step, 1)

            def nsa_maxima(u):
                t = u % 2
                dve.wait_ge(ns_ready, u + 1)
                ps = bank[u % 3][:, 0:2 * P * (t + 1)].rearrange("p (b k) -> p b k", b=2)
                link(nc.vector.tensor_tensor(ps[:, :, t * P:(t + 1) * P], ps[:, :, t * P:(t + 1) * P],
                                             const("causal").unsqueeze(1).to_broadcast([P, 2, P]), ALU.add))
                nc.vector.tensor_reduce(NM[:, 2 * u:2 * u + 2], ps, AX.X, ALU.max, negate=True)\
                    .then_inc(ns_max, 1)

            def nsa_diagonals(u):
                h, t = u // 4 + 8 * (u // 2 % 2), u % 2
                dve.wait_ge(np_ready, u + 1)
                link(nc.vector.reciprocal(RSUM[:, 2 * u:2 * u + 2], SUM[:, 2 * u:2 * u + 2]))
                link(nc.vector.tensor_tensor(RSUM[:, 2 * u:2 * u + 2], RSUM[:, 2 * u:2 * u + 2],
                                             gates[:, t, h, 1:3], ALU.mult))
                if u >= 2:
                    dve.wait_ge(npt_ready, u - 1)
                for b in range(2):
                    ins = nc.vector.tensor_scalar(DG2[:, u % 2, b, :], const("ident"),
                                                  RSUM[:, 2 * u + b:2 * u + b + 1], None, ALU.mult)
                ins.then_inc(ndg_ready, 1)

            def nsa_copy_output(n):
                r = DH * (n % 2)
                dve.wait_ge(no_ready, n + 1)
                nc.vector.tensor_copy(O32[r:r + DH, n // 2, :], bank[6 + n % 2][r:r + DH, 0:T])\
                    .then_inc(no_out, 1)

            for u in range(2 * H + 7):
                if u < 2 * H:
                    nsa_maxima(u)
                if 1 <= u <= 2 * H:
                    nsa_diagonals(u - 1)
                if 6 <= u <= 2 * H + 4 and u % 2 == 0:
                    nsa_copy_output((u - 6) // 2)
                if u >= 10 and u % 4 == 2:
                    split_output(2 * KC + (u - 10) // 4)
            split_embedding(1)
            drain_plain("nsa_out")
            norm("ffn5", T, lambda c, s: col("ffn_norm_g", KC + c))
            ffn("ffn5", T, causal=1)
            per_layer(1)

        @block.gpsimd
        def _(pool):
            pool.wait_ge(consts_in, 16)

            def ffn(name, n, gelu=False):
                S = STAGES[name]
                a = T if gelu else 0

                def group(j, q, chunks, i=0):
                    for k in range(chunks):
                        src = G[:, (j + k) % 3, a:a + n]
                        pool.wait_ge(drained, j + k + 1 + GJ * i)
                        nc.gpsimd.tensor_tensor(HDH[:, k, 0:n], src, const("one").to_broadcast([P, n]),
                                                ALU.mult).then_inc(hid_hi, 1)
                        pool.wait_ge(hid_hi, q + k + 1 + GROUP * i)
                        nc.gpsimd.tensor_tensor(HDL[:, k, 0:n], src, HDH[:, k, 0:n].bitcast(F32),
                                                ALU.subtract).then_inc(hid_ready, 1)

                with pool.Fori(0, 2) as i:
                    group(S.j, S.q, GROUP, i)
                group(S.j + 2 * GJ, S.q + 2 * GROUP, LAST)

            def add_squares(name, n):
                for c in range(1, KC - 2):
                    pool.wait_ge(sq_ready, KC * norm_no[name] + c + 1)
                    if c >= 2:
                        pool.wait_ge(sq_added, squares_added[name] + c - 1)
                    nc.gpsimd.tensor_tensor(STD[:, 0:n], SQ[:, 0, 0:n] if c == 1 else STD[:, 0:n],
                                            SQ[:, c % 2, 0:n], ALU.add).then_inc(sq_added, 1)

            ffn("ffn0", T + C)
            add_squares("conv", T + C)
            for d in range(KC * TAPS_PE):
                c, tap = d // TAPS_PE, TAPS - TAPS_PE + d % TAPS_PE
                if d >= 4:
                    pool.wait_ge(taps_done, d - 3)
                nc.gpsimd.tensor_scalar(DIAG[:, d % 4, :], const("ident"), col("w_dw", tap * KC + c), 1.0,
                                        ALU.mult, ALU.mult).then_inc(diag_ready, 1)
            add_squares("ffn1", T + C)
            ffn("ffn1", T + C)
            add_squares("ffn2", T + C)
            ffn("ffn2", T + C)
            add_squares("na", T + C)

            def load_bias(h):
                if h >= 2:
                    pool.wait_ge(s_max, 2 * h - 2)
                pool.dma_start(RB_T[:, h % 2, :], rpb[h, :, :]).then_inc(bias_in[h % 2], 16)

            load_bias(0)
            for h in range(H):
                if h + 1 < H:
                    load_bias(h + 1)
                pool.wait_ge(bias_in[h % 2], 16 * (h // 2 + 1))
                nc.gpsimd.tensor_tensor(RBT[:, h % 2, :].rearrange("p (u k) -> p u k", u=6),
                                        RB_T[:, h % 2, :].rearrange("p (u k) -> p u k", u=6),
                                        const("window").unsqueeze(1).to_broadcast([P, 6, GRID]),
                                        ALU.add).then_inc(bias_ready, 1)

            add_squares("ffn3", T)
            ffn("ffn3", T)
            add_squares("final", T)
            pool.wait_ge(x_normed, KC)
            pool.dma_start(PIN, p_in).then_inc(p_loaded, 16)
            add_squares("ffn4", T)
            ffn("ffn4", T, True)
            add_squares("pg0", T)
            add_squares("ffn5", T)
            ffn("ffn5", T, True)
            add_squares("pg1", T)




def tiles(W):
    k = W.shape[0] // P
    out = np.zeros((W.shape[1] // P, P, KC, P), W.dtype)
    out[:, :, :k] = W.reshape(k, P, -1, P).transpose(2, 1, 0, 3)
    return out.reshape(-1, P, TILE)


def wide_tiles(W):
    return W.reshape(2, 4, P, -1, 2 * P).transpose(3, 0, 2, 1, 4).reshape(-1, P, TILE)


def alternate(a, b):
    return np.stack([a, b], axis=1).reshape(-1, P, TILE)


def columns(v):
    return v.reshape(-1, P).T


def weight_stream(a):
    def ffn(gate, up, down):
        parts, f = [], 0
        for n in (GROUP, GROUP, LAST):
            s = slice(f * P, (f + n) * P)
            parts += [alternate(tiles(gate[:, s]), tiles(up[:, s])), tiles(down[s])]
            f += n
        return parts

    def cffn(i):
        up = a["ffn_w_up_2"][i]
        return ffn(up[:, :F], up[:, F:], a["ffn_w_down_2"][i])

    def ple(i):
        w = a["ple_w_2"][i].reshape(2, P, 2, 512).transpose(2, 1, 0, 3)
        return [w.reshape(2, P, TILE), tiles(a["ple_w_gate_2"][i])]

    def first_ffn(i, j):
        return ffn(a["ffn_w_gate"][i, j], a["ffn_w_up"][i, j], a["ffn_w_down"][i, j])

    pw1 = a["conv_w_pw1"][0]
    parts = first_ffn(0, 0) + [alternate(tiles(pw1[:, :D]), tiles(pw1[:, D:])), tiles(a["conv_w_pw2"][0])]
    qkv = a["na_w_qkv"][0]
    parts += first_ffn(0, 1) + first_ffn(1, 0)
    parts += [tiles(qkv[:, :2 * D]), wide_tiles(qkv[:, 2 * D:]), tiles(a["na_w_o"][0])]
    parts += first_ffn(1, 1)
    w = a["ab_w_in_2"][0]
    parts += [tiles(w[:, :512]), wide_tiles(w[:, 512:1024]), tiles(w[:, 1024:2048]),
              wide_tiles(w[:, 2048:2560]), tiles(w[:, 2560:3072]), tiles(a["ab_w_out_2"][0])]
    parts += cffn(0) + ple(0)
    w = a["nsa_w_in_2"][0]
    q = w[:, :1024].reshape(D, 2, 8, DH).transpose(0, 2, 1, 3).reshape(D, 1024)
    kc, vc, ks, vs, kw, vw = (w[:, 1024 + 128 * n:1152 + 128 * n] for n in range(6))

    def twice(m):
        return np.repeat(m.reshape(D, 2, 1, DH), 2, axis=2).reshape(D, 256)

    parts += [tiles(m) for m in (q, twice(kc), twice(vc), ks, kw)]
    parts += [wide_tiles(np.concatenate([vs, vw], axis=1))]
    for w1 in ("nsa_cmp_w1k_2", "nsa_cmp_w1v_2"):
        parts += [tiles(a[w1][0][:1024]), tiles(a[w1][0][1024:])]
    wo = a["nsa_w_out_2"][0].reshape(2, 8, DH, D).transpose(1, 0, 2, 3).reshape(D, D)
    parts += [tiles(wo)] + cffn(1) + ple(1)
    return np.concatenate(parts)


def parameters(a):
    two = lambda v: np.concatenate([v, v])
    mod_b = np.repeat(columns(a["mod_b"])[:, :, None], 2, axis=2).reshape(P, 288)
    rows4 = np.zeros((P, 2), np.float32)
    rows4[0:4, 0], rows4[0:4, 1] = a["ab_ig_b_2"][0], a["ab_fg_b_2"][0]
    cmp_pos = lambda v: v[0].reshape(16, P).T
    chunked = lambda w: w.reshape(-1, P, w.shape[-1]).transpose(1, 0, 2).reshape(P, -1)
    by_name = {
        "mod_b": mod_b, "norm_g": columns(a["norm_g"]), "b_pw1": columns(a["conv_b_pw1"]),
        "w_dw": columns(a["conv_w_dw"]), "b_dw": columns(a["conv_b_dw"]), "ln_g": columns(a["conv_ln_g"]),
        "ln_b": columns(a["conv_ln_b"]), "b_pw2": columns(a["conv_b_pw2"]), "b_qkv": columns(a["na_b_qkv"]),
        "b_o": columns(a["na_b_o"]), "final_g": columns(a["final_g"]), "ab_norm_g": columns(a["ab_norm_g_2"]),
        "ab_conv_w": columns(a["ab_conv_w_2"]), "ab_conv_b": columns(a["ab_conv_b_2"]),
        "ret_g": columns(a["ab_ret_norm_g_2"]), "m_g": columns(a["ab_m_norm_g_2"]), "gate_bias": rows4,
        "ab_wgate": chunked(a["ab_w_in_2"][0][:, 3072:]), "nsa_norm_g": columns(a["nsa_norm_g_2"]),
        "q_g": two(a["nsa_q_norm_g_2"][0])[:, None],
        "k_g": np.concatenate([a["nsa_k_norm_g_2"][0]] * 2, axis=1).T,
        "pos_k": cmp_pos(a["nsa_cmp_pos_k_2"]), "pos_v": cmp_pos(a["nsa_cmp_pos_v_2"]),
        "gate_b": np.repeat(a["nsa_gate_b_2"], P, axis=0),
        "nsa_wgate": chunked(a["nsa_w_in_2"][0][:, 1792:]),
        "w2k": chunked(a["nsa_cmp_w2k_2"][0]), "w2v": chunked(a["nsa_cmp_w2v_2"][0]),
        "ffn_norm_g": columns(a["ffn_norm_g_2"]), "ffn_conv_w": columns(a["ffn_conv_w_2"]),
        "ffn_conv_b": columns(a["ffn_conv_b_2"]), "ple_norm_g": columns(a["ple_norm_g_2"]),
        "ple_gate_norm_g": columns(a["ple_gate_norm_g_2"]),
    }
    for name, v in by_name.items():
        assert v.shape == (P, COLS[name][1]), (name, v.shape)
    return np.concatenate([by_name[name] for name in COLS], axis=1)


def constants():
    p = np.arange(P)
    t = np.arange(T)
    block64 = (p[:, None] // 64 == p[None, :] // 64) / 64
    rot = np.zeros((P, P))
    for m in range(P):
        rot[m + 32 if m % 64 < 32 else m - 32, m] = -1.0 if m % 64 < 32 else 1.0
    inv = (np.float32(10000.0) ** (-np.arange(32, dtype=np.float32) / np.float32(32))).astype(np.float32)
    ang = (t.astype(np.float32)[None, :] * inv[p % 32][:, None]).astype(np.float32)
    log_g = np.log1p(-np.exp2(-5.0 - np.arange(4)))
    diff = t[None, :] - p[:, None]
    decay = [np.where(diff >= 0, np.exp(np.maximum(diff, 0) * g), 0.0) for g in log_g]
    c, kc = p[:, None] % GRID, np.arange(GRID)[None, :]
    start = np.clip(c - 8, 0, GRID - 16)
    q = p[:, None, None] + P * np.arange(2)[None, :, None]
    n = np.arange(16)[None, None, :]
    cmp_valid = (16 * n + 31 <= q) & (n < NC_CMP)
    sel = np.zeros((P, 4, P))
    for h in range(4):
        sel[h, h, :] = 1.0
    by_name = {
        "ident": np.eye(P), "mean_all": np.full((P, P), 1 / D), "ones": np.ones((P, P)),
        "mean64": block64, "mean128": np.full((P, P), 1 / P), "rot": rot,
        "cos": np.cos(ang.astype(np.float64)), "sin": np.sin(ang.astype(np.float64)),
        "causal": np.where(p[None, :] <= p[:, None], 0.0, MASKED),
        "causal_t": np.where(p[:, None] <= p[None, :], 0.0, MASKED),
        "decay": np.concatenate(decay, axis=1),
        "window": np.where((kc >= start) & (kc < start + 16), 0.0, MASKED),
        "cmp_add": np.where(cmp_valid, 0.0, MASKED).reshape(P, 32),
        "cmp_valid": cmp_valid.reshape(P, 32), "sel": sel.reshape(P, 4 * P),
        "eps6": np.full((P, 1), 1e-6), "eps5": np.full((P, 1), 1e-5), "one": np.ones((P, 1)),
    }
    return np.concatenate([by_name[name] for name in CONST], axis=1).astype(np.float32)


def relative_bias(rpb):
    c, kc = np.arange(GRID)[:, None], np.arange(GRID)[None, :]
    col = np.clip(kc - c, -(CB // 2), CB // 2) + CB // 2
    rows = [rpb[:, 5 - r:11 - r][:, :, col].transpose(0, 2, 1, 3) for r in range(2)]
    return np.concatenate(rows, axis=1).reshape(H, P, 6 * GRID)


def kernel(**a):
    import concourse.bacc as bacc
    from concourse.bass_utils import run_bass_kernel_spmd

    a = {n: np.asarray(v) for n, v in a.items()}
    tokens = np.concatenate([a["x"][0], a["ctx"][0]])
    arrays = {
        "x_in": tokens.reshape(T + C, KC, P).transpose(2, 1, 0),
        "params": parameters(a),
        "consts": constants(),
        "cond": np.stack([a["c"][0], a["c_ctx"]]),
        "weights": weight_stream(a),
        "mod_w": a["mod_w"].transpose(0, 2, 1).reshape(-1, P, D),
        "rpb": relative_bias(a["na_rpb"][0]),
        "p_in": a["p_2"][:, 0].reshape(2, T, 2, P).transpose(3, 0, 2, 1),
    }
    arrays = {n: np.ascontiguousarray(v) for n, v in arrays.items()}
    nc = bacc.Bacc("TRN2", target_bir_lowering=False, num_devices=1)
    args = [nc.dram_tensor(n, v.shape, F32, kind="ExternalInput").ap() for n, v in arrays.items()]
    out = nc.dram_tensor("out", (P, KC, T), F32, kind="ExternalOutput").ap()
    build(nc, *args, out)
    r = run_bass_kernel_spmd(nc, [arrays], core_ids=[0])
    got = r.results[0]["out"]
    return got.transpose(2, 1, 0).reshape(1, T, D)
```
